# Optimizing a Trainium2 kernel written in Bass

```python
import functools
import jax, jax.numpy as jnp
from jax import lax
import numpy as np

D_MODEL = 1024
BATCH = 1
SEQ = 256
DEPTH = 1
DEC_BATCH = 8
DEC_SEQ = 1
PAST_LEN = 2048
PAGE_SIZE = 128

MLA_HEADS = 8
Q_LORA = 256
KV_LORA = 128
QK_NOPE = 128
QK_ROPE = 64
V_HEAD = 128
ROPE_THETA = 10000.0
ATTN_SCALE = (QK_NOPE + QK_ROPE) ** -0.5
Q_BLOCK = 128
GLA_HEADS = 4
GLA_DK = 128
GLA_DV = 256
GLA_RANK = 16
GLA_TAU = 16.0
GLA_CHUNK = 64
N_MEM = 256
MEM_HEADS = 4
MEM_HEAD_DIM = 128
N_EXPERTS = 32
TOP_K = 4
D_FF = 1024
SWIGLU_LIMIT = 7.0
SWIGLU_ALPHA = 1.702
EPS = 1e-6

MLA_V_WIDTH = MLA_HEADS * V_HEAD
GLA_K_WIDTH = GLA_HEADS * GLA_DK
GLA_V_WIDTH = GLA_HEADS * GLA_DV
MEM_WIDTH = MEM_HEADS * MEM_HEAD_DIM
IN_SPLITS = (Q_LORA, KV_LORA, QK_ROPE, GLA_K_WIDTH, GLA_K_WIDTH, GLA_V_WIDTH, GLA_V_WIDTH, GLA_RANK, D_MODEL, D_MODEL)
D_IN = Q_LORA + KV_LORA + QK_ROPE + 2 * GLA_K_WIDTH + 2 * GLA_V_WIDTH + GLA_RANK + 2 * D_MODEL

kernel_name = "hybrid_mla_gla_moe_decode_step"

def rmsnorm(x, g):
    xf = x.astype(jnp.float32)
    var = jnp.mean(xf * xf, axis=-1, keepdims=True)
    return (xf * lax.rsqrt(var + EPS)).astype(x.dtype) * g

def rope(x, pos):
    half = QK_ROPE // 2
    inv = ROPE_THETA ** (-jnp.arange(half, dtype=jnp.float32) * 2.0 / QK_ROPE)
    ang = pos[:, None] * inv[None, :]
    ang = ang.reshape((ang.shape[0],) + (1,) * (x.ndim - 3) + (half,))
    cos, sin = jnp.cos(ang), jnp.sin(ang)
    xf = x.astype(jnp.float32)
    x1, x2 = xf[..., :half], xf[..., half:]
    return jnp.concatenate([x1 * cos - x2 * sin, x1 * sin + x2 * cos], axis=-1).astype(x.dtype)

def mla_prompt(q_lat, q_rope, c_kv, k_rope):
    B, S, H, _ = q_lat.shape
    nb = S // Q_BLOCK
    ql = jnp.swapaxes(q_lat.reshape(B, nb, Q_BLOCK, H, KV_LORA), 0, 1)
    qr = jnp.swapaxes(q_rope.reshape(B, nb, Q_BLOCK, H, QK_ROPE), 0, 1)
    kpos = jnp.arange(S)

    def block(args):
        i, qlb, qrb = args
        s = (jnp.einsum('bqhr,bkr->bhqk', qlb, c_kv) + jnp.einsum('bqhp,bkp->bhqk', qrb, k_rope)).astype(jnp.float32) * ATTN_SCALE
        qpos = i * Q_BLOCK + jnp.arange(Q_BLOCK)
        s = jnp.where(kpos[None, :] <= qpos[:, None], s, -jnp.inf)
        p = jax.nn.softmax(s, axis=-1).astype(c_kv.dtype)
        return jnp.einsum('bhqk,bkr->bqhr', p, c_kv)

    o = lax.map(block, (jnp.arange(nb), ql, qr))
    return jnp.swapaxes(o, 0, 1).reshape(B, S, H, KV_LORA)

def mla_sample(q_lat, q_rope, c_kv, k_rope, cache_lat, cache_rope, page_table):
    Bd, S = q_lat.shape[:2]
    past_len = page_table.shape[1] * cache_lat.shape[1]
    past_lat = cache_lat[page_table].reshape(Bd, past_len, KV_LORA)
    past_rope = cache_rope[page_table].reshape(Bd, past_len, QK_ROPE)
    keys_lat = jnp.concatenate([past_lat, c_kv.astype(past_lat.dtype)], axis=1)
    keys_rope = jnp.concatenate([past_rope, k_rope.astype(past_rope.dtype)], axis=1)
    s = (jnp.einsum('bqhr,bkr->bhqk', q_lat, keys_lat) + jnp.einsum('bqhp,bkp->bhqk', q_rope, keys_rope)).astype(jnp.float32) * ATTN_SCALE
    kpos = jnp.arange(past_len + S)
    qpos = past_len + jnp.arange(S)
    s = jnp.where(kpos[None, :] <= qpos[:, None], s, -jnp.inf)
    p = jax.nn.softmax(s, axis=-1).astype(keys_lat.dtype)
    return jnp.einsum('bhqk,bkr->bqhr', p, keys_lat)

def gla_prompt(q, k, v, la):
    B, S, H, DK = q.shape
    DV = v.shape[-1]
    C = GLA_CHUNK
    n = S // C
    f32 = jnp.float32

    def to_chunks(t):
        return t.astype(f32).reshape(B, n, C, H, t.shape[-1]).transpose(1, 0, 3, 2, 4)

    qc, kc, vc, lac = to_chunks(q), to_chunks(k), to_chunks(v), to_chunks(la)
    b = jnp.cumsum(lac, axis=3)
    b_last = b[:, :, :, -1:, :]
    q_in = qc * jnp.exp(b)
    k_in = kc * jnp.exp(-b)
    k_out = kc * jnp.exp(b_last - b)
    mask = jnp.arange(C)[:, None] >= jnp.arange(C)[None, :]
    a = jnp.where(mask, jnp.einsum('nbhtd,nbhsd->nbhts', q_in, k_in), 0.0)
    intra = jnp.einsum('nbhts,nbhsv->nbhtv', a, vc)
    kv = jnp.einsum('nbhsd,nbhsv->nbhdv', k_out, vc)
    decay = jnp.exp(b_last[:, :, :, 0, :])

    def step(st, inp):
        d_c, kv_c = inp
        return d_c[..., None] * st + kv_c, st

    s_final, s_prev = lax.scan(step, jnp.zeros((B, H, DK, DV), f32), (decay, kv))
    inter = jnp.einsum('nbhtd,nbhdv->nbhtv', q_in, s_prev)
    o = (intra + inter).transpose(1, 0, 3, 2, 4).reshape(B, S, H, DV)
    return o.astype(q.dtype), s_final.astype(q.dtype)

def gla_sample(q, k, v, la, state):
    f32 = jnp.float32
    xs = (jnp.swapaxes(q.astype(f32), 0, 1), jnp.swapaxes(k.astype(f32), 0, 1),
          jnp.swapaxes(v.astype(f32), 0, 1), jnp.swapaxes(la.astype(f32), 0, 1))

    def step(st, inp):
        qt, kt, vt, lat = inp
        st = jnp.exp(lat)[..., None] * st + kt[..., :, None] * vt[..., None, :]
        return st, jnp.einsum('bhd,bhdv->bhv', qt, st)

    s_final, o = lax.scan(step, state.astype(f32), xs)
    return jnp.swapaxes(o, 0, 1).astype(q.dtype), s_final.astype(state.dtype)

def memory_kv(mem, g_mem, w_mk, w_mv):
    B, M, _ = mem.shape
    mn = rmsnorm(mem, g_mem)
    return ((mn @ w_mk).reshape(B, M, MEM_HEADS, MEM_HEAD_DIM),
            (mn @ w_mv).reshape(B, M, MEM_HEADS, MEM_HEAD_DIM))

def cross_attend(xn, mem_k, mem_v, w_mq, w_mo):
    B, S, _ = xn.shape
    q = (xn @ w_mq).reshape(B, S, MEM_HEADS, MEM_HEAD_DIM)
    s = jnp.einsum('bshd,bmhd->bhsm', q, mem_k).astype(jnp.float32) * MEM_HEAD_DIM ** -0.5
    p = jax.nn.softmax(s, axis=-1).astype(mem_v.dtype)
    o = jnp.einsum('bhsm,bmhd->bshd', p, mem_v).reshape(B, S, MEM_WIDTH)
    return o @ w_mo

def moe(xn, w_router, b_router, w_gate_up, b_gate_up, w_down, b_down):
    B, S, D = xn.shape
    xt = xn.reshape(B * S, D)
    logits = (xt @ w_router + b_router).astype(jnp.float32)
    top_val, top_idx = lax.top_k(logits, TOP_K)
    w_top = jax.nn.softmax(top_val, axis=-1)
    combine = jnp.einsum('tk,tke->te', w_top, jax.nn.one_hot(top_idx, N_EXPERTS, dtype=jnp.float32)).astype(xt.dtype)
    out = jnp.zeros_like(xt)
    for e in range(N_EXPERTS):
        a = xt @ w_gate_up[e] + b_gate_up[e]
        gate = jnp.minimum(a[:, :D_FF], SWIGLU_LIMIT)
        up = jnp.clip(a[:, D_FF:], -SWIGLU_LIMIT, SWIGLU_LIMIT)
        h = (up + 1.0) * gate * jax.nn.sigmoid(SWIGLU_ALPHA * gate)
        out = out + combine[:, e:e + 1] * (h @ w_down[e] + b_down[e])
    return out.reshape(B, S, D)

def decoder_layer(x, pos, mem_k, mem_v, attend, recur,
                  g_attn, w_in, g_q, g_kv, w_uq, w_uk, w_uv, w_a2, b_a, g_gla,
                  w_o_mla, w_o_gla, w_out, g_cross, w_mq, w_mo,
                  g_ffn, w_router, b_router, w_gate_up, b_gate_up, w_down, b_down):
    B, S, _ = x.shape
    xn = rmsnorm(x, g_attn)
    split_idx = np.cumsum(np.array(IN_SPLITS))[:-1].tolist()
    cq, ckv, kr, gq, gk, gv, gg, ga, z_mla, z_gla = jnp.split(xn @ w_in, split_idx, axis=-1)
    c_q = rmsnorm(cq, g_q)
    q = (c_q @ w_uq).reshape(B, S, MLA_HEADS, QK_NOPE + QK_ROPE)
    q_nope = q[..., :QK_NOPE]
    q_rope = rope(q[..., QK_NOPE:], pos)
    q_lat = jnp.einsum('bshn,rhn->bshr', q_nope, w_uk)
    c_kv = rmsnorm(ckv, g_kv)
    k_rope = rope(kr, pos)
    o_lat = attend(q_lat, q_rope, c_kv, k_rope)
    o_mla = jnp.einsum('bshr,rhv->bshv', o_lat, w_uv).reshape(B, S, MLA_V_WIDTH) @ w_o_mla
    qg = gq.reshape(B, S, GLA_HEADS, GLA_DK) * GLA_DK ** -0.5
    kg = gk.reshape(B, S, GLA_HEADS, GLA_DK)
    vg = gv.reshape(B, S, GLA_HEADS, GLA_DV)
    la = (jax.nn.log_sigmoid((ga @ w_a2 + b_a).astype(jnp.float32)) / GLA_TAU).reshape(B, S, GLA_HEADS, GLA_DK)
    o_g, gla_state = recur(qg, kg, vg, la)
    o_g = rmsnorm(o_g, g_gla) * jax.nn.silu(gg.reshape(B, S, GLA_HEADS, GLA_DV))
    o_gla = o_g.reshape(B, S, GLA_V_WIDTH) @ w_o_gla
    merged = jax.nn.sigmoid(z_mla) * o_mla + jax.nn.sigmoid(z_gla) * o_gla
    h = x + merged @ w_out
    h = h + cross_attend(rmsnorm(h, g_cross), mem_k, mem_v, w_mq, w_mo)
    h = h + moe(rmsnorm(h, g_ffn), w_router, b_router, w_gate_up, b_gate_up, w_down, b_down)
    return h, c_kv, k_rope, gla_state

def setup_inputs(seed: int = 0) -> dict:
    key = jax.random.key(seed)
    ks = jax.random.split(key, 40)
    f32 = jnp.float32

    def nrm(k, shape, scale=1.0):
        return jax.random.normal(k, shape, f32) * scale

    def gain(k, shape):
        return 1.0 + 0.02 * jax.random.normal(k, shape, f32)

    n_pages = PAST_LEN // PAGE_SIZE
    n_used = DEC_BATCH * n_pages
    n_pool = (n_used * 5) // 4
    page_table = jax.random.permutation(ks[0], n_pool)[:n_used].reshape(DEC_BATCH, n_pages).astype(jnp.int32)
    L = DEPTH
    return {
        "x_prompt": nrm(ks[1], (BATCH, SEQ, D_MODEL)),
        "x_sample": nrm(ks[2], (DEC_BATCH, DEC_SEQ, D_MODEL)),
        "cache_kv_latent": nrm(ks[3], (L, n_pool, PAGE_SIZE, KV_LORA)),
        "cache_k_rope": nrm(ks[4], (L, n_pool, PAGE_SIZE, QK_ROPE)),
        "state_gla": nrm(ks[5], (L, DEC_BATCH, GLA_HEADS, GLA_DK, GLA_DV)),
        "cache_mem_k": nrm(ks[6], (L, DEC_BATCH, N_MEM, MEM_HEADS, MEM_HEAD_DIM)),
        "cache_mem_v": nrm(ks[7], (L, DEC_BATCH, N_MEM, MEM_HEADS, MEM_HEAD_DIM)),
        "page_table": page_table,
        "mem_prompt": nrm(ks[8], (BATCH, N_MEM, D_MODEL)),
        "g_attn": gain(ks[9], (L, D_MODEL)),
        "w_in": nrm(ks[10], (L, D_MODEL, D_IN), D_MODEL ** -0.5),
        "g_q": gain(ks[11], (L, Q_LORA)),
        "g_kv": gain(ks[12], (L, KV_LORA)),
        "w_uq": nrm(ks[13], (L, Q_LORA, MLA_HEADS * (QK_NOPE + QK_ROPE)), Q_LORA ** -0.5),
        "w_uk": nrm(ks[14], (L, KV_LORA, MLA_HEADS, QK_NOPE), KV_LORA ** -0.5),
        "w_uv": nrm(ks[15], (L, KV_LORA, MLA_HEADS, V_HEAD), KV_LORA ** -0.5),
        "w_a2": nrm(ks[16], (L, GLA_RANK, GLA_K_WIDTH), GLA_RANK ** -0.5),
        "b_a": nrm(ks[17], (L, GLA_K_WIDTH), 0.01),
        "g_gla": gain(ks[18], (L, GLA_DV)),
        "w_o_mla": nrm(ks[19], (L, MLA_V_WIDTH, D_MODEL), MLA_V_WIDTH ** -0.5),
        "w_o_gla": nrm(ks[20], (L, GLA_V_WIDTH, D_MODEL), GLA_V_WIDTH ** -0.5),
        "w_out": nrm(ks[21], (L, D_MODEL, D_MODEL), D_MODEL ** -0.5),
        "g_mem": gain(ks[22], (L, D_MODEL)),
        "w_mk": nrm(ks[23], (L, D_MODEL, MEM_WIDTH), D_MODEL ** -0.5),
        "w_mv": nrm(ks[24], (L, D_MODEL, MEM_WIDTH), D_MODEL ** -0.5),
        "g_cross": gain(ks[25], (L, D_MODEL)),
        "w_mq": nrm(ks[26], (L, D_MODEL, MEM_WIDTH), D_MODEL ** -0.5),
        "w_mo": nrm(ks[27], (L, MEM_WIDTH, D_MODEL), MEM_WIDTH ** -0.5),
        "g_ffn": gain(ks[28], (L, D_MODEL)),
        "w_router": nrm(ks[29], (L, D_MODEL, N_EXPERTS), D_MODEL ** -0.5),
        "b_router": nrm(ks[30], (L, N_EXPERTS), 0.01),
        "w_gate_up": nrm(ks[31], (L, N_EXPERTS, D_MODEL, 2 * D_FF), D_MODEL ** -0.5),
        "b_gate_up": nrm(ks[32], (L, N_EXPERTS, 2 * D_FF), 0.01),
        "w_down": nrm(ks[33], (L, N_EXPERTS, D_FF, D_MODEL), D_FF ** -0.5),
        "b_down": nrm(ks[34], (L, N_EXPERTS, D_MODEL), 0.01),
        "g_final": gain(ks[35], (D_MODEL,)),
    }

def reference(x_prompt, x_sample, cache_kv_latent, cache_k_rope, state_gla, cache_mem_k, cache_mem_v,
              page_table, mem_prompt, g_attn, w_in, g_q, g_kv, w_uq, w_uk, w_uv, w_a2, b_a, g_gla,
              w_o_mla, w_o_gla, w_out, g_mem, w_mk, w_mv, g_cross, w_mq, w_mo, g_ffn,
              w_router, b_router, w_gate_up, b_gate_up, w_down, b_down, g_final):
    pos_p = jnp.arange(x_prompt.shape[1], dtype=jnp.float32)
    past_len = page_table.shape[1] * cache_kv_latent.shape[2]
    pos_s = past_len + jnp.arange(x_sample.shape[1], dtype=jnp.float32)
    h_p, h_s = x_prompt, x_sample
    lat_p, rope_p, st_p, mk_p, mv_p = [], [], [], [], []
    lat_s, rope_s, st_s = [], [], []
    for l in range(DEPTH):
        lw = (g_attn[l], w_in[l], g_q[l], g_kv[l], w_uq[l], w_uk[l], w_uv[l], w_a2[l], b_a[l], g_gla[l],
              w_o_mla[l], w_o_gla[l], w_out[l], g_cross[l], w_mq[l], w_mo[l],
              g_ffn[l], w_router[l], b_router[l], w_gate_up[l], b_gate_up[l], w_down[l], b_down[l])
        mem_k, mem_v = memory_kv(mem_prompt, g_mem[l], w_mk[l], w_mv[l])
        h_p, ckv, kr, st = decoder_layer(h_p, pos_p, mem_k, mem_v, mla_prompt, gla_prompt, *lw)
        lat_p.append(ckv); rope_p.append(kr); st_p.append(st); mk_p.append(mem_k); mv_p.append(mem_v)
        attend_s = functools.partial(mla_sample, cache_lat=cache_kv_latent[l], cache_rope=cache_k_rope[l], page_table=page_table)
        recur_s = functools.partial(gla_sample, state=state_gla[l])
        h_s, ckv, kr, st = decoder_layer(h_s, pos_s, cache_mem_k[l], cache_mem_v[l], attend_s, recur_s, *lw)
        lat_s.append(ckv); rope_s.append(kr); st_s.append(st)
    y_prompt = rmsnorm(h_p, g_final)
    y_sample = rmsnorm(h_s, g_final)
    return (y_prompt, y_sample,
            jnp.stack(lat_p), jnp.stack(rope_p), jnp.stack(st_p), jnp.stack(mk_p), jnp.stack(mv_p),
            jnp.stack(lat_s), jnp.stack(rope_s), jnp.stack(st_s))


_drawn_inputs = setup_inputs


def setup_inputs(seed=0):
    import zlib

    import numpy as np

    out = dict(_drawn_inputs(seed))
    spreads = {}
    factors = {'cache_k_rope': 4.974,
     'g_q': 8.0,
     'g_kv': 3.051,
     'b_a': 13.353,
     'g_gla': 9.98,
     'g_cross': 5.415,
     'b_gate_up': 8.0,
     'b_down': 43.788,
     'g_final': 24.899,
     'g_mem': 2.68,
     'g_ffn': 2.981,
     'b_router': 4.185}
    for name, (base, spread) in spreads.items():
        noise = np.random.default_rng([zlib.crc32(name.encode()), seed]).standard_normal(out[name].shape)
        drawn = base * np.exp(spread * noise) if base else spread * noise
        out[name] = __import__('jax').numpy.asarray(drawn.astype(out[name].dtype))
    for name, factor in factors.items():
        out[name] = (out[name] * factor).astype(out[name].dtype)
    return out
```

```python
from contextlib import ExitStack

import numpy as np

import concourse.bass as bass
from concourse import mybir

ALU = mybir.AluOpType
ACT = mybir.ActivationFunctionType
F32 = mybir.dt.float32
I32 = mybir.dt.int32
U32 = mybir.dt.uint32
AX = mybir.AxisListType.X

P = 128
D = 1024
KC = D // P
PROMPT, SAMPLE = 256, 8
T = PROMPT + SAMPLE
TILES = [(0, 128), (128, 128), (256, 8)]
H_MLA, NOPE, ROPE, LORA = 8, 128, 64, 128
H_GLA, DK, DV, CH = 4, 128, 256, 64
NCH = PROMPT // CH
H_MEM, NMEM = 4, 256
NE, TOPK, DFF = 32, 4, 1024
CAP = 64
MAX_PASS = -(-T // CAP)
PAST, PAGE, NPAGES = 2048, 128, 16
EPS = 1e-6
ATTN_SCALE = float((NOPE + ROPE) ** -0.5)
MEM_SCALE = float(P ** -0.5)
FAR = 1e4
NEG = -1e30
SLOT = 4096
TRUNK_SLOTS, MOE_SLOTS = 4, 6

C_CQ, C_CKV, C_KR, C_GQ, C_GK, C_GV, C_GG, C_GA, C_ZM, C_ZG = 0, 256, 384, 448, 960, 1472, 2496, 3520, 3536, 4560

GAINS = {"g_attn": 0, "g_mem": 8, "g_cross": 16, "g_ffn": 24, "g_final": 32, "g_q": 40, "g_kv": 42, "g_gla": 43, "b_a": 45}
N_GAINS = 49

CONSTS = {}
for _name, _n in [("ident", 128), ("ones", 128), ("before", 128), ("rot", 64), ("cos", T), ("sin", T),
                  ("carry", PROMPT), ("count", 64), ("causal", 256), ("own", 64), ("upto", 64), ("spread", 128),
                  ("within", 1), ("pick", 8 * 128)]:
    CONSTS[_name] = (sum(n for _, n in CONSTS.values()), _n)
N_CONST = sum(n for _, n in CONSTS.values())


def constants():
    f = np.float32
    c = np.zeros((P, N_CONST), f)

    def put(name, a):
        o, n = CONSTS[name]
        c[:a.shape[0], o:o + n] = a

    i = np.arange(P)
    put("ident", np.eye(P, dtype=f))
    put("ones", np.ones((P, P), f))
    put("before", (i[:, None] < i[None, :]).astype(f))
    r = np.zeros((64, 64), f)
    for a in range(32):
        r[a + 32, a] = -1
        r[a, a + 32] = 1
    put("rot", r)
    inv = (f(10000.0) ** (-np.arange(32, dtype=f) * f(2.0) / f(64))).astype(f)
    pos = np.concatenate([np.arange(PROMPT), np.full(SAMPLE, PAST)]).astype(f)
    ang = (pos[None, :] * inv[:, None]).astype(f)
    put("cos", np.tile(np.cos(ang), (2, 1)))
    put("sin", np.tile(np.sin(ang), (2, 1)))
    put("carry", np.tile((np.arange(PROMPT) % CH != 0).astype(f), (P, 1)))
    put("count", np.tile(np.arange(64, dtype=f), (P, 1)))
    put("causal", np.where(np.arange(256)[None, :] - 128 <= i[:, None], 0, NEG).astype(f))
    own = np.full((8, 8, 8), NEG, f)
    for b in range(8):
        own[b, b] = 0
    put("own", own.reshape(8, 64))
    s = np.arange(CH)
    put("upto", (s[:, None] <= s[None, :]).astype(f))
    put("spread", np.where(i[None, :] // 8 == np.arange(16)[:, None], 8, 0).astype(f))
    put("within", (i % 8).astype(f)[:, None])
    pick = np.zeros((8, 8, 128), f)
    for b in range(8):
        pick[b, b] = 1
    put("pick", pick.reshape(8, 1024))
    return c


LIN = (["cq0", "cq1", "ckv", "kr", "rotk"] + [f"mk{h}" for h in range(4)] + ["mv0", "mv1"]
       + [f"qn{h}" for h in range(8)] + [f"qr{h}" for h in range(8)] + [f"rot{h}" for h in range(8)]
       + [f"ql{h}" for h in range(8)] + ["own", "mmax", "mbc", "msum"] + [f"att{u}" for u in range(16)] + ["past"]
       + [f"uv{h}" for h in range(8)]
       + [f"gq{h}" for h in range(4)] + [f"gk{h}" for h in range(4)] + [f"gv{c}" for c in range(8)] + ["ga"]
       + [f"la{h}" for h in range(4)] + [f"vb{n}" for n in range(16)] + [f"A{c}" for c in range(4)] + [f"kv{n}" for n in range(8)]
       + [f"go{n}" for n in range(8)]
       + [f"gg{c}" for c in range(8)] + [f"zm{c}" for c in range(8)] + [f"zg{c}" for c in range(8)]
       + [f"om{c}" for c in range(8)] + [f"og{c}" for c in range(8)] + [f"wo{c}" for c in range(8)]
       + [f"mq{h}" for h in range(4)] + ["xmax", "xbc", "xsum"] + [f"att{u}" for u in range(16, 24)] + ["xpast"]
       + [f"mo{c}" for c in range(8)] + ["lg0", "lg1", "lg2", "rk0", "rk1", "rk2", "cnt"] + [f"bd{c}" for c in range(8)])
LI = {n: i for i, n in enumerate(LIN)}

TURN = (["gains", "bias"] + [f"x{c}" for c in range(8)] + ["uk0", "uk1"] + [f"m{c}" for c in range(8)]
        + ["mkt0", "mkt1", "ckvt", "krt"]
        + [f"K{b}_{g}" for b in range(8) for g in range(6)] + [f"pt{u}" for u in range(16)]
        + [f"v{n}" for n in range(10)] + [f"ko{c}" for c in range(4)]
        + [f"X{n}" for n in range(16)] + [f"pt{u}" for u in range(16, 24)]
        + [f"hn{n}" for n in range(6)] + ["cwt"] + [f"y{n}" for n in range(6)])
TI = {n: i for i, n in enumerate(TURN)}

RING = [("in_a", "kr"), ("mk", "mk3"), ("mv", "mv1"), ("uq", "qr7"), ("uv", "uv7"), ("gq", "gq3"), ("gk", "gk3"),
        ("gv0", "gv3"), ("gv1", "gv7"), ("gg0", "gg3"), ("gg1", "gg7"), ("zm0", "zm3"), ("zm1", "zm7"), ("zg0", "zg3"), ("zg1", "zg7"),
        ("om0", "om3"), ("om1", "om7"), ("og0", "og3"), ("og1", "og7"), ("wo0", "wo3"), ("wo1", "wo7"), ("mq", "mq3"), ("mo", "mo7")]
RI = {n: i for i, (n, _) in enumerate(RING)}


def build(nc, ins, outs, consts):
    (x_prompt, x_sample, cache_lat, cache_rope, state_gla, mem_k_in, mem_v_in, page_table, mem_prompt, g_attn, w_in, g_q, g_kv,
     w_uq, w_uk, w_uv, w_a2, b_a, g_gla, w_o_mla, w_o_gla, w_out, g_mem, w_mk, w_mv, g_cross, w_mq, w_mo, g_ffn,
     w_router, b_router, w_gate_up, b_gate_up, w_down, b_down, g_final) = ins
    (y_prompt, y_sample, o_lat_p, o_rope_p, o_state_p, o_memk_p, o_memv_p, o_lat_s, o_rope_s, o_state_s) = outs

    ctx = ExitStack()
    with ctx:
        sems = {}

        def S(name):
            if name not in sems:
                sems[name] = ctx.enter_context(nc.semaphore("s_" + name))
            return sems[name]

        def sb(name, n, dt=F32, p=P):
            return ctx.enter_context(nc.sbuf_tensor(name, [p, n], dt))

        B = [ctx.enter_context(nc.psum_tensor(f"bank{i}", [P, 512], F32)) for i in range(8)]
        TURN_BANKS, SCORE_BANK = [B[5], B[6]], B[7]
        SCORE_BANKS = [B[7], B[4]]
        C = sb("consts_sb", N_CONST)
        ring = sb("ring", MOE_SLOTS * SLOT)
        resid = sb("resid", KC * T)
        normed = sb("normed", KC * T)
        gT = sb("gains_t", N_GAINS)
        biasT = sb("bias_t", 512)
        A = sb("arena", 19840)
        whole = sb("npass", 4, I32)

        def con(name, p=P):
            o, n = CONSTS[name]
            return C[0:p, o:o + n]

        ident, ones = con("ident"), con("ones")

        def slot(n):
            return ring[:, n * SLOT:(n + 1) * SLOT]

        def view(o, n, b=None):
            v = A[:, o:o + n]
            return v if b is None else v.rearrange("p (a b) -> p a b", b=b)

        X = ring[:, 4 * SLOT:6 * SLOT]

        def xview(o, n, b=None):
            v = X[:, o:o + n]
            return v if b is None else v.rearrange("p (a b) -> p a b", b=b)

        h_T = resid[:].rearrange("p (c t) -> p c t", t=T)
        n_T = normed[:].rearrange("p (c t) -> p c t", t=T)
        memk = view(0, 1024, NMEM)
        memv = view(1024, 1024, 512)
        squares = view(2048, 2112)
        big2, big3, big4, big5 = (view(4160 + 2112 * i, 2112, T) for i in range(4))
        o = [12608]

        def small(n, b=None):
            v = view(o[0], n, b)
            o[0] += n
            return v

        cq, ckvT, krT, rotk = small(2 * T, T), small(T), small(T), small(T)
        rstd = small(T, T)
        own_s, mxp, mxT, gm, dg, mbc, rinv, psums = (small(n) for n in (64, 64, 136, 1, 64, 64, 64, 64))
        ckv_tok, kr_tok = small(384, 128), small(192, 64)
        assert o[0] <= 15408
        KTl, KTr = view(15508 - 100, 2048), view(15508 - 100 + 2048, 1024)
        ukT = KTl[:, 0:1024]
        scores = view(18480, 1024)
        pages = view(19504, 24)
        idx = A[:, 19528:19536].bitcast(U32)
        Q2 = view(19536, 128, 64)
        Qs = view(19664, 64)
        exps = view(19728, 4)
        w_r = sb("w_router_sb", 256)
        w_ga = sb("w_ga", 128)
        w_a2_sb = sb("w_a2_sb", 512, p=16)
        ga = A[0:16, 18816:18816 + T]
        b_r = sb("b_router_sb", NE, p=1)

        def lin_bank(name):
            return B[LI[name] % 4]

        def turn_bank(name):
            return TURN_BANKS[TI[name] % 2]

        def turn_sem(name):
            return S("turned_by_dve" if TI[name] % 2 == 0 else "turned_by_act")

        def turned(eng, name):
            eng.wait_ge(turn_sem(name), TI[name] // 2 + 1)

        def lin_done(eng, name):
            eng.wait_ge(S("product_out"), LI[name] + 1)

        def lin_full(eng, name):
            eng.wait_ge(S("product_full"), LI[name] + 1)

        def w_ready(eng, name):
            n = RI[name]
            eng.wait_ge(S(f"slot{n % TRUNK_SLOTS}_loaded"), 16 * (n // TRUNK_SLOTS + 1))

        x_tok = xview(0, 3072, D)
        m_tok = xview(3072, 2048, D)
        memT = xview(5120, 2048, NMEM)
        bias_rows = view(4160, 512, 128)
        gain_rows = view(4160 + 512, 128)
        wuk = view(10496, 1024)
        lat = [xview(2048 * i, 2048, 128) for i in range(2)]
        rop = [xview(4096 + 1024 * i, 1024) for i in range(2)]
        att = [xview(6144 + 256 * i, 256) for i in range(2)]
        attT = [xview(6656 + 256 * i, 256, 128) for i in range(2)]
        nmx = xview(7168, 48)

        UNITS = [(h, qb, (qb + 1) * 128) for h in range(H_MLA) for qb in range(2)] + [(h, qb, 256) for h in range(H_MEM) for qb in range(2)]

        gqT, gkT = view(4160, 1056, T), view(4160 + 1056, 1056, T)
        gla, gb = view(8384, 1056, T), view(8384 + 1056, 1056, T)
        gvT = big5
        ge, gtmp = view(12608, 1056, T), view(12608 + 1056, 1056, T)
        states = view(14720, 4096).rearrange("p (h c v) -> p h c v", h=H_GLA, c=NCH)
        vb = view(18816, 1024, 512)
        st_buf = [view(2048 + 1024 * i, 1024, DV) for i in range(2)]
        v_tok = X[0:64, 0:4096].rearrange("p (c v) -> p c v", c=NCH)
        ko_tok = X[0:64, 4096:6144].rearrange("p (c k) -> p c k", c=NCH)
        AT = X[0:64, 6144:7168].rearrange("p (c h t) -> p c h t", c=NCH, h=H_GLA)
        vs_tok = X[0:8, 7168:8192]
        rstd_gla = view(12608, 4 * T, T)
        silu_gg, sig_zm, sig_zg = xview(0, 2112, T), xview(2112, 2112, T), xview(4224, 2112, T)

        qx, xo = view(4160, 1056, T), view(4160 + 1056, 1056, T)
        Kx = view(10496, 8192).rearrange("p (b t n) -> p b t n", b=8, t=2)
        Vx = [view(18688, 1024, 512)]
        kxT = [view(8384 + 512 * i, 512) for i in range(2)]
        xs = view(8384 + 1024, 64)
        xmxp, xmxT, xgm, xdg, xmbc, xps, xrinv = (view(8384 + 1100 + 136 * i, 136) for i in range(7))
        xatt = [view(2048 + 256 * i, 256) for i in range(2)]
        xattT = [view(2560 + 256 * i, 256, 128) for i in range(2)]
        xnmx = view(3072, 48)
        rstd2 = view(3200, T, T)

        acc = view(16000, 2112, T)
        hn_tok = view(4160, 3072, D)
        mo_ = [7232]

        def moe_buf(n, b=None):
            v = view(mo_[0], n, b)
            mo_[0] += n
            return v

        xg = [moe_buf(512, CAP) for _ in range(2)]
        gate, up, sg, hmid = moe_buf(512, CAP), moe_buf(512, CAP), moe_buf(512, CAP), moe_buf(512, CAP)
        yT = moe_buf(1024, P)
        y_rows = moe_buf(1024)
        sel = [moe_buf(3 * CAP, CAP) for _ in range(2)]
        wsel = moe_buf(3 * 2 * CAP, 2 * CAP)
        wselT = moe_buf(T)
        posm = moe_buf(3 * 34, 34)
        cw = moe_buf(3 * 34, 34)
        take = moe_buf(3 * 32, 32)
        curp, curw, curb = moe_buf(9, 3), moe_buf(6, 2), moe_buf(32, 16)
        logits = moe_buf(96)
        top8, e4, tmp32 = moe_buf(24), moe_buf(24), moe_buf(32)
        top_i = moe_buf(24).bitcast(U32)
        top_f = moe_buf(24)
        cwT = moe_buf(T)
        b_dn = moe_buf(1024)
        cnts = moe_buf(40)
        assert mo_[0] <= 16000
        y_tok = view(4160, 3072, D)

        block = ctx.enter_context(nc.Block())

        w_cols = lambda w, a, n: w[0, :, a:a + n].rearrange("(c p) n -> p c n", p=P)

        @block.sync
        def _(sp):
            def into(n, nk, cols):
                return slot(n)[:, 0:nk * cols].rearrange("p (c n) -> p c n", c=nk)

            trunk = {"in_a": (w_cols(w_in, 0, 448), 8, 448), "mk": (w_cols(w_mk, 0, 512), 8, 512), "mv": (w_cols(w_mv, 0, 512), 8, 512),
                     "uq": (w_cols(w_uq, 0, 1536), 2, 1536),
                     "uv": (w_uv[0].rearrange("r h v -> r (h v)")[:, None, :], 1, 1024),
                     "gq": (w_cols(w_in, C_GQ, 512), 8, 512), "gk": (w_cols(w_in, C_GK, 512), 8, 512),
                     "mq": (w_cols(w_mq, 0, 512), 8, 512), "mo": (w_cols(w_mo, 0, 1024), 4, 1024)}
            for half in range(2):
                for name, w, at in (("gv", w_in, C_GV), ("gg", w_in, C_GG), ("zm", w_in, C_ZM), ("zg", w_in, C_ZG),
                                    ("om", w_o_mla, 0), ("og", w_o_gla, 0), ("wo", w_out, 0)):
                    trunk[f"{name}{half}"] = (w_cols(w, at + 512 * half, 512), 8, 512)
            sp.dma_start(C[:], consts).then_inc(S("const_loaded"), 16)
            for tt, (t0, n) in enumerate(TILES):
                src = x_prompt[0, t0:t0 + n, :] if tt < 2 else x_sample[:, 0, :]
                sp.dma_start(x_tok[0:n, tt, :], src).then_inc(S("x_loaded"), 16)
            for n, (name, _) in enumerate(RING):
                if n >= TRUNK_SLOTS:
                    lin_full(sp, RING[n - TRUNK_SLOTS][1])
                src, nk, cols = trunk[name]
                sp.dma_start(into(n % TRUNK_SLOTS, nk, cols), src).then_inc(S(f"slot{n % 4}_loaded"), 16)
                if name == "in_a":
                    sp.dma_start(wuk, w_uk[0].rearrange("r h n -> r (h n)")).then_inc(S("uk_loaded"), 16)
                    sp.dma_start(m_tok, mem_prompt[0].rearrange("(t p) d -> p t d", p=P)).then_inc(S("mem_loaded"), 16)

            def expert_weights(e):
                gu = w_gate_up[0, bass.ds(e, 1)].rearrange("o (c p) n -> p (o c) n", p=P)
                dn = w_down[0, bass.ds(e, 1)].rearrange("o (c p) n -> p (o c) n", p=P)
                return [gu[:, :, 512 * j:512 * j + 512] for j in range(4)] + [dn[:, :, 512 * j:512 * j + 512] for j in range(2)]

            last_reader = {n % TRUNK_SLOTS: reader for n, (_, reader) in enumerate(RING)}
            parts = expert_weights(0)
            for s in (4, 5, 3, 0, 1, 2):
                if s < TRUNK_SLOTS:
                    lin_full(sp, last_reader[s])
                elif s == TRUNK_SLOTS:
                    sp.wait_ge(S("merged"), 8)
                sp.dma_start(into(s, 8, 512), parts[s]).then_inc(S(f"expert_slot{s}"), 16)
            with sp.Fori(1, NE) as e:
                for s, src in enumerate(expert_weights(e)):
                    sp.wait_ge(S(f"slot{s}_used"), e)
                    sp.dma_start(into(s, 8, 512), src).then_inc(S(f"expert_slot{s}"), 16)
            sp.wait_ge(S("npass"), 1)
            npass = sp.value_load(whole[0:1, 0:1], min_val=1, max_val=MAX_PASS)
            with sp.If(npass > 1):
                with sp.Fori(1, npass) as p:
                    with sp.Fori(0, NE) as e:
                        for s, src in enumerate(expert_weights(e)):
                            sp.wait_ge(S(f"slot{s}_used"), p * NE + e)
                            sp.dma_start(into(s, 8, 512), src).then_inc(S(f"expert_slot{s}"), 16)
            turned(sp, "y4")
            turned(sp, "y5")
            for tt, (t0, n) in enumerate(TILES):
                dst = y_prompt[0, t0:t0 + n, :] if tt < 2 else y_sample[:, 0, :]
                sp.dma_start(dst, y_tok[0:n, tt, :]).then_inc(S("y_stored"), 16)
            sp.wait_ge(S("y_stored"), 48)

        @block.gpsimd
        def _(pool):
            pool.dma_start(pages[0:16, 0:8].bitcast(I32), page_table.rearrange("b j -> j b"), allow_slow_non_contiguous=True)\
                .then_inc(S("pages_loaded"), 16)
            for name, src in (("g_attn", g_attn[0]), ("g_mem", g_mem[0]), ("g_cross", g_cross[0]), ("g_ffn", g_ffn[0]), ("g_final", g_final),
                              ("g_q", g_q[0]), ("g_kv", g_kv[0]), ("g_gla", g_gla[0]), ("b_a", b_a[0])):
                r = GAINS[name]
                n = src.shape[0] // P
                pool.dma_start(gain_rows[r:r + n, :], src.rearrange("(c p) -> c p", p=P)).then_inc(S("gains_loaded"), 16)
            pool.dma_start(bias_rows, b_gate_up[0].rearrange("e (c p) -> (e c) p", p=P).rearrange("(a q) p -> q a p", q=P))\
                .then_inc(S("bias_loaded"), 16)
            pool.dma_start(w_ga.rearrange("p (c n) -> p c n", c=KC), w_cols(w_in, C_GA, 16)).then_inc(S("small_loaded"), 16)
            pool.dma_start(w_a2_sb[:], w_a2[0]).then_inc(S("small_loaded"), 16)
            pool.dma_start(w_r[:].rearrange("p (c n) -> p c n", c=KC), w_router[0].rearrange("(c p) n -> p c n", p=P)).then_inc(S("small_loaded"), 16)
            pool.dma_start(b_r[:], b_router).then_inc(S("small_loaded"), 16)

            lat_rows = cache_lat[0].rearrange("n (g t) r -> (n g) (t r)", g=8)
            rope_rows = cache_rope[0].rearrange("n (g t) r -> (n g) (t r)", g=8)
            pool.wait_ge(S("idx"), 1)
            for b in range(8):
                if b == 0:
                    lin_full(pool, "mv1")
                if b >= 2:
                    pool.wait_ge(S("turn_full"), TI[f"K{b - 2}_5"] + 1)
                off = bass.IndirectOffsetOnAxis(ap=idx[:, b:b + 1], axis=0)
                pool.indirect_dma_start(lat[b % 2].rearrange("p a b -> p (a b)"), None, lat_rows, off).then_inc(S(f"lat{b % 2}"), 16)
                pool.indirect_dma_start(rop[b % 2], None, rope_rows, off).then_inc(S(f"rope{b % 2}"), 16)
            lin_done(pool, "mv1")
            pool.dma_start(o_memv_p[0, 0].rearrange("(t p) h d -> p t (h d)", p=P), memv).then_inc(S("stored"), 16)
            mk_tok = [squares[:, 512 * i:512 * i + 512] for i in range(2)]
            for tt in range(2):
                turned(pool, f"mkt{tt}")
                pool.dma_start(o_memk_p[0, 0, tt * P:(tt + 1) * P].rearrange("p h d -> p (h d)"), mk_tok[tt]).then_inc(S("stored"), 16)
            turned(pool, "ckvt")
            turned(pool, "krt")
            for tt, (t0, n) in enumerate(TILES):
                dl = o_lat_p[0, 0, t0:t0 + n, :] if tt < 2 else o_lat_s[0, :, 0, :]
                dr = o_rope_p[0, 0, t0:t0 + n, :] if tt < 2 else o_rope_s[0, :, 0, :]
                pool.dma_start(dl, ckv_tok[0:n, tt, :]).then_inc(S("stored"), 16)
                pool.dma_start(dr, kr_tok[0:n, tt, :]).then_inc(S("stored"), 16)
            for b in range(8):
                if b < 2:
                    pool.wait_ge(S("turn_full"), TI[f"K{b + 6}_5"] + 1)
                else:
                    pool.wait_ge(S("values_read"), b - 1)
                off = bass.IndirectOffsetOnAxis(ap=idx[:, b:b + 1], axis=0)
                pool.indirect_dma_start(lat[b % 2].rearrange("p a b -> p (a b)"), None, lat_rows, off).then_inc(S(f"lat{b % 2}"), 16)
            pool.wait_ge(S("stored"), 16 * 9)
            for b in range(8):
                if b >= 2:
                    pool.wait_ge(S(f"state_out{b % 2}"), 16 * (b // 2))
                    pool.wait_ge(S("state_read"), b - 1)
                pool.dma_start(st_buf[b % 2], state_gla[0, b].rearrange("h k v -> k h v")).then_inc(S(f"state_in{b % 2}"), 16)
                if b >= 1:
                    pool.wait_ge(S("state_new"), b)
                    pool.dma_start(o_state_s[0, b - 1].rearrange("h k v -> k h v"), st_buf[(b - 1) % 2])\
                        .then_inc(S(f"state_out{(b - 1) % 2}"), 16)
            pool.wait_ge(S("state_new"), 8)
            pool.dma_start(o_state_s[0, 7].rearrange("h k v -> k h v"), st_buf[1]).then_inc(S("state_out1"), 16)
            pool.wait_ge(S("states_done"), 1)
            pool.dma_start(o_state_p[0, 0].rearrange("h k v -> k h v"), states[:, :, NCH - 1, :]).then_inc(S("state_p_out"), 16)
            pool.wait_ge(S("state_p_out"), 16)
            lin_full(pool, "og7")
            for b in range(8):
                pool.dma_start(Kx[:, b], mem_k_in[0, b].rearrange("(t p) h d -> p t (h d)", p=P)).then_inc(S(f"xkeys{b}"), 16)
            for b in range(8):
                if b >= 1:
                    pool.wait_ge(S("xvalues_read"), b)
                pool.dma_start(Vx[0], mem_v_in[0, b].rearrange("(t p) h d -> p t (h d)", p=P)).then_inc(S("xvalues"), 16)
            lin_full(pool, "xpast")
            pool.dma_start(b_dn[0:32, :], b_down[0]).then_inc(S("b_down"), 16)
            pool.wait_ge(S("stored"), 16 * 9)
            pool.wait_ge(S("state_out0"), 64)
            pool.wait_ge(S("state_out1"), 64)

        @block.tensor
        def _(pe):
            order = [0, 0]

            def open_bank(name):
                assert LIN[order[0]] == name, name
                order[0] += 1
                if LI[name] >= 4:
                    pe.wait_ge(S("product_out"), LI[name] - 3)

            def lin(name, parts, width, m=P):
                open_bank(name)
                for j, (l, r) in enumerate(parts):
                    mm = nc.tensor.matmul(lin_bank(name)[0:m, 0:width], l, r, start=(j == 0), stop=(j == len(parts) - 1))
                mm.then_inc(S("product_full"), 1)

            def turn(name, parts):
                assert TURN[order[1]] == name, name
                order[1] += 1
                i = TI[name]
                if i >= 2:
                    pe.wait_ge(turn_sem(name), i // 2)
                for at, src in parts:
                    k, m = src.shape[0], src.shape[-1]
                    mm = nc.tensor.transpose(turn_bank(name)[0:m, at:at + k], src, ident[0:k, 0:k])
                mm.then_inc(S("turn_full"), 1)

            def norm(k, src, nchunk, width, groups=1):
                pe.wait_ge(S("squares"), k)
                for g in range(groups):
                    for c in range(nchunk):
                        mm = nc.tensor.matmul(B[4 + g][:, 0:width], ones, src[:, (g * nchunk + c) * width:(g * nchunk + c + 1) * width],
                                              start=(c == 0), stop=(c == nchunk - 1))
                mm.then_inc(S("square_sums"), 1)

            def w(name, nk, cols):
                return slot(RI[name] % TRUNK_SLOTS)[:, 0:nk * cols].rearrange("p (c n) -> p c n", c=nk)

            def project(names, ring_name, nk, cols, rhs, width=T, m=P, first=0):
                w_ready(pe, ring_name)
                for j, name in enumerate(names):
                    a = first + m * j
                    lin(name, [(w(ring_name, nk, cols)[:, k, a:a + m], rhs[:, k, 0:width]) for k in range(nk)], width, m)

            pe.wait_ge(S("const_loaded"), 16)
            pe.wait_ge(S("gains_loaded"), 16 * 9)
            turn("gains", [(0, gain_rows[0:N_GAINS, :])])
            pe.wait_ge(S("bias_loaded"), 16)
            turn("bias", [(128 * a, bias_rows[:, a, :]) for a in range(4)])
            pe.wait_ge(S("pages"), 1)
            nc.tensor.matmul(SCORE_BANK[:, 0:8], con("spread", 16), pages[0:16, 8:16], start=True, stop=True).then_inc(S("page_rows"), 1)
            pe.wait_ge(S("x_loaded"), 48)
            for c in range(KC):
                turn(f"x{c}", [(t0, x_tok[0:n, tt, c * P:(c + 1) * P]) for tt, (t0, n) in enumerate(TILES)])
            pe.wait_ge(S("uk_loaded"), 16)
            for g in range(2):
                turn(f"uk{g}", [(128 * j, wuk[:, (4 * g + j) * 128:(4 * g + j + 1) * 128]) for j in range(4)])
            pe.wait_ge(S("mem_loaded"), 16)
            norm(1, squares, KC, T)
            for c in range(KC):
                turn(f"m{c}", [(128 * t, m_tok[:, t, c * P:(c + 1) * P]) for t in range(2)])
            pe.wait_ge(S("normed"), 1)
            project(["cq0", "cq1", "ckv"], "in_a", 8, 448, n_T)
            lin("kr", [(w("in_a", 8, 448)[:, k, C_KR:C_KR + ROPE], n_T[:, k, :]) for k in range(KC)], T, ROPE)
            lin_done(pe, "kr")
            lin("rotk", [(con("rot", 64), krT[0:64, :])], T, ROPE)
            norm(2, squares, KC, NMEM)
            norm(3, squares, 2, T)
            pe.wait_ge(S("normed"), 2)
            project([f"mk{h}" for h in range(4)], "mk", 8, 512, memT, NMEM)
            w_ready(pe, "mv")
            for t in range(2):
                lin(f"mv{t}", [(memT[:, k, t * P:(t + 1) * P], w("mv", 8, 512)[:, k, :]) for k in range(KC)], 512)
            norm(4, squares, 1, T)
            pe.wait_ge(S("normed"), 3)
            w_ready(pe, "uq")
            for h in range(H_MLA):
                lin(f"qn{h}", [(w("uq", 2, 1536)[:, k, 192 * h:192 * h + 128], cq[:, k, :]) for k in range(2)], T)
            for h in range(H_MLA):
                lin(f"qr{h}", [(w("uq", 2, 1536)[:, k, 192 * h + 128:192 * h + 192], cq[:, k, :]) for k in range(2)], T, ROPE)
            lin_done(pe, "mk3")
            for tt in range(2):
                turn(f"mkt{tt}", [(128 * h, memk[:, h, tt * P:(tt + 1) * P]) for h in range(4)])
            pe.wait_ge(S("normed"), 4)
            turn("ckvt", [(128 * tt, ckvT[:, t0:t0 + n]) for tt, (t0, n) in enumerate(TILES)])
            pe.wait_ge(S("k_roped"), 1)
            turn("krt", [(64 * tt, krT[0:64, t0:t0 + n]) for tt, (t0, n) in enumerate(TILES)])
            for h in range(H_MLA):
                lin_done(pe, f"qr{h}")
                lin(f"rot{h}", [(con("rot", 64), big3[0:64, h, :])], T, ROPE)
            turned(pe, "uk0")
            turned(pe, "uk1")
            for h in range(H_MLA):
                lin_done(pe, f"qn{h}")
                lin(f"ql{h}", [(ukT[:, 128 * h:128 * h + 128], big2[:, h, :])], T)
            pe.wait_ge(S("q_sample"), 3)
            lin("own", [(ckvT[:, PROMPT:T], Qs), (krT[0:64, PROMPT:T], Q2[0:64, 0, :])], 64, SAMPLE)
            for b in range(8):
                pe.wait_ge(S(f"lat{b % 2}"), 16 * (b // 2 + 1))
                for g in range(4):
                    turn(f"K{b}_{g}", [(128 * j, lat[b % 2][:, 4 * g + j, :]) for j in range(4)])
                pe.wait_ge(S(f"rope{b % 2}"), 16 * (b // 2 + 1))
                for g in range(2):
                    turn(f"K{b}_{4 + g}", [(128 * j, rop[b % 2][:, (4 * g + j) * 128:(4 * g + j + 1) * 128]) for j in range(4)])
                if b >= 2:
                    pe.wait_ge(S("past_scores_read"), b - 1)
                turned(pe, f"K{b}_4")
                turned(pe, f"K{b}_5")
                for i in range(16):
                    out = SCORE_BANKS[b % 2][:, 8 * i:8 * i + 8]
                    nc.tensor.matmul(out, KTl[:, 128 * i:128 * i + 128], Qs[:, 8 * b:8 * b + 8], start=True, stop=False)
                    mm = nc.tensor.matmul(out, KTr[:, 128 * (i // 2):128 * (i // 2) + 128], Q2[:, i % 2, 8 * b:8 * b + 8],
                                          start=False, stop=True)
                mm.then_inc(S("past_scores"), 1)

            def batch_softmax(a, nbh, part, own):
                pe.wait_ge(S(a + "_part_max"), 1)
                open_bank(a + "max")
                mm = nc.tensor.transpose(lin_bank(a + "max")[0:nbh, 0:P], part, ident)
                if own is not None:
                    mm = nc.tensor.transpose(lin_bank(a + "max")[0:nbh, P:P + 8], own, ident[0:8, 0:8])
                mm.then_inc(S("product_full"), 1)
                pe.wait_ge(S(a + "_max_diag"), 1)
                lin(a + "bc", [(ones[0:nbh, :], (dg if a == "m" else xdg)[0:nbh, 0:nbh])], nbh)

            batch_softmax("m", 64, mxp, own_s[0:8, :])
            pe.wait_ge(S("m_part_sum"), 1)
            lin("msum", [(ones, psums), (ones[0:8, :], own_s[0:8, :])], 64)

            def unit_scores(u):
                h, qb, kw = UNITS[u]
                if u % 16 == 0 and u < 16:
                    pe.wait_ge(S("past_scores_read"), 8)
                    pe.wait_ge(S("q_roped"), 1)
                if u >= 2:
                    pe.wait_ge(S("scores_read"), u - 1)
                out = SCORE_BANKS[u % 2][:, 0:kw]
                q0 = qb * P
                if u < 16:
                    nc.tensor.matmul(out, big4[:, h, q0:q0 + P], ckvT[:, 0:kw], start=True, stop=False)
                    mm = nc.tensor.matmul(out, big3[:, h, q0:q0 + P], krT[:, 0:kw], start=False, stop=True)
                else:
                    mm = nc.tensor.matmul(out, qx[:, h, q0:q0 + P], memk[:, h, 0:kw], start=True, stop=True)
                mm.then_inc(S("scores"), 1)

            def unit_values(u):
                h, qb, kw = UNITS[u]
                pe.wait_ge(S("probs"), u + 1)
                buf, bufT = (att, attT) if u < 16 else (xatt, xattT)
                turn(f"pt{u}", [(128 * j, buf[u % 2][:, 128 * j:128 * j + 128]) for j in range(kw // 128)])
                turned(pe, f"pt{u}")
                if u < 16:
                    parts = [(ckv_tok[:, j, :], bufT[u % 2][:, j, :]) for j in range(kw // 128)]
                else:
                    parts = [(memv[:, j, 128 * h:128 * h + 128], bufT[u % 2][:, j, :]) for j in range(kw // 128)]
                lin(f"att{u}", parts, P)

            turned(pe, "ckvt")
            unit_scores(0)
            for u in range(16):
                if u < 15:
                    unit_scores(u + 1)
                unit_values(u)
            open_bank("past")
            for b in range(8):
                out = lin_bank("past")[:, 8 * b:8 * b + 8]
                nc.tensor.matmul(out, ckv_tok[0:8, 2, :], own_s[0:8, 8 * b:8 * b + 8], start=True, stop=False)
                pe.wait_ge(S(f"lat{b % 2}"), 16 * (5 + b // 2))
                for t in range(16):
                    mm = nc.tensor.matmul(out, lat[b % 2][:, t, :], scores[:, 128 * b + 8 * t:128 * b + 8 * t + 8],
                                          start=False, stop=(t == 15))
                mm.then_inc(S("values_read") if b < 7 else S("product_full"), 1)
            pe.wait_ge(S("olat_sample"), 1)
            w_ready(pe, "uv")
            lin_done(pe, "att15")
            for h in range(H_MLA):
                lin(f"uv{h}", [(w("uv", 1, 1024)[:, 0, 128 * h:128 * h + 128], big2[:, h, :])], T)

            project([f"gq{h}" for h in range(4)], "gq", 8, 512, n_T)
            project([f"gk{h}" for h in range(4)], "gk", 8, 512, n_T)
            for half in range(2):
                project([f"gv{c}" for c in range(4 * half, 4 * half + 4)], f"gv{half}", 8, 512, n_T)
            pe.wait_ge(S("small_loaded"), 64)
            lin("ga", [(w_ga[:, 16 * k:16 * k + 16], n_T[:, k, :]) for k in range(KC)], T, 16)
            lin_done(pe, "ga")
            for h in range(H_GLA):
                lin(f"la{h}", [(w_a2_sb[:, 128 * h:128 * h + 128], ga)], T)
            lin_done(pe, "gv7")
            for c in range(NCH):
                for g in range(2):
                    turn(f"v{2 * c + g}", [(128 * j, gvT[:, 4 * g + j, CH * c:CH * c + CH]) for j in range(4)])
            for g in range(2):
                turn(f"v{8 + g}", [(128 * j, gvT[:, 4 * g + j, PROMPT:T]) for j in range(4)])
            turned(pe, "v8")
            turned(pe, "v9")

            def state_times_q(b):
                pe.wait_ge(S("state_new"), b + 1)
                for hj in range(8):
                    mm = nc.tensor.matmul(SCORE_BANK[:, 8 * hj + b:8 * hj + b + 1],
                                          st_buf[b % 2][:, hj // 2, 128 * (hj % 2):128 * (hj % 2) + 128],
                                          gqT[:, hj // 2, PROMPT + b:PROMPT + b + 1], start=True, stop=True)
                mm.then_inc(S("state_read"), 1)

            for b in range(8):
                for half in range(2):
                    lin(f"vb{2 * b + half}", [(con("pick", 8)[:, 128 * b:128 * b + 128], vs_tok[:, 512 * half:512 * half + 512])], 512)
                if b >= 1:
                    state_times_q(b - 1)
            state_times_q(7)
            pe.wait_ge(S("gla_qk"), 1)
            for c in range(NCH):
                name = f"A{c}"
                open_bank(name)
                for h in range(H_GLA):
                    mm = nc.tensor.matmul(lin_bank(name)[0:CH, CH * h:CH * h + CH], gkT[:, h, CH * c:CH * c + CH],
                                          gqT[:, h, CH * c:CH * c + CH], start=True, stop=True)
                mm.then_inc(S("product_full"), 1)
            pe.wait_ge(S("gla_kout"), 1)
            for c in range(NCH):
                turn(f"ko{c}", [(128 * h, gtmp[:, h, CH * c:CH * c + CH]) for h in range(H_GLA)])
            turned(pe, "v6")
            turned(pe, "v7")
            for h in range(H_GLA):
                for half in range(2):
                    name = f"kv{2 * h + half}"
                    open_bank(name)
                    for c in range(2 * half, 2 * half + 2):
                        turned(pe, f"ko{c}")
                        mm = nc.tensor.matmul(lin_bank(name)[:, DV * (c % 2):DV * (c % 2) + DV], ko_tok[:, c, 128 * h:128 * h + 128],
                                              v_tok[:, c, DV * h:DV * h + DV], start=True, stop=True)
                    mm.then_inc(S("product_full"), 1)
            pe.wait_ge(S("gla_scores"), 1)
            pe.wait_ge(S("states_done"), 1)
            for h in range(H_GLA):
                for j in range(2):
                    name = f"go{2 * h + j}"
                    open_bank(name)
                    for c in range(NCH):
                        out = lin_bank(name)[:, CH * c:CH * c + CH]
                        a = DV * h + 128 * j
                        mm = nc.tensor.matmul(out, v_tok[:, c, a:a + 128], AT[:, c, h, :], start=True, stop=(c == 0))
                        if c:
                            mm = nc.tensor.matmul(out, states[:, h, c - 1, 128 * j:128 * j + 128], gqT[:, h, CH * c:CH * c + CH],
                                                  start=False, stop=True)
                    mm.then_inc(S("product_full"), 1)
            for name in ("gg", "zm", "zg"):
                for half in range(2):
                    project([f"{name}{c}" for c in range(4 * half, 4 * half + 4)], f"{name}{half}", 8, 512, n_T)
            for half in range(2):
                project([f"om{c}" for c in range(4 * half, 4 * half + 4)], f"om{half}", 8, 512, big3)
            turned(pe, "ko2")
            turned(pe, "ko3")
            norm(5, squares, 2, T, groups=4)
            pe.wait_ge(S("gla_gated"), 1)
            for half in range(2):
                project([f"og{c}" for c in range(4 * half, 4 * half + 4)], f"og{half}", 8, 512, big5)
            pe.wait_ge(S("merged"), 8)
            for half in range(2):
                project([f"wo{c}" for c in range(4 * half, 4 * half + 4)], f"wo{half}", 8, 512, big4)
            norm(6, squares, KC, T)
            pe.wait_ge(S("normed"), 6)
            project([f"mq{h}" for h in range(4)], "mq", 8, 512, n_T)
            lin_done(pe, "mq3")
            for n in range(17):
                if n < 16:
                    b, t = n // 2, n % 2
                    pe.wait_ge(S(f"xkeys{b}"), 16)
                    turn(f"X{n}", [(128 * h, Kx[:, b, t, 128 * h:128 * h + 128]) for h in range(4)])
                if n >= 1:
                    m = n - 1
                    turned(pe, f"X{m}")
                    for h in range(4):
                        mm = nc.tensor.matmul(SCORE_BANK[:, 4 * m + h:4 * m + h + 1], kxT[m % 2][:, 128 * h:128 * h + 128],
                                              qx[:, h, PROMPT + m // 2:PROMPT + m // 2 + 1], start=True, stop=True)
                    mm.then_inc(S("x_scores"), 1)
            batch_softmax("x", 32, xmxp[:, 0:32], None)
            pe.wait_ge(S("x_part_sum"), 1)
            lin("xsum", [(ones, xps[:, 0:32])], 32)
            unit_scores(16)
            for u in range(16, 24):
                if u < 23:
                    unit_scores(u + 1)
                unit_values(u)
            open_bank("xpast")
            for b in range(8):
                pe.wait_ge(S("xvalues"), 16 * (b + 1))
                for h in range(4):
                    for t in range(2):
                        mm = nc.tensor.matmul(lin_bank("xpast")[:, 4 * b + h:4 * b + h + 1], Vx[0][:, t, 128 * h:128 * h + 128],
                                              xs[:, 8 * b + 4 * t + h:8 * b + 4 * t + h + 1], start=(t == 0), stop=(t == 1))
                mm.then_inc(S("xvalues_read") if b < 7 else S("product_full"), 1)
            pe.wait_ge(S("xo_sample"), 1)
            lin_done(pe, "att23")
            w_ready(pe, "mo")
            for c in range(KC):
                lin(f"mo{c}", [(w("mo", 4, 1024)[:, k, 128 * c:128 * c + 128], xo[:, k, :]) for k in range(4)], T)
            norm(7, squares, KC, T)
            pe.wait_ge(S("normed"), 7)
            for tt, (t0, n) in enumerate(TILES):
                lin(f"lg{tt}", [(n_T[:, k, t0:t0 + n], w_r[:, 32 * k:32 * k + 32]) for k in range(KC)]
                    + [(ones[0:1, 0:n], b_r[:])], NE, n)
            for i in range(6):
                tt, g = i // 2, i % 2
                t0, n = TILES[tt]
                turn(f"hn{i}", [(128 * j, n_T[:, 4 * g + j, t0:t0 + n]) for j in range(4)])
            pe.wait_ge(S("routed"), 3)
            for tt, (t0, n) in enumerate(TILES):
                lin(f"rk{tt}", [(ones[:, 0:n], take[:, j, :]) for j in range(tt)] + [(con("before")[0:n, 0:n], take[0:n, tt, :])], NE, n)
            lin("cnt", [(ones[0:n, :], take[0:n, tt, :]) for tt, (_, n) in enumerate(TILES)], NE)
            turn("cwt", [(t0, cw[0:n, tt, 0:32]) for tt, (t0, n) in enumerate(TILES)])
            turned(pe, "cwt")
            pe.wait_ge(S("b_down"), 16)
            for c in range(KC):
                lin(f"bd{c}", [(b_dn[0:32, 128 * c:128 * c + 128], cwT[0:32, :])], T)
            lin_done(pe, "bd7")

            def gather(buf):
                for k in range(KC):
                    for tt, (_, n) in enumerate(TILES):
                        mm = nc.tensor.matmul(B[2][:, CAP * k:CAP * k + CAP], hn_tok[0:n, tt, 128 * k:128 * k + 128],
                                              sel[buf][0:n, tt, :], start=(tt == 0), stop=(tt == 2))
                mm.then_inc(S("gathered"), 1)

            def expert_pair(n0, g0, q0):
                for e in range(2):
                    pe.wait_ge(S("x_expert"), g0 + e + 1)
                    for j in range(4):
                        pe.wait_ge(S(f"expert_slot{j}"), 16 * n0 + 16 * (e + 1))
                        wj = slot(j)[:].rearrange("p (c n) -> p c n", c=KC)
                        bank = B[j // 2]
                        for m in range(4):
                            at = CAP * (4 * (j % 2) + m)
                            for k in range(KC):
                                mm = nc.tensor.matmul(bank[:, at:at + CAP], wj[:, k, 128 * m:128 * m + 128], xg[e][:, k, :],
                                                      start=(k == 0), stop=(k == KC - 1))
                        mm.then_inc(S(f"slot{j}_used"), 1)
                    pe.wait_ge(S("selected"), g0 + e + 2)
                    gather(1 - e)
                    if e == 0:
                        pe.wait_ge(S("weighted"), q0 + 1)
                        for tt, (t0, n) in enumerate(TILES):
                            mm = nc.tensor.transpose(B[6][:, t0:t0 + n], wsel[0:n, tt, :], ident[0:n, 0:n])
                        mm.then_inc(S("weights_turned"), 1)
                    else:
                        pe.wait_ge(S("yT_copied"), n0 + 1)
                    pe.wait_ge(S("hidden"), n0 + e + 1)
                    for j in range(2):
                        pe.wait_ge(S(f"expert_slot{4 + j}"), 16 * n0 + 16 * (e + 1))
                        wj = slot(4 + j)[:].rearrange("p (c n) -> p c n", c=KC)
                        for m in range(4):
                            at = CAP * (4 * j + m)
                            for k in range(KC):
                                mm = nc.tensor.matmul(B[3][:, at:at + CAP], wj[:, k, 128 * m:128 * m + 128], hmid[:, k, :],
                                                      start=(k == 0), stop=(k == KC - 1))
                        mm.then_inc(S(f"slot{4 + j}_used"), 1)
                pe.wait_ge(S("yT_copied"), n0 + 2)
                for g in range(2):
                    for j in range(4):
                        mm = nc.tensor.transpose(B[4 + g][:, 128 * j:128 * j + 128], yT[:, 4 * g + j, :], ident)
                    mm.then_inc(S("y_turned"), 1)
                pe.wait_ge(S("weights_copied"), q0 + 1)
                for c in range(KC):
                    if c % 4 == 0:
                        pe.wait_ge(S("y_rows"), 2 * q0 + c // 4 + 1)
                    if c >= 2:
                        pe.wait_ge(S("added"), 8 * q0 + c - 1)
                    nc.tensor.matmul(B[6 + c % 2][:, 0:T], y_rows[:, 128 * c:128 * c + 128], wselT, start=True, stop=True)\
                        .then_inc(S("scattered"), 1)

            turned(pe, "hn4")
            turned(pe, "hn5")
            pe.wait_ge(S("selected"), 1)
            gather(0)
            with pe.Fori(0, NE // 2) as q:
                expert_pair(2 * q, 2 * q, q)
            npass = pe.value_load(whole[0:1, 0:1], min_val=1, max_val=MAX_PASS)
            with pe.If(npass > 1):
                with pe.Fori(1, npass) as p:
                    pe.wait_ge(S("selected"), p * (NE + 1) + 1)
                    gather(0)
                    with pe.Fori(0, NE // 2) as q:
                        expert_pair(p * NE + 2 * q, p * (NE + 1) + 2 * q, p * (NE // 2) + q)
            norm(8, squares, KC, T)
            pe.wait_ge(S("normed"), 8)
            for i in range(6):
                tt, g = i // 2, i % 2
                t0, n = TILES[tt]
                turn(f"y{i}", [(128 * j, n_T[:, 4 * g + j, t0:t0 + n]) for j in range(4)])
            assert order == [len(LIN), len(TURN)]

        @block.scalar
        def _(act):
            order = [0]
            steps = [0]

            def link(ins):
                steps[0] += 1
                ins.then_inc(S("act_step"), 1)
                act.wait_ge(S("act_step"), steps[0])

            def out(name, dst, func=ACT.Copy, m=P, width=T, src=None, **kw):
                assert LIN[order[0]] == name, name
                order[0] += 1
                lin_full(act, name)
                nc.scalar.activation(dst, lin_bank(name)[0:m, 0:width] if src is None else src, func, **kw).then_inc(S("product_out"), 1)

            def turn_out(name, parts):
                assert TI[name] % 2 == 1, name
                act.wait_ge(S("turn_full"), TI[name] + 1)
                for dst, m, (a, b) in parts:
                    ins = nc.scalar.copy(dst, turn_bank(name)[0:m, a:b])
                ins.then_inc(S("turned_by_act"), 1)

            def root(k, dst):
                act.wait_ge(S("inverse"), k)
                nc.scalar.activation(dst, dst, ACT.Sqrt).then_inc(S("rstd"), 1)

            turn_out("bias", [(biasT[:], P, (0, 512))])
            for c in range(1, KC, 2):
                turn_out(f"x{c}", [(h_T[:, c, :], P, (0, T))])
            act.wait_ge(S("square_sums"), 1)
            turn_out("uk1", [(ukT[:, 512:1024], P, (0, 512))])
            root(1, rstd)
            for c in range(1, KC, 2):
                turn_out(f"m{c}", [(memT[:, c, :], P, (0, NMEM))])
            for c in range(2):
                out(f"cq{c}", cq[:, c, :])
            out("ckv", ckvT)
            act.wait_ge(S("rope_cleared"), 1)
            out("kr", krT[0:64, :], m=ROPE)
            out("rotk", rotk[0:64, :], m=ROPE)
            root(2, rstd[:, :, 0:NMEM])
            root(3, rstd)
            for h in range(4):
                out(f"mk{h}", memk[:, h, :], width=NMEM)
            for t in range(2):
                out(f"mv{t}", memv[:, t, :], width=512)
            root(4, rstd)
            for h in range(H_MLA):
                out(f"qn{h}", big2[:, h, :])
            for h in range(H_MLA):
                out(f"qr{h}", big3[0:64, h, :], m=ROPE)
            turn_out("mkt1", [(squares[:, 512:1024], P, (0, 512))])
            turn_out("krt", [(kr_tok[:, 0:2, :], P, (0, 128)), (kr_tok[0:8, 2, :], 8, (128, 192))])
            for h in range(H_MLA):
                out(f"rot{h}", big5[0:64, h, :], m=ROPE)
            for h in range(H_MLA):
                out(f"ql{h}", big4[:, h, :])
            out("own", own_s[0:8, :], m=8, width=64, scale=ATTN_SCALE)
            for b in range(8):
                if b:
                    act.wait_ge(S("past_scores"), b)
                else:
                    lin_full(act, "ql7")
                for g in (1, 3, 5):
                    dst = KTl[:, 512 * g:512 * g + 512] if g < 4 else KTr[:, 512:1024]
                    turn_out(f"K{b}_{g}", [(dst, P, (0, 512))])

            def batch(a, nbh, own_n, exps_of):
                out(a + "max", (mxT if a == "m" else xmxT)[0:nbh, 0:P + own_n], m=nbh, width=P + own_n)
                out(a + "bc", (mbc if a == "m" else xmbc)[:, 0:nbh], width=nbh)
                act.wait_ge(S(a + "_shifted"), len(exps_of))
                for e in exps_of:
                    nc.scalar.activation(e, e, ACT.Exp).then_inc(S(a + "_exp"), 1)

            batch("m", 64, 8, [scores, own_s[0:8, :]])
            out("msum", mbc, width=64)

            def unit_exp(u):
                buf, nb = (att, nmx) if u < 16 else (xatt, xnmx)
                kw, v = UNITS[u][2], u % 16
                act.wait_ge(S("shifted"), u + 1)
                nc.scalar.activation(buf[u % 2][:, 0:kw], buf[u % 2][:, 0:kw], ACT.Exp, bias=nb[:, v:v + 1],
                                     accum_out=nb[:, 16 + v:17 + v]).then_inc(S("exped"), 1)

            def unit_out(u):
                h, qb, kw = UNITS[u]
                bufT = attT if u < 16 else xattT
                if TI[f"pt{u}"] % 2:
                    turn_out(f"pt{u}", [(bufT[u % 2].rearrange("p a b -> p (a b)")[:, 0:kw], P, (0, kw))])
                out(f"att{u}", (big2 if u < 16 else xo)[:, h, qb * P:qb * P + P], width=P)

            unit_exp(0)
            for u in range(16):
                if u < 15:
                    unit_exp(u + 1)
                unit_out(u)
            out("past", mxp, width=64)
            for h in range(H_MLA):
                out(f"uv{h}", big3[:, h, :])
            for h in range(4):
                out(f"gq{h}", gqT[:, h, :], scale=float(DK ** -0.5))
            for h in range(4):
                out(f"gk{h}", gkT[:, h, :])
            for c in range(KC):
                out(f"gv{c}", gvT[:, c, :])
            out("ga", ga, m=16)
            for h in range(4):
                out(f"la{h}", gla[:, h, :], ACT.Identity, bias=gT[:, GAINS["b_a"] + h:GAINS["b_a"] + h + 1])
            lin_done(act, "la3")
            link(nc.scalar.activation(gb, gla, ACT.Abs))
            link(nc.scalar.activation(gb, gb, ACT.Exp, scale=-1.0))
            nc.scalar.activation(gb, gb, ACT.Ln, bias=1.0).then_inc(S("softplus"), 1)
            for n in range(10):
                if TI[f"v{n}"] % 2:
                    c, g = n // 2, n % 2
                    dst, m = (v_tok[:, c, 512 * g:512 * g + 512], CH) if n < 8 else (vs_tok[:, 512 * g:512 * g + 512], 8)
                    turn_out(f"v{n}", [(dst, m, (0, 512))])
            act.wait_ge(S("cumulated"), 4)
            nc.scalar.activation(ge[:, :, 0:PROMPT], gb[:, :, 0:PROMPT], ACT.Exp, scale=1.0 / 16)
            nc.scalar.activation(ge[:, :, PROMPT:T], gla[:, :, PROMPT:T], ACT.Exp, scale=1.0 / 16).then_inc(S("decays"), 1)
            act.wait_ge(S("to_chunk_end"), 4)
            nc.scalar.activation(gtmp[:, :, 0:PROMPT], gtmp[:, :, 0:PROMPT], ACT.Exp, scale=1.0 / 16)
            nc.scalar.activation(gb[:, :, 0:PROMPT], gb[:, :, 0:PROMPT], ACT.Exp, scale=-1.0 / 16).then_inc(S("k_factors"), 1)
            for b in range(8):
                if b:
                    act.wait_ge(S("state_new"), b)
                for half in range(2):
                    out(f"vb{2 * b + half}", vb[:, half, :], width=512)
            act.wait_ge(S("state_read"), 8)
            nc.scalar.copy(gvT[:, :, PROMPT:T], SCORE_BANK[:, 0:64].rearrange("p (c b) -> p c b", b=8)).then_inc(S("gla_sample"), 1)
            for c in range(NCH):
                out(f"A{c}", AT[:, c].rearrange("p h t -> p (h t)"), m=CH, width=256)
            for c in range(NCH):
                if TI[f"ko{c}"] % 2:
                    turn_out(f"ko{c}", [(ko_tok[:, c, :], CH, (0, 512))])
            for n in range(8):
                h, half = n // 2, n % 2
                out(f"kv{n}", states[:, h, 2 * half:2 * half + 2, :].rearrange("p c v -> p (c v)"), width=512)
            for n in range(8):
                out(f"go{n}", gvT[:, n, 0:PROMPT], width=PROMPT)
            for c in range(KC):
                out(f"gg{c}", silu_gg[:, c, :], ACT.Silu)
            for c in range(KC):
                out(f"zm{c}", sig_zm[:, c, :], ACT.Sigmoid)
            for c in range(KC):
                out(f"zg{c}", sig_zg[:, c, :], ACT.Sigmoid)
            for c in range(KC):
                out(f"om{c}", big4[:, c, :])
            root(5, rstd_gla)
            for c in range(KC):
                out(f"og{c}", big2[:, c, :])
            for c in range(KC):
                out(f"wo{c}", big2[:, c, :])
            root(6, rstd2)
            for h in range(4):
                out(f"mq{h}", qx[:, h, :])
            for n in range(16):
                if TI[f"X{n}"] % 2:
                    if n >= 2:
                        act.wait_ge(S("x_scores"), n - 1)
                    turn_out(f"X{n}", [(kxT[n % 2], P, (0, 512))])
            batch("x", 32, 0, [xs])
            out("xsum", xmbc[:, 0:32], width=32)
            unit_exp(16)
            for u in range(16, 24):
                if u < 23:
                    unit_exp(u + 1)
                unit_out(u)
            out("xpast", xps[:, 0:32], width=32)
            for c in range(KC):
                out(f"mo{c}", big4[:, c, :])
            root(7, rstd2)
            for tt, (_, n) in enumerate(TILES):
                out(f"lg{tt}", logits[0:n, 32 * tt:32 * tt + 32], m=n, width=NE)
            for i in range(6):
                if TI[f"hn{i}"] % 2:
                    tt, g = i // 2, i % 2
                    n = TILES[tt][1]
                    turn_out(f"hn{i}", [(hn_tok[0:n, tt, 512 * g:512 * g + 512], n, (0, 512))])
            for tt, (_, n) in enumerate(TILES):
                act.wait_ge(S("top_shifted"), tt + 1)
                nc.scalar.activation(e4[0:n, 8 * tt:8 * tt + 4], e4[0:n, 8 * tt:8 * tt + 4], ACT.Exp,
                                     accum_out=e4[0:n, 8 * tt + 4:8 * tt + 5]).then_inc(S("top_exp"), 1)
            for tt, (_, n) in enumerate(TILES):
                out(f"rk{tt}", posm[0:n, tt, 0:NE], m=n, width=NE)
            out("cnt", cnts[:, 0:NE], width=NE)
            if TI["cwt"] % 2:
                turn_out("cwt", [(cwT[0:NE, :], NE, (0, T))])
            for c in range(KC):
                out(f"bd{c}", acc[:, c, :])

            def gathered(n, buf):
                act.wait_ge(S("gathered"), n)
                nc.scalar.copy(xg[buf].rearrange("p a b -> p (a b)"), B[2][:]).then_inc(S("x_expert"), 1)

            def expert_pair(n0, g0, q0):
                for e in range(2):
                    act.wait_ge(S("gate"), n0 + e + 1)
                    nc.scalar.activation(sg, gate, ACT.Sigmoid, scale=1.702).then_inc(S("sigmoid"), 1)
                    gathered(g0 + e + 2, 1 - e)
                    if e == 0:
                        act.wait_ge(S("weights_turned"), q0 + 1)
                        nc.scalar.copy(wselT, B[6][:, 0:T]).then_inc(S("weights_copied"), 1)
                    act.wait_ge(S("slot5_used"), n0 + e + 1)
                    nc.scalar.copy(yT[:, :, CAP * e:CAP * e + CAP], B[3][:].rearrange("p (a b) -> p a b", b=CAP)).then_inc(S("yT_copied"), 1)
                for g in range(2):
                    act.wait_ge(S("y_turned"), 2 * q0 + g + 1)
                    nc.scalar.copy(y_rows[:, 512 * g:512 * g + 512], B[4 + g][:]).then_inc(S("y_rows"), 1)

            gathered(1, 0)
            with act.Fori(0, NE // 2) as q:
                expert_pair(2 * q, 2 * q, q)
            act.wait_ge(S("npass"), 1)
            npass = act.value_load(whole[0:1, 0:1], min_val=1, max_val=MAX_PASS)
            with act.If(npass > 1):
                with act.Fori(1, npass) as p:
                    gathered(p * (NE + 1) + 1, 0)
                    with act.Fori(0, NE // 2) as q:
                        expert_pair(p * NE + 2 * q, p * (NE + 1) + 2 * q, p * (NE // 2) + q)
            root(8, rstd2)
            for i in range(6):
                if TI[f"y{i}"] % 2:
                    tt, g = i // 2, i % 2
                    n = TILES[tt][1]
                    turn_out(f"y{i}", [(y_tok[0:n, tt, 512 * g:512 * g + 512], n, (0, 512))])
            assert order[0] == len(LIN)

        @block.vector
        def _(dve):
            V = nc.vector
            steps = [0]

            def link(ins):
                steps[0] += 1
                ins.then_inc(S("dve_step"), 1)
                dve.wait_ge(S("dve_step"), steps[0])

            def turn_out(name, parts):
                assert TI[name] % 2 == 0, name
                dve.wait_ge(S("turn_full"), TI[name] + 1)
                for dst, m, (a, b) in parts:
                    ins = V.tensor_copy(dst, turn_bank(name)[0:m, a:b])
                ins.then_inc(S("turned_by_dve"), 1)

            def square(src, dst):
                V.tensor_tensor(dst, src, src, ALU.mult).then_inc(S("squares"), 1)

            def scale_by_rms(k, src, dst, gain, nchunk, width, dim, rs, groups=1):
                dve.wait_ge(S("square_sums"), k)
                for g in range(groups):
                    ins = V.tensor_scalar(rs[:, g, 0:width], B[4 + g][:, 0:width], 1.0 / dim, EPS, ALU.mult, ALU.add)
                link(ins)
                V.reciprocal(rs[:, :, 0:width], rs[:, :, 0:width]).then_inc(S("inverse"), 1)
                dve.wait_ge(S("rstd"), k)
                for c in range(nchunk * groups):
                    r = GAINS[gain] + c % nchunk
                    ins = V.scalar_tensor_tensor(out=dst[:, c, :], in0=src[:, c, :], scalar=gT[:, r:r + 1], in1=rs[:, c // nchunk, 0:width],
                                                 op0=ALU.mult, op1=ALU.mult)
                ins.then_inc(S("normed"), 1)

            def flat(v):
                return v.rearrange("p a b -> p (a b)")

            def bc(v, shape):
                return v.to_broadcast(shape)

            V.memset(krT[64:128, :], 0.0)
            V.memset(big3[64:128, :, :], 0.0).then_inc(S("rope_cleared"), 1)
            dve.wait_ge(S("pages_loaded"), 16)
            V.tensor_copy(pages[0:16, 8:16], pages[0:16, 0:8].bitcast(I32)).then_inc(S("pages"), 1)
            turn_out("gains", [(gT[:], P, (0, N_GAINS))])
            dve.wait_ge(S("page_rows"), 1)
            V.tensor_scalar(idx, SCORE_BANK[:, 0:8], con("within"), None, ALU.add).then_inc(S("idx"), 1)
            for c in range(0, KC, 2):
                turn_out(f"x{c}", [(h_T[:, c, :], P, (0, T))])
            dve.wait_ge(turn_sem("x7"), TI["x7"] // 2 + 1)
            dve.wait_ge(turn_sem("x6"), TI["x6"] // 2 + 1)
            square(resid[:], squares)
            turn_out("uk0", [(ukT[:, 0:512], P, (0, 512))])
            scale_by_rms(1, h_T, n_T, "g_attn", KC, T, D, rstd)
            for c in range(0, KC, 2):
                turn_out(f"m{c}", [(memT[:, c, :], P, (0, NMEM))])
            turned(dve, "m7")
            turned(dve, "m6")
            square(flat(memT), squares[:, 0:KC * NMEM])
            scale_by_rms(2, memT, memT, "g_mem", KC, NMEM, D, rstd)
            lin_done(dve, "cq1")
            square(flat(cq), squares[:, 0:2 * T])
            scale_by_rms(3, cq, cq, "g_q", 2, T, 256, rstd)
            lin_done(dve, "rotk")
            V.tensor_tensor(krT[0:64, :], krT[0:64, :], con("cos", 64), ALU.mult)
            link(V.tensor_tensor(rotk[0:64, :], rotk[0:64, :], con("sin", 64), ALU.mult))
            V.tensor_tensor(krT[0:64, :], krT[0:64, :], rotk[0:64, :], ALU.add).then_inc(S("k_roped"), 1)
            square(ckvT, squares[:, 0:T])
            scale_by_rms(4, ckvT[:, None, :], ckvT[:, None, :], "g_kv", 1, T, LORA, rstd)
            turn_out("mkt0", [(squares[:, 0:512], P, (0, 512))])
            turn_out("ckvt", [(flat(ckv_tok)[:, 0:256], P, (0, 256)), (ckv_tok[0:8, 2, :], 8, (256, 384))])
            lin_done(dve, "rot7")
            V.tensor_tensor(big3[0:64], big3[0:64], bc(con("cos", 64)[:, None, :], [64, 8, T]), ALU.mult)
            link(V.tensor_tensor(big5[0:64], big5[0:64], bc(con("sin", 64)[:, None, :], [64, 8, T]), ALU.mult))
            V.tensor_tensor(big3[0:64], big3[0:64], big5[0:64], ALU.add).then_inc(S("q_roped"), 1)
            link(V.memset(Q2, 0.0))
            dve.wait_ge(S("q_roped"), 1)
            for i in range(2):
                V.tensor_copy(Q2[64 * i:64 * i + 64, i, :].rearrange("p (b h) -> p h b", b=8), big3[0:64, :, PROMPT:T]).then_inc(S("q_sample"), 1)
            lin_done(dve, "ql7")
            V.tensor_copy(Qs.rearrange("p (b h) -> p h b", b=8), big4[:, :, PROMPT:T]).then_inc(S("q_sample"), 1)
            for b in range(8):
                if b:
                    dve.wait_ge(S("past_scores"), b)
                for g in (0, 2, 4):
                    dst = KTl[:, 512 * g:512 * g + 512] if g < 4 else KTr[:, 0:512]
                    turn_out(f"K{b}_{g}", [(dst, P, (0, 512))])
                dve.wait_ge(S("past_scores"), b + 1)
                V.tensor_scalar(scores[:, 128 * b:128 * b + 128], SCORE_BANKS[b % 2][:, 0:128], ATTN_SCALE, None,
                                ALU.mult).then_inc(S("past_scores_read"), 1)
            lin_done(dve, "own")
            link(V.tensor_tensor(own_s[0:8, :], own_s[0:8, :], con("own", 8), ALU.add))

            def batch(a, nbh, sc, nb, ntile, bufs, own):
                part, mT, g1, diag, mb, ps, inv = bufs
                by_bh = sc.rearrange("p (b i h) -> p b h i", b=nb, i=ntile)
                V.tensor_reduce(part[:, 0:nbh].rearrange("p (b h) -> p b h", b=nb), by_bh, AX, ALU.max).then_inc(S(a + "_part_max"), 1)
                lin_done(dve, a + "max")
                link(V.tensor_reduce(g1[0:nbh, 0:1], mT[0:nbh, 0:P + (8 if own is not None else 0)], AX, ALU.max))
                V.tensor_scalar(diag[0:nbh, 0:nbh], ident[0:nbh, 0:nbh], g1[0:nbh, 0:1], None, ALU.mult).then_inc(S(a + "_max_diag"), 1)
                lin_done(dve, a + "bc")
                V.tensor_tensor(by_bh, by_bh, bc(mb[:, 0:nbh].rearrange("p (b h o) -> p b h o", b=nb, o=1), [P, nb, nbh // nb, ntile]),
                                ALU.subtract).then_inc(S(a + "_shifted"), 1)
                n = 1
                if own is not None:
                    n = 2
                    V.tensor_tensor(own, own, mb[0:8, 0:nbh], ALU.subtract).then_inc(S(a + "_shifted"), 1)
                dve.wait_ge(S(a + "_exp"), n)
                V.tensor_reduce(ps[:, 0:nbh].rearrange("p (b h) -> p b h", b=nb), by_bh, AX, ALU.add).then_inc(S(a + "_part_sum"), 1)
                lin_done(dve, a + "sum")
                link(V.reciprocal(inv[:, 0:nbh], mb[:, 0:nbh]))

            dve.wait_ge(S("past_scores_read"), 8)
            batch("m", 64, scores, 8, 16, (mxp, mxT, gm, dg, mbc, psums, rinv), own_s[0:8, :])

            def unit_scores(u):
                buf, nb = (att, nmx) if u < 16 else (xatt, xnmx)
                h, qb, kw = UNITS[u]
                v = u % 16
                dve.wait_ge(S("scores"), u + 1)
                if u >= 2 and u != 16 and u != 17:
                    dve.wait_ge(S("turn_full"), TI[f"pt{u - 2}"] + 1)
                s, ps = buf[u % 2][:, 0:kw], SCORE_BANKS[u % 2][:, 0:kw]
                if u < 16:
                    V.scalar_tensor_tensor(out=s, in0=ps, scalar=ATTN_SCALE, in1=con("causal")[:, 256 - kw:256], op0=ALU.mult, op1=ALU.add)\
                        .then_inc(S("scores_read"), 1)
                else:
                    V.tensor_scalar(s, ps, MEM_SCALE, None, ALU.mult).then_inc(S("scores_read"), 1)
                dve.wait_ge(S("scores_read"), u + 1)
                V.tensor_reduce(nb[:, v:v + 1], s, AX, ALU.max, negate=True).then_inc(S("shifted"), 1)

            def unit_probs(u):
                buf, nb, bufT = (att, nmx, attT) if u < 16 else (xatt, xnmx, xattT)
                kw, v = UNITS[u][2], u % 16
                dve.wait_ge(S("exped"), u + 1)
                link(V.reciprocal(nb[:, 32 + v:33 + v], nb[:, 16 + v:17 + v]))
                s = buf[u % 2][:, 0:kw]
                V.tensor_scalar(s, s, nb[:, 32 + v:33 + v], None, ALU.mult).then_inc(S("probs"), 1)
                if TI[f"pt{u}"] % 2 == 0:
                    turn_out(f"pt{u}", [(flat(bufT[u % 2])[:, 0:kw], P, (0, kw))])

            unit_scores(0)
            for u in range(16):
                if u < 15:
                    unit_scores(u + 1)
                unit_probs(u)
            lin_done(dve, "past")
            V.tensor_tensor(big2[:, :, PROMPT:T], mxp.rearrange("p (b h) -> p h b", b=8), rinv.rearrange("p (b h) -> p h b", b=8),
                            ALU.mult).then_inc(S("olat_sample"), 1)
            for n in range(10):
                if TI[f"v{n}"] % 2 == 0:
                    c, g = n // 2, n % 2
                    dst, m = (v_tok[:, c, 512 * g:512 * g + 512], CH) if n < 8 else (vs_tok[:, 512 * g:512 * g + 512], 8)
                    turn_out(f"v{n}", [(dst, m, (0, 512))])
            dve.wait_ge(S("softplus"), 1)
            link(V.scalar_tensor_tensor(out=gla, in0=gla, scalar=0.0, in1=gb, op0=ALU.min, op1=ALU.subtract))
            for h in range(4):
                V.tensor_tensor_scan(gb[:, h, 0:PROMPT], con("carry"), gla[:, h, 0:PROMPT], 0.0, ALU.mult, ALU.add).then_inc(S("cumulated"), 1)
            dve.wait_ge(S("cumulated"), 4)
            for h in range(4):
                bh = gb[:, h, 0:PROMPT].rearrange("p (c t) -> p c t", c=NCH)
                V.tensor_tensor(gtmp[:, h, 0:PROMPT].rearrange("p (c t) -> p c t", c=NCH), bc(bh[:, :, CH - 1:CH], [P, NCH, CH]), bh,
                                ALU.subtract).then_inc(S("to_chunk_end"), 1)
            dve.wait_ge(S("k_factors"), 1)
            pr = slice(0, PROMPT)
            V.tensor_tensor(gtmp[:, :, pr], gtmp[:, :, pr], gkT[:, :, pr], ALU.mult).then_inc(S("gla_kout"), 1)
            V.tensor_tensor(gkT[:, :, pr], gkT[:, :, pr], gb[:, :, pr], ALU.mult)
            V.tensor_tensor(gqT[:, :, pr], gqT[:, :, pr], ge[:, :, pr], ALU.mult).then_inc(S("gla_qk"), 1)
            for b in range(8):
                st = st_buf[b % 2]
                t = PROMPT + b
                dve.wait_ge(S(f"state_in{b % 2}"), 16 * (b // 2 + 1))
                for h in range(4):
                    ins = V.tensor_scalar(st[:, h, :], st[:, h, :], ge[:, h, t:t + 1], None, ALU.mult)
                link(ins)
                lin_done(dve, f"vb{2 * b + 1}")
                for h in range(4):
                    ins = V.scalar_tensor_tensor(out=st[:, h, :], in0=vb[:, h // 2, DV * (h % 2):DV * (h % 2) + DV], scalar=gkT[:, h, t:t + 1],
                                                 in1=st[:, h, :], op0=ALU.mult, op1=ALU.add)
                ins.then_inc(S("state_new"), 1)
            lin_done(dve, "A3")
            AT3 = AT.rearrange("p c h t -> p (c h) t")
            link(V.tensor_scalar(AT3, AT3, 3.0e38, -3.0e38, ALU.min, ALU.max))
            V.tensor_tensor(AT3, AT3, bc(con("upto", CH)[:, None, :], [CH, 16, CH]), ALU.mult).then_inc(S("gla_scores"), 1)
            for c in range(NCH):
                if TI[f"ko{c}"] % 2 == 0:
                    turn_out(f"ko{c}", [(ko_tok[:, c, :], CH, (0, 512))])
            lin_done(dve, "kv7")
            for c in range(1, NCH):
                for h in range(4):
                    ins = V.scalar_tensor_tensor(out=states[:, h, c, :], in0=states[:, h, c - 1, :], scalar=ge[:, h, CH * c + CH - 1:CH * c + CH],
                                                 in1=states[:, h, c, :], op0=ALU.mult, op1=ALU.add)
                if c < NCH - 1:
                    link(ins)
            ins.then_inc(S("states_done"), 1)
            lin_done(dve, "go7")
            dve.wait_ge(S("gla_sample"), 1)
            dve.wait_ge(S("state_out0"), 64)
            dve.wait_ge(S("state_out1"), 64)
            square(flat(gvT), squares)
            scale_by_rms(5, gvT, gvT, "g_gla", 2, T, DV, rstd_gla, groups=4)
            dve.wait_ge(S("normed"), 5)
            lin_done(dve, "gg7")
            V.tensor_tensor(gvT, gvT, silu_gg, ALU.mult).then_inc(S("gla_gated"), 1)
            lin_done(dve, "om7")
            link(V.tensor_tensor(big4, big4, sig_zm, ALU.mult))
            for c in range(KC):
                lin_done(dve, f"og{c}")
                link(V.tensor_tensor(big2[:, c, :], big2[:, c, :], sig_zg[:, c, :], ALU.mult))
                V.tensor_tensor(big4[:, c, :], big4[:, c, :], big2[:, c, :], ALU.add).then_inc(S("merged"), 1)

            def add_to_residual(name, src):
                for c in range(KC):
                    lin_done(dve, f"{name}{c}")
                    ins = V.tensor_tensor(h_T[:, c, :], h_T[:, c, :], src[:, c, :], ALU.add)
                link(ins)

            add_to_residual("wo", big2)
            square(resid[:], squares)
            scale_by_rms(6, h_T, n_T, "g_cross", KC, T, D, rstd2)
            for n in range(16):
                if TI[f"X{n}"] % 2 == 0:
                    if n >= 2:
                        dve.wait_ge(S("x_scores"), n - 1)
                    turn_out(f"X{n}", [(kxT[n % 2], P, (0, 512))])
            dve.wait_ge(S("x_scores"), 16)
            link(V.tensor_scalar(xs, SCORE_BANK[:, 0:64], MEM_SCALE, None, ALU.mult))
            batch("x", 32, xs, 8, 2, (xmxp, xmxT, xgm, xdg, xmbc, xps, xrinv), None)
            unit_scores(16)
            for u in range(16, 24):
                if u < 23:
                    unit_scores(u + 1)
                unit_probs(u)
            lin_done(dve, "xpast")
            V.tensor_tensor(xo[:, :, PROMPT:T], xps[:, 0:32].rearrange("p (b h) -> p h b", b=8), xrinv[:, 0:32].rearrange("p (b h) -> p h b", b=8),
                            ALU.mult).then_inc(S("xo_sample"), 1)
            add_to_residual("mo", big4)
            square(resid[:], squares)
            scale_by_rms(7, h_T, n_T, "g_ffn", KC, T, D, rstd2)
            V.memset(posm, FAR)
            link(V.memset(take, 0.0))
            for i in range(6):
                if TI[f"hn{i}"] % 2 == 0:
                    tt, g = i // 2, i % 2
                    n = TILES[tt][1]
                    turn_out(f"hn{i}", [(hn_tok[0:n, tt, 512 * g:512 * g + 512], n, (0, 512))])
            for tt, (_, n) in enumerate(TILES):
                lin_done(dve, f"lg{tt}")
                lg, t8 = logits[0:n, 32 * tt:32 * tt + 32], top8[0:n, 8 * tt:8 * tt + 8]
                ti, tf = top_i[0:n, 8 * tt:8 * tt + 8], top_f[0:n, 8 * tt:8 * tt + 8]
                link(V.max(t8, lg))
                link(V.max_index(ti, t8, lg))
                V.tensor_copy(tf, ti)
                V.tensor_scalar(e4[0:n, 8 * tt:8 * tt + 4], t8[:, 0:4], t8[:, 0:1], None, ALU.subtract).then_inc(S("top_shifted"), 1)
            for tt, (_, n) in enumerate(TILES):
                tf, e = top_f[0:n, 8 * tt:8 * tt + 8], e4[0:n, 8 * tt:8 * tt + 8]
                dve.wait_ge(S("top_exp"), tt + 1)
                link(V.reciprocal(e[:, 5:6], e[:, 4:5]))
                link(V.tensor_scalar(e[:, 0:4], e[:, 0:4], e[:, 5:6], None, ALU.mult))
                c32 = con("count", n)[:, 0:NE]
                link(V.tensor_scalar(cw[0:n, tt, 0:NE], c32, tf[:, 0:1], e[:, 0:1], ALU.is_equal, ALU.mult))
                for k in range(1, TOPK):
                    link(V.tensor_scalar(tmp32[0:n, :], c32, tf[:, k:k + 1], e[:, k:k + 1], ALU.is_equal, ALU.mult))
                    link(V.tensor_tensor(cw[0:n, tt, 0:NE], cw[0:n, tt, 0:NE], tmp32[0:n, :], ALU.add))
                V.tensor_scalar(take[0:n, tt, :], cw[0:n, tt, 0:NE], 0.0, None, ALU.is_gt).then_inc(S("routed"), 1)
            if TI["cwt"] % 2 == 0:
                turn_out("cwt", [(cwT[0:NE, :], NE, (0, T))])
            lin_done(dve, "rk2")
            for tt, (_, n) in enumerate(TILES):
                ins = V.tensor_scalar(logits[0:n, 32 * tt:32 * tt + 32], take[0:n, tt, :], -FAR, FAR, ALU.mult, ALU.add)
            link(ins)
            for tt, (_, n) in enumerate(TILES):
                ins = V.tensor_tensor(posm[0:n, tt, 0:NE], posm[0:n, tt, 0:NE], logits[0:n, 32 * tt:32 * tt + 32], ALU.add)
            link(ins)

            def select(buf, col):
                for tt, (_, n) in enumerate(TILES):
                    ins = V.tensor_scalar(sel[buf][0:n, tt, :], con("count", n), col(tt, n), None, ALU.is_equal)
                ins.then_inc(S("selected"), 1)

            select(0, lambda tt, n: posm[0:n, tt, 0:1])
            lin_done(dve, "cnt")
            link(V.tensor_reduce(cnts[0:1, 32:33], cnts[0:1, 0:NE], AX, ALU.max))
            link(V.tensor_scalar(cnts[0:1, 33:34], cnts[0:1, 32:33], float(CAP), 1.0, ALU.is_gt, ALU.add))
            for j in range(2, MAX_PASS):
                link(V.scalar_tensor_tensor(out=cnts[0:1, 32 + j:33 + j], in0=cnts[0:1, 32:33], scalar=float(CAP * j), in1=cnts[0:1, 31 + j:32 + j],
                                            op0=ALU.is_gt, op1=ALU.add))
            V.tensor_copy(whole[0:1, 0:1], cnts[0:1, 31 + MAX_PASS:32 + MAX_PASS]).then_inc(S("npass"), 1)
            lin_done(dve, "bd7")

            def expert_pair(q, n0, g0, q0):
                V.tensor_copy(curp, posm[:, :, bass.ds(2 * q, 3)])
                V.tensor_copy(curw, cw[:, :, bass.ds(2 * q, 2)])
                V.tensor_copy(flat(curb), biasT[:, bass.ds(32 * q, 32)]).then_inc(S("pair_columns"), 1)
                dve.wait_ge(S("pair_columns"), q0 + 1)
                select(1, lambda tt, n: curp[0:n, tt, 1:2])
                for e in range(2):
                    for tt, (_, n) in enumerate(TILES):
                        ins = V.tensor_scalar(wsel[0:n, tt, CAP * e:CAP * e + CAP], con("count", n), curp[0:n, tt, e:e + 1],
                                              curw[0:n, tt, e:e + 1], ALU.is_equal, ALU.mult)
                ins.then_inc(S("weighted"), 1)
                for e in range(2):
                    m = n0 + e
                    dve.wait_ge(S("slot1_used"), m + 1)
                    V.tensor_tensor(gate, B[0][:].rearrange("p (a b) -> p a b", b=CAP), bc(curb[:, e, 0:8].rearrange("p (a o) -> p a o", o=1),
                                    [P, 8, CAP]), ALU.add).then_inc(S("gate_biased"), 1)
                    dve.wait_ge(S("gate_biased"), m + 1)
                    V.tensor_scalar(gate, gate, 7.0, None, ALU.min).then_inc(S("gate"), 1)
                    if e == 1:
                        dve.wait_ge(S("x_expert"), g0 + 2)
                        select(0, lambda tt, n: curp[0:n, tt, 2:3])
                    dve.wait_ge(S("slot3_used"), m + 1)
                    V.tensor_tensor(up, B[1][:].rearrange("p (a b) -> p a b", b=CAP), bc(curb[:, e, 8:16].rearrange("p (a o) -> p a o", o=1),
                                    [P, 8, CAP]), ALU.add).then_inc(S("up_biased"), 1)
                    dve.wait_ge(S("up_biased"), m + 1)
                    V.tensor_scalar(up, up, 7.0, -7.0, ALU.min, ALU.max).then_inc(S("up_clipped"), 1)
                    dve.wait_ge(S("up_clipped"), m + 1)
                    V.scalar_tensor_tensor(out=up, in0=up, scalar=1.0, in1=gate, op0=ALU.add, op1=ALU.mult).then_inc(S("gated_up"), 1)
                    dve.wait_ge(S("gated_up"), m + 1)
                    dve.wait_ge(S("sigmoid"), m + 1)
                    V.tensor_tensor(hmid, up, sg, ALU.mult).then_inc(S("hidden"), 1)
                for c in range(KC):
                    dve.wait_ge(S("scattered"), 8 * q0 + c + 1)
                    V.tensor_tensor(acc[:, c, :], acc[:, c, :], B[6 + c % 2][:, 0:T], ALU.add).then_inc(S("added"), 1)

            with dve.Fori(0, NE // 2) as q:
                expert_pair(q, 2 * q, 2 * q, q)
            dve.wait_ge(S("npass"), 1)
            npass = dve.value_load(whole[0:1, 0:1], min_val=1, max_val=MAX_PASS)
            with dve.If(npass > 1):
                with dve.Fori(1, npass) as p:
                    V.tensor_scalar(posm, posm, float(-CAP), None, ALU.add).then_inc(S("next_ranks"), 1)
                    dve.wait_ge(S("next_ranks"), p)
                    select(0, lambda tt, n: posm[0:n, tt, 0:1])
                    with dve.Fori(0, NE // 2) as q:
                        expert_pair(q, p * NE + 2 * q, p * (NE + 1) + 2 * q, p * (NE // 2) + q)
            dve.wait_ge(S("added"), npass * (8 * NE // 2))
            link(V.tensor_tensor(resid[:], resid[:], flat(acc), ALU.add))
            square(resid[:], squares)
            scale_by_rms(8, h_T, n_T, "g_final", KC, T, D, rstd2)
            for i in range(6):
                if TI[f"y{i}"] % 2 == 0:
                    tt, g = i // 2, i % 2
                    n = TILES[tt][1]
                    turn_out(f"y{i}", [(y_tok[0:n, tt, 512 * g:512 * g + 512], n, (0, 512))])


_INS = ["x_prompt", "x_sample", "cache_kv_latent", "cache_k_rope", "state_gla", "cache_mem_k", "cache_mem_v", "page_table", "mem_prompt",
        "g_attn", "w_in", "g_q", "g_kv", "w_uq", "w_uk", "w_uv", "w_a2", "b_a", "g_gla", "w_o_mla", "w_o_gla", "w_out", "g_mem", "w_mk",
        "w_mv", "g_cross", "w_mq", "w_mo", "g_ffn", "w_router", "b_router", "w_gate_up", "b_gate_up", "w_down", "b_down", "g_final"]
_OUTS = [(1, 256, 1024), (8, 1, 1024), (1, 1, 256, 128), (1, 1, 256, 64), (1, 1, 4, 128, 256), (1, 1, 256, 4, 128), (1, 1, 256, 4, 128),
         (1, 8, 1, 128), (1, 8, 1, 64), (1, 8, 4, 128, 256)]


def kernel(**inputs):
    import concourse.bacc as _bacc
    from concourse.bass_utils import run_bass_kernel_spmd as _run

    nc = _bacc.Bacc("TRN2", target_bir_lowering=False, num_devices=1)
    arrays, ins = {}, []
    for name in _INS:
        a = np.ascontiguousarray(inputs[name])
        arrays[f"in_{name}"] = a
        ins.append(nc.dram_tensor(f"in_{name}", a.shape, mybir.dt.from_np(a.dtype), kind="ExternalInput").ap())
    table = constants()
    arrays["in_constants"] = table
    consts = nc.dram_tensor("in_constants", table.shape, F32, kind="ExternalInput").ap()
    outs = [nc.dram_tensor(f"out_{i}", shape, F32, kind="ExternalOutput").ap() for i, shape in enumerate(_OUTS)]
    build(nc, ins, outs, consts)
    r = _run(nc, [arrays], core_ids=[0])
    return tuple(r.results[0][f"out_{i}"] for i in range(len(_OUTS)))
```

```python
from contextlib import ExitStack

import numpy as np

import concourse.bass as bass
from concourse import mybir

ALU = mybir.AluOpType
ACT = mybir.ActivationFunctionType
F32 = mybir.dt.float32
I32 = mybir.dt.int32
U32 = mybir.dt.uint32
AX = mybir.AxisListType.X

P = 128
D = 1024
KC = D // P
PROMPT, SAMPLE = 256, 8
T = PROMPT + SAMPLE
TILES = [(0, 128), (128, 128), (256, 8)]
H_MLA, NOPE, ROPE, LORA = 8, 128, 64, 128
H_GLA, DK, DV, CH = 4, 128, 256, 64
NCH = PROMPT // CH
H_MEM, NMEM = 4, 256
NE, TOPK, DFF = 32, 4, 1024
CAP = 64
MAX_PASS = -(-T // CAP)
PAST, PAGE, NPAGES = 2048, 128, 16
EPS = 1e-6
ATTN_SCALE = float((NOPE + ROPE) ** -0.5)
MEM_SCALE = float(P ** -0.5)
FAR = 1e4
NEG = -1e30
SLOT = 4096
TRUNK_SLOTS, MOE_SLOTS = 4, 6

C_CQ, C_CKV, C_KR, C_GQ, C_GK, C_GV, C_GG, C_GA, C_ZM, C_ZG = 0, 256, 384, 448, 960, 1472, 2496, 3520, 3536, 4560

GAINS = {"g_attn": 0, "g_mem": 8, "g_cross": 16, "g_ffn": 24, "g_final": 32, "g_q": 40, "g_kv": 42, "g_gla": 43, "b_a": 45}
N_GAINS = 49

CONSTS = {}
for _name, _n in [("ident", 128), ("ones", 128), ("before", 128), ("rot", 64), ("cos", T), ("sin", T),
                  ("carry", PROMPT), ("count", 64), ("causal", 256), ("own", 64), ("upto", 64), ("spread", 128),
                  ("within", 1), ("pick", 8 * 128)]:
    CONSTS[_name] = (sum(n for _, n in CONSTS.values()), _n)
N_CONST = sum(n for _, n in CONSTS.values())


def constants():
    f = np.float32
    c = np.zeros((P, N_CONST), f)

    def put(name, a):
        o, n = CONSTS[name]
        c[:a.shape[0], o:o + n] = a

    i = np.arange(P)
    put("ident", np.eye(P, dtype=f))
    put("ones", np.ones((P, P), f))
    put("before", (i[:, None] < i[None, :]).astype(f))
    r = np.zeros((64, 64), f)
    for a in range(32):
        r[a + 32, a] = -1
        r[a, a + 32] = 1
    put("rot", r)
    inv = (f(10000.0) ** (-np.arange(32, dtype=f) * f(2.0) / f(64))).astype(f)
    pos = np.concatenate([np.arange(PROMPT), np.full(SAMPLE, PAST)]).astype(f)
    ang = (pos[None, :] * inv[:, None]).astype(f)
    put("cos", np.tile(np.cos(ang), (2, 1)))
    put("sin", np.tile(np.sin(ang), (2, 1)))
    put("carry", np.tile((np.arange(PROMPT) % CH != 0).astype(f), (P, 1)))
    put("count", np.tile(np.arange(64, dtype=f), (P, 1)))
    put("causal", np.where(np.arange(256)[None, :] - 128 <= i[:, None], 0, NEG).astype(f))
    own = np.full((8, 8, 8), NEG, f)
    for b in range(8):
        own[b, b] = 0
    put("own", own.reshape(8, 64))
    s = np.arange(CH)
    put("upto", (s[:, None] <= s[None, :]).astype(f))
    put("spread", np.where(i[None, :] // 8 == np.arange(16)[:, None], 8, 0).astype(f))
    put("within", (i % 8).astype(f)[:, None])
    pick = np.zeros((8, 8, 128), f)
    for b in range(8):
        pick[b, b] = 1
    put("pick", pick.reshape(8, 1024))
    return c


LIN = (["cq0", "cq1", "ckv", "kr", "rotk"] + [f"mk{h}" for h in range(4)] + ["mv0", "mv1"]
       + [f"qn{h}" for h in range(8)] + [f"qr{h}" for h in range(8)] + [f"rot{h}" for h in range(8)]
       + [f"ql{h}" for h in range(8)] + ["own", "mmax", "mbc", "msum"] + [f"att{u}" for u in range(16)] + ["past"]
       + [f"uv{h}" for h in range(8)]
       + [f"gq{h}" for h in range(4)] + [f"gk{h}" for h in range(4)] + [f"gv{c}" for c in range(8)] + ["ga"]
       + [f"la{h}" for h in range(4)] + [f"vb{n}" for n in range(16)] + [f"A{c}" for c in range(4)] + [f"kv{n}" for n in range(8)]
       + [f"go{n}" for n in range(8)]
       + [f"gg{c}" for c in range(8)] + [f"zm{c}" for c in range(8)] + [f"zg{c}" for c in range(8)]
       + [f"om{c}" for c in range(8)] + [f"og{c}" for c in range(8)] + [f"wo{c}" for c in range(8)]
       + [f"mq{h}" for h in range(4)] + ["xmax", "xbc", "xsum"] + [f"att{u}" for u in range(16, 24)] + ["xpast"]
       + [f"mo{c}" for c in range(8)] + ["lg0", "lg1", "lg2", "rk0", "rk1", "rk2", "cnt"] + [f"bd{c}" for c in range(8)])
LI = {n: i for i, n in enumerate(LIN)}

TURN = (["gains0", "gains1"] + [f"x{c}" for c in range(8)] + ["uk0", "uk1"] + [f"m{c}" for c in range(8)]
        + ["mkt0", "mkt1", "ckvt", "krt"]
        + [f"K{b}_{g}" for b in range(8) for g in range(6)] + [f"pt{u}" for u in range(16)]
        + [f"v{n}" for n in range(10)] + [f"ko{c}" for c in range(4)]
        + [f"X{n}" for n in range(16)] + [f"pt{u}" for u in range(16, 24)]
        + [f"hn{n}" for n in range(6)] + ["cwt"] + [f"y{n}" for n in range(6)])
TI = {n: i for i, n in enumerate(TURN)}

RING = [("in_a", "kr"), ("mk", "mk3"), ("mv", "mv1"), ("uq", "qr7"), ("uv", "uv7"), ("gq", "gq3"), ("gk", "gk3"),
        ("gv0", "gv3"), ("gv1", "gv7"), ("gg0", "gg3"), ("gg1", "gg7"), ("zm0", "zm3"), ("zm1", "zm7"), ("zg0", "zg3"), ("zg1", "zg7"),
        ("om0", "om3"), ("om1", "om7"), ("og0", "og3"), ("og1", "og7"), ("wo0", "wo3"), ("wo1", "wo7"), ("mq", "mq3"), ("mo", "mo7")]
RI = {n: i for i, (n, _) in enumerate(RING)}


def build(nc, ins, outs, consts):
    (x_prompt, x_sample, cache_lat, cache_rope, state_gla, mem_k_in, mem_v_in, page_table, mem_prompt, g_attn, w_in, g_q, g_kv,
     w_uq, w_uk, w_uv, w_a2, b_a, g_gla, w_o_mla, w_o_gla, w_out, g_mem, w_mk, w_mv, g_cross, w_mq, w_mo, g_ffn,
     w_router, b_router, w_gate_up, b_gate_up, w_down, b_down, g_final) = ins
    (y_prompt, y_sample, o_lat_p, o_rope_p, o_state_p, o_memk_p, o_memv_p, o_lat_s, o_rope_s, o_state_s) = outs

    ctx = ExitStack()
    with ctx:
        sems = {}

        def S(name):
            if name not in sems:
                sems[name] = ctx.enter_context(nc.semaphore("s_" + name))
            return sems[name]

        def sb(name, n, dt=F32, p=P):
            return ctx.enter_context(nc.sbuf_tensor(name, [p, n], dt))

        B = [ctx.enter_context(nc.psum_tensor(f"bank{i}", [P, 512], F32)) for i in range(8)]
        TURN_BANKS, SCORE_BANK = [B[5], B[6]], B[7]
        SCORE_BANKS = [B[7], B[4]]
        C = sb("consts_sb", N_CONST)
        ring = sb("ring", MOE_SLOTS * SLOT)
        resid = sb("resid", KC * T)
        normed = sb("normed", KC * T)
        gT = sb("gains_t", N_GAINS)
        A = sb("arena", 19840)
        whole = sb("npass", 4, I32)

        def con(name, p=P):
            o, n = CONSTS[name]
            return C[0:p, o:o + n]

        ident, ones = con("ident"), con("ones")

        def slot(n):
            return ring[:, n * SLOT:(n + 1) * SLOT]

        def view(o, n, b=None):
            v = A[:, o:o + n]
            return v if b is None else v.rearrange("p (a b) -> p a b", b=b)

        X = ring[:, 4 * SLOT:6 * SLOT]

        def xview(o, n, b=None):
            v = X[:, o:o + n]
            return v if b is None else v.rearrange("p (a b) -> p a b", b=b)

        h_T = resid[:].rearrange("p (c t) -> p c t", t=T)
        n_T = normed[:].rearrange("p (c t) -> p c t", t=T)
        memk = view(0, 1024, NMEM)
        memv = view(1024, 1024, 512)
        squares = view(2048, 2112)
        big2, big3, big4, big5 = (view(4160 + 2112 * i, 2112, T) for i in range(4))
        o = [12608]

        def small(n, b=None):
            v = view(o[0], n, b)
            o[0] += n
            return v

        cq, ckvT, krT, rotk = small(2 * T, T), small(T), small(T), small(T)
        rstd = small(T, T)
        own_s, mxp, mxT, gm, dg, mbc, rinv, psums = (small(n) for n in (64, 64, 136, 1, 64, 64, 64, 64))
        ckv_tok, kr_tok = small(384, 128), small(192, 64)
        assert o[0] <= 15408
        KTl, KTr = view(15508 - 100, 2048), view(15508 - 100 + 2048, 1024)
        ukT = KTl[:, 0:1024]
        scores = view(18480, 1024)
        pages = view(19504, 24)
        idx = A[:, 19528:19536].bitcast(U32)
        Q2 = view(19536, 128, 64)
        Qs = view(19664, 64)
        exps = view(19728, 4)
        w_r = sb("w_router_sb", 256)
        w_ga = sb("w_ga", 128)
        w_a2_sb = sb("w_a2_sb", 512, p=16)
        ga = A[0:16, 18816:18816 + T]
        b_r = sb("b_router_sb", NE, p=1)

        def lin_bank(name):
            return B[LI[name] % 4]

        def turn_bank(name):
            return TURN_BANKS[TI[name] % 2]

        def turn_sem(name):
            return S("turned_by_dve" if TI[name] % 2 == 0 else "turned_by_act")

        def turned(eng, name):
            eng.wait_ge(turn_sem(name), TI[name] // 2 + 1)

        def lin_done(eng, name):
            eng.wait_ge(S("product_out"), LI[name] + 1)

        def lin_full(eng, name):
            eng.wait_ge(S("product_full"), LI[name] + 1)

        def w_ready(eng, name):
            n = RI[name]
            eng.wait_ge(S(f"slot{n % TRUNK_SLOTS}_loaded"), 16 * (n // TRUNK_SLOTS + 1))

        x_tok = xview(0, 3072, D)
        m_tok = xview(3072, 2048, D)
        memT = xview(5120, 2048, NMEM)
        gain_rows = view(4160 + 512, 128)
        wuk = view(10496, 1024)
        lat = [xview(2048 * i, 2048, 128) for i in range(2)]
        rop = [xview(4096 + 1024 * i, 1024) for i in range(2)]
        att = [xview(6144 + 256 * i, 256) for i in range(2)]
        attT = [xview(6656 + 256 * i, 256, 128) for i in range(2)]
        nmx = xview(7168, 48)

        UNITS = [(h, qb, (qb + 1) * 128) for h in range(H_MLA) for qb in range(2)] + [(h, qb, 256) for h in range(H_MEM) for qb in range(2)]

        gqT, gkT = view(4160, 1056, T), view(4160 + 1056, 1056, T)
        gla, gb = view(8384, 1056, T), view(8384 + 1056, 1056, T)
        gvT = big5
        ge, gtmp = view(12608, 1056, T), view(12608 + 1056, 1056, T)
        states = view(14720, 4096).rearrange("p (h c v) -> p h c v", h=H_GLA, c=NCH)
        vb = view(18816, 1024, 512)
        st_buf = [view(2048 + 1024 * i, 1024, DV) for i in range(2)]
        v_tok = X[0:64, 0:4096].rearrange("p (c v) -> p c v", c=NCH)
        ko_tok = X[0:64, 4096:6144].rearrange("p (c k) -> p c k", c=NCH)
        AT = X[0:64, 6144:7168].rearrange("p (c h t) -> p c h t", c=NCH, h=H_GLA)
        vs_tok = X[0:8, 7168:8192]
        rstd_gla = view(12608, 4 * T, T)
        silu_gg, sig_zm, sig_zg = xview(0, 2112, T), xview(2112, 2112, T), xview(4224, 2112, T)

        qx, xo = view(4160, 1056, T), view(4160 + 1056, 1056, T)
        Kx = view(10496, 8192).rearrange("p (b t n) -> p b t n", b=8, t=2)
        Vx = [view(18688, 1024, 512)]
        kxT = [view(8384 + 512 * i, 512) for i in range(2)]
        xs = view(8384 + 1024, 64)
        xmxp, xmxT, xgm, xdg, xmbc, xps, xrinv = (view(8384 + 1100 + 136 * i, 136) for i in range(7))
        xatt = [view(2048 + 256 * i, 256) for i in range(2)]
        xattT = [view(2560 + 256 * i, 256, 128) for i in range(2)]
        xnmx = view(3072, 48)
        rstd2 = view(3200, T, T)

        acc = view(17000, 2112, T)
        hn_tok = view(4160, 3072, D)
        mo_ = [7232]

        def moe_buf(n, b=None):
            v = view(mo_[0], n, b)
            mo_[0] += n
            return v

        xg = moe_buf(1024, P)
        gate, up, sg = moe_buf(512), moe_buf(512), moe_buf(512)
        hT = moe_buf(512, P)
        y_rows = moe_buf(1024)
        sel = moe_buf(3 * 2 * CAP, 2 * CAP)
        wsel = moe_buf(3 * 2 * CAP, 2 * CAP)
        wselT = moe_buf(T)
        pick_b = moe_buf(2 * CAP, CAP)
        b_gu = moe_buf(2 * DFF)
        posm = moe_buf(3 * 36, 36)
        cw = moe_buf(3 * 36, 36)
        take = moe_buf(3 * 32, 32)
        curp, curw, cureye = moe_buf(12, 4), moe_buf(6, 2), moe_buf(4)
        logits = moe_buf(96)
        top8, e4, tmp32 = moe_buf(24), moe_buf(24), moe_buf(32)
        top_i = moe_buf(24).bitcast(U32)
        top_f = moe_buf(24)
        cwT = moe_buf(T)
        b_dn = moe_buf(1024)
        cnts = moe_buf(40)
        assert mo_[0] <= 17000
        y_tok = view(4160, 3072, D)

        block = ctx.enter_context(nc.Block())

        w_cols = lambda w, a, n: w[0, :, a:a + n].rearrange("(c p) n -> p c n", p=P)

        @block.sync
        def _(sp):
            def into(n, nk, cols):
                return slot(n)[:, 0:nk * cols].rearrange("p (c n) -> p c n", c=nk)

            trunk = {"in_a": (w_cols(w_in, 0, 448), 8, 448), "mk": (w_cols(w_mk, 0, 512), 8, 512), "mv": (w_cols(w_mv, 0, 512), 8, 512),
                     "uq": (w_cols(w_uq, 0, 1536), 2, 1536),
                     "uv": (w_uv[0].rearrange("r h v -> r (h v)")[:, None, :], 1, 1024),
                     "gq": (w_cols(w_in, C_GQ, 512), 8, 512), "gk": (w_cols(w_in, C_GK, 512), 8, 512),
                     "mq": (w_cols(w_mq, 0, 512), 8, 512), "mo": (w_cols(w_mo, 0, 1024), 4, 1024)}
            for half in range(2):
                for name, w, at in (("gv", w_in, C_GV), ("gg", w_in, C_GG), ("zm", w_in, C_ZM), ("zg", w_in, C_ZG),
                                    ("om", w_o_mla, 0), ("og", w_o_gla, 0), ("wo", w_out, 0)):
                    trunk[f"{name}{half}"] = (w_cols(w, at + 512 * half, 512), 8, 512)
            sp.dma_start(C[:], consts).then_inc(S("const_loaded"), 16)
            for tt, (t0, n) in enumerate(TILES):
                src = x_prompt[0, t0:t0 + n, :] if tt < 2 else x_sample[:, 0, :]
                sp.dma_start(x_tok[0:n, tt, :], src).then_inc(S("x_loaded"), 16)
            for n, (name, _) in enumerate(RING):
                if n >= TRUNK_SLOTS:
                    lin_full(sp, RING[n - TRUNK_SLOTS][1])
                src, nk, cols = trunk[name]
                sp.dma_start(into(n % TRUNK_SLOTS, nk, cols), src).then_inc(S(f"slot{n % 4}_loaded"), 16)
                if name == "in_a":
                    sp.dma_start(wuk, w_uk[0].rearrange("r h n -> r (h n)")).then_inc(S("uk_loaded"), 16)
                    sp.dma_start(m_tok, mem_prompt[0].rearrange("(t p) d -> p t d", p=P)).then_inc(S("mem_loaded"), 16)

            def expert_weights(e):
                gu = w_gate_up[0, bass.ds(e, 1)].rearrange("o (c p) n -> p (o c) n", p=P)
                dn = w_down[0, bass.ds(e, 1)].rearrange("o (c p) n -> p (o c) n", p=P)
                return [gu[:, :, 512 * j:512 * j + 512] for j in range(4)] + [dn[:, :, 512 * j:512 * j + 512] for j in range(2)]

            last_reader = {n % TRUNK_SLOTS: reader for n, (_, reader) in enumerate(RING)}
            parts = expert_weights(0)
            for s in (4, 5, 3, 0, 1, 2):
                if s < TRUNK_SLOTS:
                    lin_full(sp, last_reader[s])
                elif s == TRUNK_SLOTS:
                    sp.wait_ge(S("merged"), 8)
                sp.dma_start(into(s, 8, 512), parts[s]).then_inc(S(f"expert_slot{s}"), 16)
            with sp.Fori(1, NE) as e:
                for s, src in enumerate(expert_weights(e)):
                    sp.wait_ge(S(f"slot{s}_used"), e)
                    sp.dma_start(into(s, 8, 512), src).then_inc(S(f"expert_slot{s}"), 16)
            sp.wait_ge(S("npass"), 1)
            npass = sp.value_load(whole[0:1, 0:1], min_val=1, max_val=MAX_PASS)
            with sp.If(npass > 1):
                with sp.Fori(1, npass) as p:
                    with sp.Fori(0, NE) as e:
                        for s, src in enumerate(expert_weights(e)):
                            sp.wait_ge(S(f"slot{s}_used"), p * NE + e)
                            sp.dma_start(into(s, 8, 512), src).then_inc(S(f"expert_slot{s}"), 16)
            turned(sp, "y4")
            turned(sp, "y5")
            for tt, (t0, n) in enumerate(TILES):
                dst = y_prompt[0, t0:t0 + n, :] if tt < 2 else y_sample[:, 0, :]
                sp.dma_start(dst, y_tok[0:n, tt, :]).then_inc(S("y_stored"), 16)
            sp.wait_ge(S("y_stored"), 48)

        @block.gpsimd
        def _(pool):
            pool.dma_start(pages[0:16, 0:8].bitcast(I32), page_table.rearrange("b j -> j b"), allow_slow_non_contiguous=True)\
                .then_inc(S("pages_loaded"), 16)
            for name, src in (("g_attn", g_attn[0]), ("g_mem", g_mem[0]), ("g_cross", g_cross[0]), ("g_ffn", g_ffn[0]), ("g_final", g_final),
                              ("g_q", g_q[0]), ("g_kv", g_kv[0]), ("g_gla", g_gla[0]), ("b_a", b_a[0])):
                r = GAINS[name]
                n = src.shape[0] // P
                pool.dma_start(gain_rows[r:r + n, :], src.rearrange("(c p) -> c p", p=P)).then_inc(S("gains_loaded"), 16)
            pool.dma_start(w_ga.rearrange("p (c n) -> p c n", c=KC), w_cols(w_in, C_GA, 16)).then_inc(S("small_loaded"), 16)
            pool.dma_start(w_a2_sb[:], w_a2[0]).then_inc(S("small_loaded"), 16)
            pool.dma_start(w_r[:].rearrange("p (c n) -> p c n", c=KC), w_router[0].rearrange("(c p) n -> p c n", p=P)).then_inc(S("small_loaded"), 16)
            pool.dma_start(b_r[:], b_router).then_inc(S("small_loaded"), 16)

            lat_rows = cache_lat[0].rearrange("n (g t) r -> (n g) (t r)", g=8)
            rope_rows = cache_rope[0].rearrange("n (g t) r -> (n g) (t r)", g=8)
            pool.wait_ge(S("idx"), 1)
            for b in range(8):
                if b == 0:
                    lin_full(pool, "mv1")
                if b >= 2:
                    pool.wait_ge(S("turn_full"), TI[f"K{b - 2}_5"] + 1)
                off = bass.IndirectOffsetOnAxis(ap=idx[:, b:b + 1], axis=0)
                pool.indirect_dma_start(lat[b % 2].rearrange("p a b -> p (a b)"), None, lat_rows, off).then_inc(S(f"lat{b % 2}"), 16)
                pool.indirect_dma_start(rop[b % 2], None, rope_rows, off).then_inc(S(f"rope{b % 2}"), 16)
            lin_done(pool, "mv1")
            pool.dma_start(o_memv_p[0, 0].rearrange("(t p) h d -> p t (h d)", p=P), memv).then_inc(S("stored"), 16)
            mk_tok = [squares[:, 512 * i:512 * i + 512] for i in range(2)]
            for tt in range(2):
                turned(pool, f"mkt{tt}")
                pool.dma_start(o_memk_p[0, 0, tt * P:(tt + 1) * P].rearrange("p h d -> p (h d)"), mk_tok[tt]).then_inc(S("stored"), 16)
            turned(pool, "ckvt")
            turned(pool, "krt")
            for tt, (t0, n) in enumerate(TILES):
                dl = o_lat_p[0, 0, t0:t0 + n, :] if tt < 2 else o_lat_s[0, :, 0, :]
                dr = o_rope_p[0, 0, t0:t0 + n, :] if tt < 2 else o_rope_s[0, :, 0, :]
                pool.dma_start(dl, ckv_tok[0:n, tt, :]).then_inc(S("stored"), 16)
                pool.dma_start(dr, kr_tok[0:n, tt, :]).then_inc(S("stored"), 16)
            for b in range(8):
                if b < 2:
                    pool.wait_ge(S("turn_full"), TI[f"K{b + 6}_5"] + 1)
                else:
                    pool.wait_ge(S("values_read"), b - 1)
                off = bass.IndirectOffsetOnAxis(ap=idx[:, b:b + 1], axis=0)
                pool.indirect_dma_start(lat[b % 2].rearrange("p a b -> p (a b)"), None, lat_rows, off).then_inc(S(f"lat{b % 2}"), 16)
            pool.wait_ge(S("stored"), 16 * 9)
            for b in range(8):
                if b >= 2:
                    pool.wait_ge(S(f"state_out{b % 2}"), 16 * (b // 2))
                    pool.wait_ge(S("state_read"), b - 1)
                pool.dma_start(st_buf[b % 2], state_gla[0, b].rearrange("h k v -> k h v")).then_inc(S(f"state_in{b % 2}"), 16)
                if b >= 1:
                    pool.wait_ge(S("state_new"), b)
                    pool.dma_start(o_state_s[0, b - 1].rearrange("h k v -> k h v"), st_buf[(b - 1) % 2])\
                        .then_inc(S(f"state_out{(b - 1) % 2}"), 16)
            pool.wait_ge(S("state_new"), 8)
            pool.dma_start(o_state_s[0, 7].rearrange("h k v -> k h v"), st_buf[1]).then_inc(S("state_out1"), 16)
            pool.wait_ge(S("states_done"), 1)
            pool.dma_start(o_state_p[0, 0].rearrange("h k v -> k h v"), states[:, :, NCH - 1, :]).then_inc(S("state_p_out"), 16)
            pool.wait_ge(S("state_p_out"), 16)
            lin_full(pool, "og7")
            for b in range(8):
                pool.dma_start(Kx[:, b], mem_k_in[0, b].rearrange("(t p) h d -> p t (h d)", p=P)).then_inc(S(f"xkeys{b}"), 16)
            for b in range(8):
                if b >= 1:
                    pool.wait_ge(S("xvalues_read"), b)
                pool.dma_start(Vx[0], mem_v_in[0, b].rearrange("(t p) h d -> p t (h d)", p=P)).then_inc(S("xvalues"), 16)
            lin_full(pool, "xpast")
            pool.dma_start(b_dn[0:32, :], b_down[0]).then_inc(S("b_down"), 16)
            pool.wait_ge(S("bias_cleared"), 1)
            pool.dma_start(b_gu[0:32, :], b_gate_up[0]).then_inc(S("b_gate_up"), 16)
            pool.wait_ge(S("stored"), 16 * 9)
            pool.wait_ge(S("state_out0"), 64)
            pool.wait_ge(S("state_out1"), 64)

        @block.tensor
        def _(pe):
            order = [0, 0]

            def open_bank(name):
                assert LIN[order[0]] == name, name
                order[0] += 1
                if LI[name] >= 4:
                    pe.wait_ge(S("product_out"), LI[name] - 3)

            def lin(name, parts, width, m=P):
                open_bank(name)
                for j, (l, r) in enumerate(parts):
                    mm = nc.tensor.matmul(lin_bank(name)[0:m, 0:width], l, r, start=(j == 0), stop=(j == len(parts) - 1))
                mm.then_inc(S("product_full"), 1)

            def turn(name, parts):
                assert TURN[order[1]] == name, name
                order[1] += 1
                i = TI[name]
                if i >= 2:
                    pe.wait_ge(turn_sem(name), i // 2)
                for at, src in parts:
                    k, m = src.shape[0], src.shape[-1]
                    r = src.base_partition()
                    mm = nc.tensor.transpose(turn_bank(name)[0:m, at:at + k], src, ident[r:r + k, r:r + k])
                mm.then_inc(S("turn_full"), 1)

            def norm(k, src, nchunk, width, groups=1):
                pe.wait_ge(S("squares"), k)
                for g in range(groups):
                    for c in range(nchunk):
                        mm = nc.tensor.matmul(B[4 + g][:, 0:width], ones, src[:, (g * nchunk + c) * width:(g * nchunk + c + 1) * width],
                                              start=(c == 0), stop=(c == nchunk - 1))
                mm.then_inc(S("square_sums"), 1)

            def w(name, nk, cols):
                return slot(RI[name] % TRUNK_SLOTS)[:, 0:nk * cols].rearrange("p (c n) -> p c n", c=nk)

            def project(names, ring_name, nk, cols, rhs, width=T, m=P, first=0):
                w_ready(pe, ring_name)
                for j, name in enumerate(names):
                    a = first + m * j
                    lin(name, [(w(ring_name, nk, cols)[:, k, a:a + m], rhs[:, k, 0:width]) for k in range(nk)], width, m)

            pe.wait_ge(S("const_loaded"), 16)
            pe.wait_ge(S("gains_loaded"), 16 * 9)
            turn("gains0", [(0, gain_rows[0:32, :])])
            turn("gains1", [(0, gain_rows[32:N_GAINS, :])])
            pe.wait_ge(S("pages"), 1)
            nc.tensor.matmul(SCORE_BANK[:, 0:8], con("spread", 16), pages[0:16, 8:16], start=True, stop=True).then_inc(S("page_rows"), 1)
            pe.wait_ge(S("x_loaded"), 48)
            for c in range(KC):
                turn(f"x{c}", [(t0, x_tok[0:n, tt, c * P:(c + 1) * P]) for tt, (t0, n) in enumerate(TILES)])
            pe.wait_ge(S("uk_loaded"), 16)
            for g in range(2):
                turn(f"uk{g}", [(128 * j, wuk[:, (4 * g + j) * 128:(4 * g + j + 1) * 128]) for j in range(4)])
            pe.wait_ge(S("mem_loaded"), 16)
            norm(1, squares, KC, T)
            for c in range(KC):
                turn(f"m{c}", [(128 * t, m_tok[:, t, c * P:(c + 1) * P]) for t in range(2)])
            pe.wait_ge(S("normed"), 1)
            project(["cq0", "cq1", "ckv"], "in_a", 8, 448, n_T)
            lin("kr", [(w("in_a", 8, 448)[:, k, C_KR:C_KR + ROPE], n_T[:, k, :]) for k in range(KC)], T, ROPE)
            lin_done(pe, "kr")
            lin("rotk", [(con("rot", 64), krT[0:64, :])], T, ROPE)
            norm(2, squares, KC, NMEM)
            norm(3, squares, 2, T)
            pe.wait_ge(S("normed"), 2)
            project([f"mk{h}" for h in range(4)], "mk", 8, 512, memT, NMEM)
            w_ready(pe, "mv")
            for t in range(2):
                lin(f"mv{t}", [(memT[:, k, t * P:(t + 1) * P], w("mv", 8, 512)[:, k, :]) for k in range(KC)], 512)
            norm(4, squares, 1, T)
            pe.wait_ge(S("normed"), 3)
            w_ready(pe, "uq")
            for h in range(H_MLA):
                lin(f"qn{h}", [(w("uq", 2, 1536)[:, k, 192 * h:192 * h + 128], cq[:, k, :]) for k in range(2)], T)
            for h in range(H_MLA):
                lin(f"qr{h}", [(w("uq", 2, 1536)[:, k, 192 * h + 128:192 * h + 192], cq[:, k, :]) for k in range(2)], T, ROPE)
            lin_done(pe, "mk3")
            for tt in range(2):
                turn(f"mkt{tt}", [(128 * h, memk[:, h, tt * P:(tt + 1) * P]) for h in range(4)])
            pe.wait_ge(S("normed"), 4)
            turn("ckvt", [(128 * tt, ckvT[:, t0:t0 + n]) for tt, (t0, n) in enumerate(TILES)])
            pe.wait_ge(S("k_roped"), 1)
            turn("krt", [(64 * tt, krT[0:64, t0:t0 + n]) for tt, (t0, n) in enumerate(TILES)])
            for h in range(H_MLA):
                lin_done(pe, f"qr{h}")
                lin(f"rot{h}", [(con("rot", 64), big3[0:64, h, :])], T, ROPE)
            turned(pe, "uk0")
            turned(pe, "uk1")
            for h in range(H_MLA):
                lin_done(pe, f"qn{h}")
                lin(f"ql{h}", [(ukT[:, 128 * h:128 * h + 128], big2[:, h, :])], T)
            pe.wait_ge(S("q_sample"), 3)
            lin("own", [(ckvT[:, PROMPT:T], Qs), (krT[0:64, PROMPT:T], Q2[0:64, 0, :])], 64, SAMPLE)
            for b in range(8):
                pe.wait_ge(S(f"lat{b % 2}"), 16 * (b // 2 + 1))
                for g in range(4):
                    turn(f"K{b}_{g}", [(128 * j, lat[b % 2][:, 4 * g + j, :]) for j in range(4)])
                pe.wait_ge(S(f"rope{b % 2}"), 16 * (b // 2 + 1))
                for g in range(2):
                    turn(f"K{b}_{4 + g}", [(128 * j, rop[b % 2][:, (4 * g + j) * 128:(4 * g + j + 1) * 128]) for j in range(4)])
                if b >= 2:
                    pe.wait_ge(S("past_scores_read"), b - 1)
                turned(pe, f"K{b}_4")
                turned(pe, f"K{b}_5")
                for i in range(16):
                    out = SCORE_BANKS[b % 2][:, 8 * i:8 * i + 8]
                    nc.tensor.matmul(out, KTl[:, 128 * i:128 * i + 128], Qs[:, 8 * b:8 * b + 8], start=True, stop=False)
                    mm = nc.tensor.matmul(out, KTr[:, 128 * (i // 2):128 * (i // 2) + 128], Q2[:, i % 2, 8 * b:8 * b + 8],
                                          start=False, stop=True)
                mm.then_inc(S("past_scores"), 1)

            def batch_softmax(a, nbh, part, own):
                pe.wait_ge(S(a + "_part_max"), 1)
                open_bank(a + "max")
                mm = nc.tensor.transpose(lin_bank(a + "max")[0:nbh, 0:P], part, ident)
                if own is not None:
                    mm = nc.tensor.transpose(lin_bank(a + "max")[0:nbh, P:P + 8], own, ident[0:8, 0:8])
                mm.then_inc(S("product_full"), 1)
                pe.wait_ge(S(a + "_max_diag"), 1)
                lin(a + "bc", [(ones[0:nbh, :], (dg if a == "m" else xdg)[0:nbh, 0:nbh])], nbh)

            batch_softmax("m", 64, mxp, own_s[0:8, :])
            pe.wait_ge(S("m_part_sum"), 1)
            lin("msum", [(ones, psums), (ones[0:8, :], own_s[0:8, :])], 64)

            def unit_scores(u):
                h, qb, kw = UNITS[u]
                if u % 16 == 0 and u < 16:
                    pe.wait_ge(S("past_scores_read"), 8)
                    pe.wait_ge(S("q_roped"), 1)
                if u >= 2:
                    pe.wait_ge(S("scores_read"), u - 1)
                out = SCORE_BANKS[u % 2][:, 0:kw]
                q0 = qb * P
                if u < 16:
                    nc.tensor.matmul(out, big4[:, h, q0:q0 + P], ckvT[:, 0:kw], start=True, stop=False)
                    mm = nc.tensor.matmul(out, big3[:, h, q0:q0 + P], krT[:, 0:kw], start=False, stop=True)
                else:
                    mm = nc.tensor.matmul(out, qx[:, h, q0:q0 + P], memk[:, h, 0:kw], start=True, stop=True)
                mm.then_inc(S("scores"), 1)

            def unit_values(u):
                h, qb, kw = UNITS[u]
                pe.wait_ge(S("probs"), u + 1)
                buf, bufT = (att, attT) if u < 16 else (xatt, xattT)
                turn(f"pt{u}", [(128 * j, buf[u % 2][:, 128 * j:128 * j + 128]) for j in range(kw // 128)])
                turned(pe, f"pt{u}")
                if u < 16:
                    parts = [(ckv_tok[:, j, :], bufT[u % 2][:, j, :]) for j in range(kw // 128)]
                else:
                    parts = [(memv[:, j, 128 * h:128 * h + 128], bufT[u % 2][:, j, :]) for j in range(kw // 128)]
                lin(f"att{u}", parts, P)

            turned(pe, "ckvt")
            unit_scores(0)
            for u in range(16):
                if u < 15:
                    unit_scores(u + 1)
                unit_values(u)
            open_bank("past")
            for b in range(8):
                out = lin_bank("past")[:, 8 * b:8 * b + 8]
                nc.tensor.matmul(out, ckv_tok[0:8, 2, :], own_s[0:8, 8 * b:8 * b + 8], start=True, stop=False)
                pe.wait_ge(S(f"lat{b % 2}"), 16 * (5 + b // 2))
                for t in range(16):
                    mm = nc.tensor.matmul(out, lat[b % 2][:, t, :], scores[:, 128 * b + 8 * t:128 * b + 8 * t + 8],
                                          start=False, stop=(t == 15))
                mm.then_inc(S("values_read") if b < 7 else S("product_full"), 1)
            pe.wait_ge(S("olat_sample"), 1)
            w_ready(pe, "uv")
            lin_done(pe, "att15")
            for h in range(H_MLA):
                lin(f"uv{h}", [(w("uv", 1, 1024)[:, 0, 128 * h:128 * h + 128], big2[:, h, :])], T)

            project([f"gq{h}" for h in range(4)], "gq", 8, 512, n_T)
            project([f"gk{h}" for h in range(4)], "gk", 8, 512, n_T)
            for half in range(2):
                project([f"gv{c}" for c in range(4 * half, 4 * half + 4)], f"gv{half}", 8, 512, n_T)
            pe.wait_ge(S("small_loaded"), 64)
            lin("ga", [(w_ga[:, 16 * k:16 * k + 16], n_T[:, k, :]) for k in range(KC)], T, 16)
            lin_done(pe, "ga")
            for h in range(H_GLA):
                lin(f"la{h}", [(w_a2_sb[:, 128 * h:128 * h + 128], ga)], T)
            lin_done(pe, "gv7")
            for c in range(NCH):
                for g in range(2):
                    turn(f"v{2 * c + g}", [(128 * j, gvT[:, 4 * g + j, CH * c:CH * c + CH]) for j in range(4)])
            for g in range(2):
                turn(f"v{8 + g}", [(128 * j, gvT[:, 4 * g + j, PROMPT:T]) for j in range(4)])
            turned(pe, "v8")
            turned(pe, "v9")

            def state_times_q(b):
                pe.wait_ge(S("state_new"), b + 1)
                for hj in range(8):
                    mm = nc.tensor.matmul(SCORE_BANK[:, 8 * hj + b:8 * hj + b + 1],
                                          st_buf[b % 2][:, hj // 2, 128 * (hj % 2):128 * (hj % 2) + 128],
                                          gqT[:, hj // 2, PROMPT + b:PROMPT + b + 1], start=True, stop=True)
                mm.then_inc(S("state_read"), 1)

            for b in range(8):
                for half in range(2):
                    lin(f"vb{2 * b + half}", [(con("pick", 8)[:, 128 * b:128 * b + 128], vs_tok[:, 512 * half:512 * half + 512])], 512)
                if b >= 1:
                    state_times_q(b - 1)
            state_times_q(7)
            pe.wait_ge(S("gla_qk"), 1)
            for c in range(NCH):
                name = f"A{c}"
                open_bank(name)
                for h in range(H_GLA):
                    mm = nc.tensor.matmul(lin_bank(name)[0:CH, CH * h:CH * h + CH], gkT[:, h, CH * c:CH * c + CH],
                                          gqT[:, h, CH * c:CH * c + CH], start=True, stop=True)
                mm.then_inc(S("product_full"), 1)
            pe.wait_ge(S("gla_kout"), 1)
            for c in range(NCH):
                turn(f"ko{c}", [(128 * h, gtmp[:, h, CH * c:CH * c + CH]) for h in range(H_GLA)])
            turned(pe, "v6")
            turned(pe, "v7")
            for h in range(H_GLA):
                for half in range(2):
                    name = f"kv{2 * h + half}"
                    open_bank(name)
                    for c in range(2 * half, 2 * half + 2):
                        turned(pe, f"ko{c}")
                        mm = nc.tensor.matmul(lin_bank(name)[:, DV * (c % 2):DV * (c % 2) + DV], ko_tok[:, c, 128 * h:128 * h + 128],
                                              v_tok[:, c, DV * h:DV * h + DV], start=True, stop=True)
                    mm.then_inc(S("product_full"), 1)
            pe.wait_ge(S("gla_scores"), 1)
            pe.wait_ge(S("states_done"), 1)
            for h in range(H_GLA):
                for j in range(2):
                    name = f"go{2 * h + j}"
                    open_bank(name)
                    for c in range(NCH):
                        out = lin_bank(name)[:, CH * c:CH * c + CH]
                        a = DV * h + 128 * j
                        mm = nc.tensor.matmul(out, v_tok[:, c, a:a + 128], AT[:, c, h, :], start=True, stop=(c == 0))
                        if c:
                            mm = nc.tensor.matmul(out, states[:, h, c - 1, 128 * j:128 * j + 128], gqT[:, h, CH * c:CH * c + CH],
                                                  start=False, stop=True)
                    mm.then_inc(S("product_full"), 1)
            for name in ("gg", "zm", "zg"):
                for half in range(2):
                    project([f"{name}{c}" for c in range(4 * half, 4 * half + 4)], f"{name}{half}", 8, 512, n_T)
            for half in range(2):
                project([f"om{c}" for c in range(4 * half, 4 * half + 4)], f"om{half}", 8, 512, big3)
            turned(pe, "ko2")
            turned(pe, "ko3")
            norm(5, squares, 2, T, groups=4)
            pe.wait_ge(S("gla_gated"), 1)
            for half in range(2):
                project([f"og{c}" for c in range(4 * half, 4 * half + 4)], f"og{half}", 8, 512, big5)
            pe.wait_ge(S("merged"), 8)
            for half in range(2):
                project([f"wo{c}" for c in range(4 * half, 4 * half + 4)], f"wo{half}", 8, 512, big4)
            norm(6, squares, KC, T)
            pe.wait_ge(S("normed"), 6)
            project([f"mq{h}" for h in range(4)], "mq", 8, 512, n_T)
            lin_done(pe, "mq3")
            for n in range(17):
                if n < 16:
                    b, t = n // 2, n % 2
                    pe.wait_ge(S(f"xkeys{b}"), 16)
                    turn(f"X{n}", [(128 * h, Kx[:, b, t, 128 * h:128 * h + 128]) for h in range(4)])
                if n >= 1:
                    m = n - 1
                    turned(pe, f"X{m}")
                    for h in range(4):
                        mm = nc.tensor.matmul(SCORE_BANK[:, 4 * m + h:4 * m + h + 1], kxT[m % 2][:, 128 * h:128 * h + 128],
                                              qx[:, h, PROMPT + m // 2:PROMPT + m // 2 + 1], start=True, stop=True)
                    mm.then_inc(S("x_scores"), 1)
            batch_softmax("x", 32, xmxp[:, 0:32], None)
            pe.wait_ge(S("x_part_sum"), 1)
            lin("xsum", [(ones, xps[:, 0:32])], 32)
            unit_scores(16)
            for u in range(16, 24):
                if u < 23:
                    unit_scores(u + 1)
                unit_values(u)
            open_bank("xpast")
            for b in range(8):
                pe.wait_ge(S("xvalues"), 16 * (b + 1))
                for h in range(4):
                    for t in range(2):
                        mm = nc.tensor.matmul(lin_bank("xpast")[:, 4 * b + h:4 * b + h + 1], Vx[0][:, t, 128 * h:128 * h + 128],
                                              xs[:, 8 * b + 4 * t + h:8 * b + 4 * t + h + 1], start=(t == 0), stop=(t == 1))
                mm.then_inc(S("xvalues_read") if b < 7 else S("product_full"), 1)
            pe.wait_ge(S("xo_sample"), 1)
            lin_done(pe, "att23")
            w_ready(pe, "mo")
            for c in range(KC):
                lin(f"mo{c}", [(w("mo", 4, 1024)[:, k, 128 * c:128 * c + 128], xo[:, k, :]) for k in range(4)], T)
            norm(7, squares, KC, T)
            pe.wait_ge(S("normed"), 7)
            for tt, (t0, n) in enumerate(TILES):
                lin(f"lg{tt}", [(n_T[:, k, t0:t0 + n], w_r[:, 32 * k:32 * k + 32]) for k in range(KC)]
                    + [(ones[0:1, 0:n], b_r[:])], NE, n)
            for i in range(6):
                tt, g = i // 2, i % 2
                t0, n = TILES[tt]
                turn(f"hn{i}", [(128 * j, n_T[:, 4 * g + j, t0:t0 + n]) for j in range(4)])
            pe.wait_ge(S("routed"), 3)
            for tt, (t0, n) in enumerate(TILES):
                lin(f"rk{tt}", [(ones[:, 0:n], take[:, j, :]) for j in range(tt)] + [(con("before")[0:n, 0:n], take[0:n, tt, :])], NE, n)
            lin("cnt", [(ones[0:n, :], take[0:n, tt, :]) for tt, (_, n) in enumerate(TILES)], NE)
            turn("cwt", [(t0, cw[0:n, tt, 0:32]) for tt, (t0, n) in enumerate(TILES)])
            turned(pe, "cwt")
            pe.wait_ge(S("b_down"), 16)
            for c in range(KC):
                lin(f"bd{c}", [(b_dn[0:32, 128 * c:128 * c + 128], cwT[0:32, :])], T)
            lin_done(pe, "bd7")

            def gather():
                for k in range(KC):
                    for tt, (_, n) in enumerate(TILES):
                        mm = nc.tensor.matmul(B[2 + 3 * (k // 4)][:, P * (k % 4):P * (k % 4) + P], hn_tok[0:n, tt, 128 * k:128 * k + 128],
                                              sel[0:n, tt, :], start=(tt == 0), stop=(tt == 2))
                    if k % 4 == 3:
                        mm.then_inc(S("gathered"), 1)

            def slot_w(j):
                return slot(j)[:].rearrange("p (c n) -> p c n", c=KC)

            def both_halves(bank, lhs_of, j, first):
                for k in range(KC):
                    for half in range(2):
                        mm = nc.tensor.matmul(bank[CAP * half:CAP * half + CAP, :], lhs_of(k), slot_w(j + half)[:, k, :],
                                              start=(k == 0 and first), stop=(k == KC - 1))
                        if k == KC - 1:
                            mm.then_inc(S(f"slot{j + half}_used"), 1)

            def scatter(m, first, last):
                pe.wait_ge(S("y_rows"), 4 * m + 4)
                pe.wait_ge(S("weights_copied"), m + 1)
                for c in range(first, last):
                    if c >= 3:
                        pe.wait_ge(S("added"), 8 * m + c - 2)
                    nc.tensor.matmul(B[5 + c % 3][:, 0:T], y_rows[:, 128 * c:128 * c + 128], wselT, start=True, stop=True)\
                        .then_inc(S("scattered"), 1)

            def expert_pair(m, p):
                pe.wait_ge(S("x_pair"), 2 * m + 2 * p + 2)
                pe.wait_ge(S("bias_picked"), m + p + 1)
                for e in range(2):
                    n = 2 * m + e
                    for bank in range(2):
                        if e == 0 and bank == 1:
                            scatter(m, 0, 5)
                        for half in range(2):
                            nc.tensor.matmul(B[bank][CAP * half:CAP * half + CAP, :], pick_b[:, e, :],
                                             b_gu[:, 1024 * bank + 512 * half:1024 * bank + 512 * half + 512], start=True, stop=False)
                        for half in range(2):
                            pe.wait_ge(S(f"expert_slot{2 * bank + half}"), 16 * n + 16)
                        both_halves(B[bank], lambda k: xg[:, k, CAP * e:CAP * e + CAP], 2 * bank, False)
                    if e == 0:
                        scatter(m, 5, KC)
                        pe.wait_ge(S("weighted"), m + 1)
                        for tt, (t0, k) in enumerate(TILES):
                            mm = nc.tensor.transpose(B[2][:, t0:t0 + k], wsel[0:k, tt, :], ident[0:k, 0:k])
                        mm.then_inc(S("weights_turned"), 1)
                    else:
                        pe.wait_ge(S("selected"), m + p + 2)
                        pe.wait_ge(S("weights_copied"), m + 2)
                        pe.wait_ge(S("added"), 8 * m + 8)
                        gather()
                    pe.wait_ge(S("hidden"), n + 1)
                    for j in range(4):
                        mm = nc.tensor.transpose(B[3][:, 128 * j:128 * j + 128], up[:, 128 * j:128 * j + 128], ident)
                    mm.then_inc(S("hidden_turned"), 1)
                    pe.wait_ge(S("hT"), n + 1)
                    pe.wait_ge(S("y_rows"), 2 * n + 4)
                    for half in range(2):
                        pe.wait_ge(S(f"expert_slot{4 + half}"), 16 * n + 16)
                    both_halves(B[4], lambda k: hT[:, k % 4, CAP * (k // 4):CAP * (k // 4) + CAP], 4, True)

            turned(pe, "hn4")
            turned(pe, "hn5")
            pe.wait_ge(S("b_gate_up"), 16)
            pe.wait_ge(S("selected"), 1)
            gather()
            with pe.Fori(0, NE // 2) as q:
                expert_pair(q, 0)
            npass = pe.value_load(whole[0:1, 0:1], min_val=1, max_val=MAX_PASS)
            with pe.If(npass > 1):
                with pe.Fori(1, npass) as p:
                    pe.wait_ge(S("selected"), p * (NE // 2 + 1) + 1)
                    pe.wait_ge(S("x_pair"), 2 * p * (NE // 2 + 1))
                    gather()
                    with pe.Fori(0, NE // 2) as q:
                        expert_pair(p * (NE // 2) + q, p)
            pe.wait_ge(S("added"), npass * (8 * NE // 2))
            scatter(npass * (NE // 2), 0, KC)
            norm(8, squares, KC, T)
            pe.wait_ge(S("normed"), 8)
            for i in range(6):
                tt, g = i // 2, i % 2
                t0, n = TILES[tt]
                turn(f"y{i}", [(128 * j, n_T[:, 4 * g + j, t0:t0 + n]) for j in range(4)])
            assert order == [len(LIN), len(TURN)]

        @block.scalar
        def _(act):
            order = [0]
            steps = [0]

            def link(ins):
                steps[0] += 1
                ins.then_inc(S("act_step"), 1)
                act.wait_ge(S("act_step"), steps[0])

            def out(name, dst, func=ACT.Copy, m=P, width=T, src=None, **kw):
                assert LIN[order[0]] == name, name
                order[0] += 1
                lin_full(act, name)
                nc.scalar.activation(dst, lin_bank(name)[0:m, 0:width] if src is None else src, func, **kw).then_inc(S("product_out"), 1)

            def turn_out(name, parts):
                assert TI[name] % 2 == 1, name
                act.wait_ge(S("turn_full"), TI[name] + 1)
                for dst, m, (a, b) in parts:
                    ins = nc.scalar.copy(dst, turn_bank(name)[0:m, a:b])
                ins.then_inc(S("turned_by_act"), 1)

            def root(k, dst):
                act.wait_ge(S("inverse"), k)
                nc.scalar.activation(dst, dst, ACT.Sqrt).then_inc(S("rstd"), 1)

            turn_out("gains1", [(gT[:, 32:N_GAINS], P, (0, N_GAINS - 32))])
            for c in range(1, KC, 2):
                turn_out(f"x{c}", [(h_T[:, c, :], P, (0, T))])
            act.wait_ge(S("square_sums"), 1)
            turn_out("uk1", [(ukT[:, 512:1024], P, (0, 512))])
            root(1, rstd)
            for c in range(1, KC, 2):
                turn_out(f"m{c}", [(memT[:, c, :], P, (0, NMEM))])
            for c in range(2):
                out(f"cq{c}", cq[:, c, :])
            out("ckv", ckvT)
            act.wait_ge(S("rope_cleared"), 1)
            out("kr", krT[0:64, :], m=ROPE)
            out("rotk", rotk[0:64, :], m=ROPE)
            root(2, rstd[:, :, 0:NMEM])
            root(3, rstd)
            for h in range(4):
                out(f"mk{h}", memk[:, h, :], width=NMEM)
            for t in range(2):
                out(f"mv{t}", memv[:, t, :], width=512)
            root(4, rstd)
            for h in range(H_MLA):
                out(f"qn{h}", big2[:, h, :])
            for h in range(H_MLA):
                out(f"qr{h}", big3[0:64, h, :], m=ROPE)
            turn_out("mkt1", [(squares[:, 512:1024], P, (0, 512))])
            turn_out("krt", [(kr_tok[:, 0:2, :], P, (0, 128)), (kr_tok[0:8, 2, :], 8, (128, 192))])
            for h in range(H_MLA):
                out(f"rot{h}", big5[0:64, h, :], m=ROPE)
            for h in range(H_MLA):
                out(f"ql{h}", big4[:, h, :])
            out("own", own_s[0:8, :], m=8, width=64, scale=ATTN_SCALE)
            for b in range(8):
                if b:
                    act.wait_ge(S("past_scores"), b)
                else:
                    lin_full(act, "ql7")
                for g in (1, 3, 5):
                    dst = KTl[:, 512 * g:512 * g + 512] if g < 4 else KTr[:, 512:1024]
                    turn_out(f"K{b}_{g}", [(dst, P, (0, 512))])

            def batch(a, nbh, own_n, exps_of):
                out(a + "max", (mxT if a == "m" else xmxT)[0:nbh, 0:P + own_n], m=nbh, width=P + own_n)
                out(a + "bc", (mbc if a == "m" else xmbc)[:, 0:nbh], width=nbh)
                act.wait_ge(S(a + "_shifted"), len(exps_of))
                for e in exps_of:
                    nc.scalar.activation(e, e, ACT.Exp).then_inc(S(a + "_exp"), 1)

            batch("m", 64, 8, [scores, own_s[0:8, :]])
            out("msum", mbc, width=64)

            def unit_exp(u):
                buf, nb = (att, nmx) if u < 16 else (xatt, xnmx)
                kw, v = UNITS[u][2], u % 16
                act.wait_ge(S("shifted"), u + 1)
                nc.scalar.activation(buf[u % 2][:, 0:kw], buf[u % 2][:, 0:kw], ACT.Exp, bias=nb[:, v:v + 1],
                                     accum_out=nb[:, 16 + v:17 + v]).then_inc(S("exped"), 1)

            def unit_out(u):
                h, qb, kw = UNITS[u]
                bufT = attT if u < 16 else xattT
                if TI[f"pt{u}"] % 2:
                    turn_out(f"pt{u}", [(bufT[u % 2].rearrange("p a b -> p (a b)")[:, 0:kw], P, (0, kw))])
                out(f"att{u}", (big2 if u < 16 else xo)[:, h, qb * P:qb * P + P], width=P)

            unit_exp(0)
            for u in range(16):
                if u < 15:
                    unit_exp(u + 1)
                unit_out(u)
            out("past", mxp, width=64)
            for h in range(H_MLA):
                out(f"uv{h}", big3[:, h, :])
            for h in range(4):
                out(f"gq{h}", gqT[:, h, :], scale=float(DK ** -0.5))
            for h in range(4):
                out(f"gk{h}", gkT[:, h, :])
            for c in range(KC):
                out(f"gv{c}", gvT[:, c, :])
            out("ga", ga, m=16)
            for h in range(4):
                out(f"la{h}", gla[:, h, :], ACT.Identity, bias=gT[:, GAINS["b_a"] + h:GAINS["b_a"] + h + 1])
            lin_done(act, "la3")
            link(nc.scalar.activation(gb, gla, ACT.Abs))
            link(nc.scalar.activation(gb, gb, ACT.Exp, scale=-1.0))
            nc.scalar.activation(gb, gb, ACT.Ln, bias=1.0).then_inc(S("softplus"), 1)
            for n in range(10):
                if TI[f"v{n}"] % 2:
                    c, g = n // 2, n % 2
                    dst, m = (v_tok[:, c, 512 * g:512 * g + 512], CH) if n < 8 else (vs_tok[:, 512 * g:512 * g + 512], 8)
                    turn_out(f"v{n}", [(dst, m, (0, 512))])
            act.wait_ge(S("cumulated"), 4)
            nc.scalar.activation(ge[:, :, 0:PROMPT], gb[:, :, 0:PROMPT], ACT.Exp, scale=1.0 / 16)
            nc.scalar.activation(ge[:, :, PROMPT:T], gla[:, :, PROMPT:T], ACT.Exp, scale=1.0 / 16).then_inc(S("decays"), 1)
            act.wait_ge(S("to_chunk_end"), 4)
            nc.scalar.activation(gtmp[:, :, 0:PROMPT], gtmp[:, :, 0:PROMPT], ACT.Exp, scale=1.0 / 16)
            nc.scalar.activation(gb[:, :, 0:PROMPT], gb[:, :, 0:PROMPT], ACT.Exp, scale=-1.0 / 16).then_inc(S("k_factors"), 1)
            for b in range(8):
                if b:
                    act.wait_ge(S("state_new"), b)
                for half in range(2):
                    out(f"vb{2 * b + half}", vb[:, half, :], width=512)
            act.wait_ge(S("state_read"), 8)
            nc.scalar.copy(gvT[:, :, PROMPT:T], SCORE_BANK[:, 0:64].rearrange("p (c b) -> p c b", b=8)).then_inc(S("gla_sample"), 1)
            for c in range(NCH):
                out(f"A{c}", AT[:, c].rearrange("p h t -> p (h t)"), m=CH, width=256)
            for c in range(NCH):
                if TI[f"ko{c}"] % 2:
                    turn_out(f"ko{c}", [(ko_tok[:, c, :], CH, (0, 512))])
            for n in range(8):
                h, half = n // 2, n % 2
                out(f"kv{n}", states[:, h, 2 * half:2 * half + 2, :].rearrange("p c v -> p (c v)"), width=512)
            for n in range(8):
                out(f"go{n}", gvT[:, n, 0:PROMPT], width=PROMPT)
            for c in range(KC):
                out(f"gg{c}", silu_gg[:, c, :], ACT.Silu)
            for c in range(KC):
                out(f"zm{c}", sig_zm[:, c, :], ACT.Sigmoid)
            for c in range(KC):
                out(f"zg{c}", sig_zg[:, c, :], ACT.Sigmoid)
            for c in range(KC):
                out(f"om{c}", big4[:, c, :])
            root(5, rstd_gla)
            for c in range(KC):
                out(f"og{c}", big2[:, c, :])
            for c in range(KC):
                out(f"wo{c}", big2[:, c, :])
            root(6, rstd2)
            for h in range(4):
                out(f"mq{h}", qx[:, h, :])
            for n in range(16):
                if TI[f"X{n}"] % 2:
                    if n >= 2:
                        act.wait_ge(S("x_scores"), n - 1)
                    turn_out(f"X{n}", [(kxT[n % 2], P, (0, 512))])
            batch("x", 32, 0, [xs])
            out("xsum", xmbc[:, 0:32], width=32)
            unit_exp(16)
            for u in range(16, 24):
                if u < 23:
                    unit_exp(u + 1)
                unit_out(u)
            out("xpast", xps[:, 0:32], width=32)
            for c in range(KC):
                out(f"mo{c}", big4[:, c, :])
            root(7, rstd2)
            for tt, (_, n) in enumerate(TILES):
                out(f"lg{tt}", logits[0:n, 32 * tt:32 * tt + 32], m=n, width=NE)
            for i in range(6):
                if TI[f"hn{i}"] % 2:
                    tt, g = i // 2, i % 2
                    n = TILES[tt][1]
                    turn_out(f"hn{i}", [(hn_tok[0:n, tt, 512 * g:512 * g + 512], n, (0, 512))])
            for tt, (_, n) in enumerate(TILES):
                act.wait_ge(S("top_shifted"), tt + 1)
                nc.scalar.activation(e4[0:n, 8 * tt:8 * tt + 4], e4[0:n, 8 * tt:8 * tt + 4], ACT.Exp,
                                     accum_out=e4[0:n, 8 * tt + 4:8 * tt + 5]).then_inc(S("top_exp"), 1)
            for tt, (_, n) in enumerate(TILES):
                out(f"rk{tt}", posm[0:n, tt, 0:NE], m=n, width=NE)
            out("cnt", cnts[:, 0:NE], width=NE)
            if TI["cwt"] % 2:
                turn_out("cwt", [(cwT[0:NE, :], NE, (0, T))])
            for c in range(KC):
                out(f"bd{c}", acc[:, c, :])

            def gathered(g):
                for half in range(2):
                    act.wait_ge(S("gathered"), 2 * g + half + 1)
                    nc.scalar.copy(xg[:, 4 * half:4 * half + 4, :].rearrange("p a b -> p (a b)"), B[2 + 3 * half][:]).then_inc(S("x_pair"), 1)

            def expert_pair(m, p):
                for e in range(2):
                    n = 2 * m + e
                    act.wait_ge(S("gate"), n + 1)
                    nc.scalar.activation(sg, gate, ACT.Sigmoid, scale=1.702).then_inc(S("sigmoid"), 1)
                    if e == 0:
                        act.wait_ge(S("weights_turned"), m + 1)
                        nc.scalar.copy(wselT, B[2][:, 0:T]).then_inc(S("weights_copied"), 1)
                    else:
                        act.wait_ge(S("slot3_used"), n + 1)
                        gathered(m + p + 1)
                    act.wait_ge(S("hidden_turned"), n + 1)
                    nc.scalar.copy(hT.rearrange("p a b -> p (a b)"), B[3][:]).then_inc(S("hT"), 1)
                    act.wait_ge(S("slot5_used"), n + 1)
                    for half in range(2):
                        nc.scalar.copy(y_rows[CAP * e:CAP * e + CAP, 512 * half:512 * half + 512], B[4][CAP * half:CAP * half + CAP, :])\
                            .then_inc(S("y_rows"), 1)

            gathered(0)
            with act.Fori(0, NE // 2) as q:
                expert_pair(q, 0)
            act.wait_ge(S("npass"), 1)
            npass = act.value_load(whole[0:1, 0:1], min_val=1, max_val=MAX_PASS)
            with act.If(npass > 1):
                with act.Fori(1, npass) as p:
                    gathered(p * (NE // 2 + 1))
                    with act.Fori(0, NE // 2) as q:
                        expert_pair(p * (NE // 2) + q, p)
            root(8, rstd2)
            for i in range(6):
                if TI[f"y{i}"] % 2:
                    tt, g = i // 2, i % 2
                    n = TILES[tt][1]
                    turn_out(f"y{i}", [(y_tok[0:n, tt, 512 * g:512 * g + 512], n, (0, 512))])
            assert order[0] == len(LIN)

        @block.vector
        def _(dve):
            V = nc.vector
            steps = [0]

            def link(ins):
                steps[0] += 1
                ins.then_inc(S("dve_step"), 1)
                dve.wait_ge(S("dve_step"), steps[0])

            def turn_out(name, parts):
                assert TI[name] % 2 == 0, name
                dve.wait_ge(S("turn_full"), TI[name] + 1)
                for dst, m, (a, b) in parts:
                    ins = V.tensor_copy(dst, turn_bank(name)[0:m, a:b])
                ins.then_inc(S("turned_by_dve"), 1)

            def square(src, dst):
                V.tensor_tensor(dst, src, src, ALU.mult).then_inc(S("squares"), 1)

            def scale_by_rms(k, src, dst, gain, nchunk, width, dim, rs, groups=1):
                dve.wait_ge(S("square_sums"), k)
                for g in range(groups):
                    ins = V.tensor_scalar(rs[:, g, 0:width], B[4 + g][:, 0:width], 1.0 / dim, EPS, ALU.mult, ALU.add)
                link(ins)
                V.reciprocal(rs[:, :, 0:width], rs[:, :, 0:width]).then_inc(S("inverse"), 1)
                dve.wait_ge(S("rstd"), k)
                for c in range(nchunk * groups):
                    r = GAINS[gain] + c % nchunk
                    ins = V.scalar_tensor_tensor(out=dst[:, c, :], in0=src[:, c, :], scalar=gT[:, r:r + 1], in1=rs[:, c // nchunk, 0:width],
                                                 op0=ALU.mult, op1=ALU.mult)
                ins.then_inc(S("normed"), 1)

            def flat(v):
                return v.rearrange("p a b -> p (a b)")

            def bc(v, shape):
                return v.to_broadcast(shape)

            V.memset(krT[64:128, :], 0.0)
            V.memset(big3[64:128, :, :], 0.0).then_inc(S("rope_cleared"), 1)
            dve.wait_ge(S("pages_loaded"), 16)
            V.tensor_copy(pages[0:16, 8:16], pages[0:16, 0:8].bitcast(I32)).then_inc(S("pages"), 1)
            turn_out("gains0", [(gT[:, 0:32], P, (0, 32))])
            dve.wait_ge(S("page_rows"), 1)
            V.tensor_scalar(idx, SCORE_BANK[:, 0:8], con("within"), None, ALU.add).then_inc(S("idx"), 1)
            for c in range(0, KC, 2):
                turn_out(f"x{c}", [(h_T[:, c, :], P, (0, T))])
            dve.wait_ge(turn_sem("x7"), TI["x7"] // 2 + 1)
            dve.wait_ge(turn_sem("x6"), TI["x6"] // 2 + 1)
            square(resid[:], squares)
            turn_out("uk0", [(ukT[:, 0:512], P, (0, 512))])
            scale_by_rms(1, h_T, n_T, "g_attn", KC, T, D, rstd)
            for c in range(0, KC, 2):
                turn_out(f"m{c}", [(memT[:, c, :], P, (0, NMEM))])
            turned(dve, "m7")
            turned(dve, "m6")
            square(flat(memT), squares[:, 0:KC * NMEM])
            scale_by_rms(2, memT, memT, "g_mem", KC, NMEM, D, rstd)
            lin_done(dve, "cq1")
            square(flat(cq), squares[:, 0:2 * T])
            scale_by_rms(3, cq, cq, "g_q", 2, T, 256, rstd)
            lin_done(dve, "rotk")
            V.tensor_tensor(krT[0:64, :], krT[0:64, :], con("cos", 64), ALU.mult)
            link(V.tensor_tensor(rotk[0:64, :], rotk[0:64, :], con("sin", 64), ALU.mult))
            V.tensor_tensor(krT[0:64, :], krT[0:64, :], rotk[0:64, :], ALU.add).then_inc(S("k_roped"), 1)
            square(ckvT, squares[:, 0:T])
            scale_by_rms(4, ckvT[:, None, :], ckvT[:, None, :], "g_kv", 1, T, LORA, rstd)
            turn_out("mkt0", [(squares[:, 0:512], P, (0, 512))])
            turn_out("ckvt", [(flat(ckv_tok)[:, 0:256], P, (0, 256)), (ckv_tok[0:8, 2, :], 8, (256, 384))])
            lin_done(dve, "rot7")
            V.tensor_tensor(big3[0:64], big3[0:64], bc(con("cos", 64)[:, None, :], [64, 8, T]), ALU.mult)
            link(V.tensor_tensor(big5[0:64], big5[0:64], bc(con("sin", 64)[:, None, :], [64, 8, T]), ALU.mult))
            V.tensor_tensor(big3[0:64], big3[0:64], big5[0:64], ALU.add).then_inc(S("q_roped"), 1)
            link(V.memset(Q2, 0.0))
            dve.wait_ge(S("q_roped"), 1)
            for i in range(2):
                V.tensor_copy(Q2[64 * i:64 * i + 64, i, :].rearrange("p (b h) -> p h b", b=8), big3[0:64, :, PROMPT:T]).then_inc(S("q_sample"), 1)
            lin_done(dve, "ql7")
            V.tensor_copy(Qs.rearrange("p (b h) -> p h b", b=8), big4[:, :, PROMPT:T]).then_inc(S("q_sample"), 1)
            for b in range(8):
                if b:
                    dve.wait_ge(S("past_scores"), b)
                for g in (0, 2, 4):
                    dst = KTl[:, 512 * g:512 * g + 512] if g < 4 else KTr[:, 0:512]
                    turn_out(f"K{b}_{g}", [(dst, P, (0, 512))])
                dve.wait_ge(S("past_scores"), b + 1)
                V.tensor_scalar(scores[:, 128 * b:128 * b + 128], SCORE_BANKS[b % 2][:, 0:128], ATTN_SCALE, None,
                                ALU.mult).then_inc(S("past_scores_read"), 1)
            lin_done(dve, "own")
            link(V.tensor_tensor(own_s[0:8, :], own_s[0:8, :], con("own", 8), ALU.add))

            def batch(a, nbh, sc, nb, ntile, bufs, own):
                part, mT, g1, diag, mb, ps, inv = bufs
                by_bh = sc.rearrange("p (b i h) -> p b h i", b=nb, i=ntile)
                V.tensor_reduce(part[:, 0:nbh].rearrange("p (b h) -> p b h", b=nb), by_bh, AX, ALU.max).then_inc(S(a + "_part_max"), 1)
                lin_done(dve, a + "max")
                link(V.tensor_reduce(g1[0:nbh, 0:1], mT[0:nbh, 0:P + (8 if own is not None else 0)], AX, ALU.max))
                V.tensor_scalar(diag[0:nbh, 0:nbh], ident[0:nbh, 0:nbh], g1[0:nbh, 0:1], None, ALU.mult).then_inc(S(a + "_max_diag"), 1)
                lin_done(dve, a + "bc")
                V.tensor_tensor(by_bh, by_bh, bc(mb[:, 0:nbh].rearrange("p (b h o) -> p b h o", b=nb, o=1), [P, nb, nbh // nb, ntile]),
                                ALU.subtract).then_inc(S(a + "_shifted"), 1)
                n = 1
                if own is not None:
                    n = 2
                    V.tensor_tensor(own, own, mb[0:8, 0:nbh], ALU.subtract).then_inc(S(a + "_shifted"), 1)
                dve.wait_ge(S(a + "_exp"), n)
                V.tensor_reduce(ps[:, 0:nbh].rearrange("p (b h) -> p b h", b=nb), by_bh, AX, ALU.add).then_inc(S(a + "_part_sum"), 1)
                lin_done(dve, a + "sum")
                link(V.reciprocal(inv[:, 0:nbh], mb[:, 0:nbh]))

            dve.wait_ge(S("past_scores_read"), 8)
            batch("m", 64, scores, 8, 16, (mxp, mxT, gm, dg, mbc, psums, rinv), own_s[0:8, :])

            def unit_scores(u):
                buf, nb = (att, nmx) if u < 16 else (xatt, xnmx)
                h, qb, kw = UNITS[u]
                v = u % 16
                dve.wait_ge(S("scores"), u + 1)
                if u >= 2 and u != 16 and u != 17:
                    dve.wait_ge(S("turn_full"), TI[f"pt{u - 2}"] + 1)
                s, ps = buf[u % 2][:, 0:kw], SCORE_BANKS[u % 2][:, 0:kw]
                if u < 16:
                    V.scalar_tensor_tensor(out=s, in0=ps, scalar=ATTN_SCALE, in1=con("causal")[:, 256 - kw:256], op0=ALU.mult, op1=ALU.add)\
                        .then_inc(S("scores_read"), 1)
                else:
                    V.tensor_scalar(s, ps, MEM_SCALE, None, ALU.mult).then_inc(S("scores_read"), 1)
                dve.wait_ge(S("scores_read"), u + 1)
                V.tensor_reduce(nb[:, v:v + 1], s, AX, ALU.max, negate=True).then_inc(S("shifted"), 1)

            def unit_probs(u):
                buf, nb, bufT = (att, nmx, attT) if u < 16 else (xatt, xnmx, xattT)
                kw, v = UNITS[u][2], u % 16
                dve.wait_ge(S("exped"), u + 1)
                link(V.reciprocal(nb[:, 32 + v:33 + v], nb[:, 16 + v:17 + v]))
                s = buf[u % 2][:, 0:kw]
                V.tensor_scalar(s, s, nb[:, 32 + v:33 + v], None, ALU.mult).then_inc(S("probs"), 1)
                if TI[f"pt{u}"] % 2 == 0:
                    turn_out(f"pt{u}", [(flat(bufT[u % 2])[:, 0:kw], P, (0, kw))])

            unit_scores(0)
            for u in range(16):
                if u < 15:
                    unit_scores(u + 1)
                unit_probs(u)
            lin_done(dve, "past")
            V.tensor_tensor(big2[:, :, PROMPT:T], mxp.rearrange("p (b h) -> p h b", b=8), rinv.rearrange("p (b h) -> p h b", b=8),
                            ALU.mult).then_inc(S("olat_sample"), 1)
            for n in range(10):
                if TI[f"v{n}"] % 2 == 0:
                    c, g = n // 2, n % 2
                    dst, m = (v_tok[:, c, 512 * g:512 * g + 512], CH) if n < 8 else (vs_tok[:, 512 * g:512 * g + 512], 8)
                    turn_out(f"v{n}", [(dst, m, (0, 512))])
            dve.wait_ge(S("softplus"), 1)
            link(V.scalar_tensor_tensor(out=gla, in0=gla, scalar=0.0, in1=gb, op0=ALU.min, op1=ALU.subtract))
            for h in range(4):
                V.tensor_tensor_scan(gb[:, h, 0:PROMPT], con("carry"), gla[:, h, 0:PROMPT], 0.0, ALU.mult, ALU.add).then_inc(S("cumulated"), 1)
            dve.wait_ge(S("cumulated"), 4)
            for h in range(4):
                bh = gb[:, h, 0:PROMPT].rearrange("p (c t) -> p c t", c=NCH)
                V.tensor_tensor(gtmp[:, h, 0:PROMPT].rearrange("p (c t) -> p c t", c=NCH), bc(bh[:, :, CH - 1:CH], [P, NCH, CH]), bh,
                                ALU.subtract).then_inc(S("to_chunk_end"), 1)
            dve.wait_ge(S("k_factors"), 1)
            pr = slice(0, PROMPT)
            V.tensor_tensor(gtmp[:, :, pr], gtmp[:, :, pr], gkT[:, :, pr], ALU.mult).then_inc(S("gla_kout"), 1)
            V.tensor_tensor(gkT[:, :, pr], gkT[:, :, pr], gb[:, :, pr], ALU.mult)
            V.tensor_tensor(gqT[:, :, pr], gqT[:, :, pr], ge[:, :, pr], ALU.mult).then_inc(S("gla_qk"), 1)
            for b in range(8):
                st = st_buf[b % 2]
                t = PROMPT + b
                dve.wait_ge(S(f"state_in{b % 2}"), 16 * (b // 2 + 1))
                for h in range(4):
                    ins = V.tensor_scalar(st[:, h, :], st[:, h, :], ge[:, h, t:t + 1], None, ALU.mult)
                link(ins)
                lin_done(dve, f"vb{2 * b + 1}")
                for h in range(4):
                    ins = V.scalar_tensor_tensor(out=st[:, h, :], in0=vb[:, h // 2, DV * (h % 2):DV * (h % 2) + DV], scalar=gkT[:, h, t:t + 1],
                                                 in1=st[:, h, :], op0=ALU.mult, op1=ALU.add)
                ins.then_inc(S("state_new"), 1)
            lin_done(dve, "A3")
            AT3 = AT.rearrange("p c h t -> p (c h) t")
            link(V.tensor_scalar(AT3, AT3, 3.0e38, -3.0e38, ALU.min, ALU.max))
            V.tensor_tensor(AT3, AT3, bc(con("upto", CH)[:, None, :], [CH, 16, CH]), ALU.mult).then_inc(S("gla_scores"), 1)
            for c in range(NCH):
                if TI[f"ko{c}"] % 2 == 0:
                    turn_out(f"ko{c}", [(ko_tok[:, c, :], CH, (0, 512))])
            lin_done(dve, "kv7")
            for c in range(1, NCH):
                for h in range(4):
                    ins = V.scalar_tensor_tensor(out=states[:, h, c, :], in0=states[:, h, c - 1, :], scalar=ge[:, h, CH * c + CH - 1:CH * c + CH],
                                                 in1=states[:, h, c, :], op0=ALU.mult, op1=ALU.add)
                if c < NCH - 1:
                    link(ins)
            ins.then_inc(S("states_done"), 1)
            lin_done(dve, "go7")
            dve.wait_ge(S("gla_sample"), 1)
            dve.wait_ge(S("state_out0"), 64)
            dve.wait_ge(S("state_out1"), 64)
            square(flat(gvT), squares)
            scale_by_rms(5, gvT, gvT, "g_gla", 2, T, DV, rstd_gla, groups=4)
            dve.wait_ge(S("normed"), 5)
            lin_done(dve, "gg7")
            V.tensor_tensor(gvT, gvT, silu_gg, ALU.mult).then_inc(S("gla_gated"), 1)
            lin_done(dve, "om7")
            link(V.tensor_tensor(big4, big4, sig_zm, ALU.mult))
            for c in range(KC):
                lin_done(dve, f"og{c}")
                link(V.tensor_tensor(big2[:, c, :], big2[:, c, :], sig_zg[:, c, :], ALU.mult))
                V.tensor_tensor(big4[:, c, :], big4[:, c, :], big2[:, c, :], ALU.add).then_inc(S("merged"), 1)

            def add_to_residual(name, src):
                for c in range(KC):
                    lin_done(dve, f"{name}{c}")
                    ins = V.tensor_tensor(h_T[:, c, :], h_T[:, c, :], src[:, c, :], ALU.add)
                link(ins)

            add_to_residual("wo", big2)
            square(resid[:], squares)
            scale_by_rms(6, h_T, n_T, "g_cross", KC, T, D, rstd2)
            for n in range(16):
                if TI[f"X{n}"] % 2 == 0:
                    if n >= 2:
                        dve.wait_ge(S("x_scores"), n - 1)
                    turn_out(f"X{n}", [(kxT[n % 2], P, (0, 512))])
            dve.wait_ge(S("x_scores"), 16)
            link(V.tensor_scalar(xs, SCORE_BANK[:, 0:64], MEM_SCALE, None, ALU.mult))
            batch("x", 32, xs, 8, 2, (xmxp, xmxT, xgm, xdg, xmbc, xps, xrinv), None)
            unit_scores(16)
            for u in range(16, 24):
                if u < 23:
                    unit_scores(u + 1)
                unit_probs(u)
            lin_done(dve, "xpast")
            V.tensor_tensor(xo[:, :, PROMPT:T], xps[:, 0:32].rearrange("p (b h) -> p h b", b=8), xrinv[:, 0:32].rearrange("p (b h) -> p h b", b=8),
                            ALU.mult).then_inc(S("xo_sample"), 1)
            add_to_residual("mo", big4)
            square(resid[:], squares)
            scale_by_rms(7, h_T, n_T, "g_ffn", KC, T, D, rstd2)
            V.memset(posm, FAR)
            V.memset(cw, 0.0)
            V.memset(b_gu, 0.0).then_inc(S("bias_cleared"), 1)
            link(V.memset(take, 0.0))
            for i in range(6):
                if TI[f"hn{i}"] % 2 == 0:
                    tt, g = i // 2, i % 2
                    n = TILES[tt][1]
                    turn_out(f"hn{i}", [(hn_tok[0:n, tt, 512 * g:512 * g + 512], n, (0, 512))])
            for tt, (_, n) in enumerate(TILES):
                lin_done(dve, f"lg{tt}")
                lg, t8 = logits[0:n, 32 * tt:32 * tt + 32], top8[0:n, 8 * tt:8 * tt + 8]
                ti, tf = top_i[0:n, 8 * tt:8 * tt + 8], top_f[0:n, 8 * tt:8 * tt + 8]
                link(V.max(t8, lg))
                link(V.max_index(ti, t8, lg))
                V.tensor_copy(tf, ti)
                V.tensor_scalar(e4[0:n, 8 * tt:8 * tt + 4], t8[:, 0:4], t8[:, 0:1], None, ALU.subtract).then_inc(S("top_shifted"), 1)
            for tt, (_, n) in enumerate(TILES):
                tf, e = top_f[0:n, 8 * tt:8 * tt + 8], e4[0:n, 8 * tt:8 * tt + 8]
                dve.wait_ge(S("top_exp"), tt + 1)
                link(V.reciprocal(e[:, 5:6], e[:, 4:5]))
                link(V.tensor_scalar(e[:, 0:4], e[:, 0:4], e[:, 5:6], None, ALU.mult))
                c32 = con("count", n)[:, 0:NE]
                link(V.tensor_scalar(cw[0:n, tt, 0:NE], c32, tf[:, 0:1], e[:, 0:1], ALU.is_equal, ALU.mult))
                for k in range(1, TOPK):
                    link(V.tensor_scalar(tmp32[0:n, :], c32, tf[:, k:k + 1], e[:, k:k + 1], ALU.is_equal, ALU.mult))
                    link(V.tensor_tensor(cw[0:n, tt, 0:NE], cw[0:n, tt, 0:NE], tmp32[0:n, :], ALU.add))
                V.tensor_scalar(take[0:n, tt, :], cw[0:n, tt, 0:NE], 0.0, None, ALU.is_gt).then_inc(S("routed"), 1)
            if TI["cwt"] % 2 == 0:
                turn_out("cwt", [(cwT[0:NE, :], NE, (0, T))])
            lin_done(dve, "rk2")
            for tt, (_, n) in enumerate(TILES):
                ins = V.tensor_scalar(logits[0:n, 32 * tt:32 * tt + 32], take[0:n, tt, :], -FAR, FAR, ALU.mult, ALU.add)
            link(ins)
            for tt, (_, n) in enumerate(TILES):
                ins = V.tensor_tensor(posm[0:n, tt, 0:NE], posm[0:n, tt, 0:NE], logits[0:n, 32 * tt:32 * tt + 32], ALU.add)
            link(ins)

            def one_hots(dst, ranks, weights, done):
                for e in range(2):
                    for tt, (_, n) in enumerate(TILES):
                        ins = V.tensor_scalar(dst[0:n, tt, CAP * e:CAP * e + CAP], con("count", n), ranks[0:n, tt, e:e + 1],
                                              None if weights is None else weights[0:n, tt, e:e + 1], ALU.is_equal,
                                              ALU.bypass if weights is None else ALU.mult)
                ins.then_inc(S(done), 1)

            def pick_bias(eye):
                V.tensor_copy(pick_b, bc(eye.rearrange("p (e o) -> p e o", o=1), [P, 2, CAP])).then_inc(S("bias_picked"), 1)

            def start_pass():
                one_hots(sel, posm[:, :, 0:2], None, "selected")
                pick_bias(ident[:, 0:2])

            start_pass()
            V.memset(y_rows, 0.0).then_inc(S("y_rows"), 4)
            V.memset(wselT, 0.0).then_inc(S("weights_copied"), 1)
            lin_done(dve, "cnt")
            link(V.tensor_reduce(cnts[0:1, 32:33], cnts[0:1, 0:NE], AX, ALU.max))
            link(V.tensor_scalar(cnts[0:1, 33:34], cnts[0:1, 32:33], float(CAP), 1.0, ALU.is_gt, ALU.add))
            for j in range(2, MAX_PASS):
                link(V.scalar_tensor_tensor(out=cnts[0:1, 32 + j:33 + j], in0=cnts[0:1, 32:33], scalar=float(CAP * j), in1=cnts[0:1, 31 + j:32 + j],
                                            op0=ALU.is_gt, op1=ALU.add))
            V.tensor_copy(whole[0:1, 0:1], cnts[0:1, 31 + MAX_PASS:32 + MAX_PASS]).then_inc(S("npass"), 1)
            lin_done(dve, "bd7")

            def add_scattered(m, first, last):
                for c in range(first, last):
                    dve.wait_ge(S("scattered"), 8 * m + c + 1)
                    V.tensor_tensor(acc[:, c, :], acc[:, c, :], B[5 + c % 3][:, 0:T], ALU.add).then_inc(S("added"), 1)

            def expert_pair(q, m, p):
                dve.wait_ge(S("bias_picked"), m + p + 1)
                V.tensor_copy(curp, posm[:, :, bass.ds(2 * q, 4)])
                V.tensor_copy(curw, cw[:, :, bass.ds(2 * q, 2)])
                V.tensor_copy(cureye, ident[:, bass.ds(2 * q, 4)]).then_inc(S("pair_columns"), 1)
                dve.wait_ge(S("pair_columns"), m + 1)
                one_hots(wsel, curp, curw, "weighted")
                dve.wait_ge(S("gathered"), 2 * m + 2 * p + 2)
                one_hots(sel, curp[:, :, 2:4], None, "selected")
                for e in range(2):
                    n = 2 * m + e
                    dve.wait_ge(S("slot1_used"), n + 1)
                    V.tensor_scalar(gate, B[0][:], 7.0, None, ALU.min).then_inc(S("gate"), 1)
                    if e == 0:
                        add_scattered(m, 0, 5)
                    dve.wait_ge(S("slot3_used"), n + 1)
                    V.tensor_scalar(up, B[1][:], 7.0, -7.0, ALU.min, ALU.max).then_inc(S("up_clipped"), 1)
                    dve.wait_ge(S("up_clipped"), n + 1)
                    V.scalar_tensor_tensor(out=up, in0=up, scalar=1.0, in1=gate, op0=ALU.add, op1=ALU.mult).then_inc(S("gated_up"), 1)
                    dve.wait_ge(S("gated_up"), n + 1)
                    dve.wait_ge(S("sigmoid"), n + 1)
                    V.tensor_tensor(up, up, sg, ALU.mult).then_inc(S("hidden"), 1)
                    if e == 0:
                        add_scattered(m, 5, KC)
                pick_bias(cureye[:, 2:4])

            with dve.Fori(0, NE // 2) as q:
                expert_pair(q, q, 0)
            dve.wait_ge(S("npass"), 1)
            npass = dve.value_load(whole[0:1, 0:1], min_val=1, max_val=MAX_PASS)
            with dve.If(npass > 1):
                with dve.Fori(1, npass) as p:
                    V.tensor_scalar(posm, posm, float(-CAP), None, ALU.add).then_inc(S("next_ranks"), 1)
                    dve.wait_ge(S("next_ranks"), p)
                    dve.wait_ge(S("gathered"), 2 * p * (NE // 2 + 1))
                    start_pass()
                    with dve.Fori(0, NE // 2) as q:
                        expert_pair(q, p * (NE // 2) + q, p)
            add_scattered(npass * (NE // 2), 0, KC)
            dve.wait_ge(S("added"), (npass * (NE // 2) + 1) * 8)
            link(V.tensor_tensor(resid[:], resid[:], flat(acc), ALU.add))
            square(resid[:], squares)
            scale_by_rms(8, h_T, n_T, "g_final", KC, T, D, rstd2)
            for i in range(6):
                if TI[f"y{i}"] % 2 == 0:
                    tt, g = i // 2, i % 2
                    n = TILES[tt][1]
                    turn_out(f"y{i}", [(y_tok[0:n, tt, 512 * g:512 * g + 512], n, (0, 512))])


_INS = ["x_prompt", "x_sample", "cache_kv_latent", "cache_k_rope", "state_gla", "cache_mem_k", "cache_mem_v", "page_table", "mem_prompt",
        "g_attn", "w_in", "g_q", "g_kv", "w_uq", "w_uk", "w_uv", "w_a2", "b_a", "g_gla", "w_o_mla", "w_o_gla", "w_out", "g_mem", "w_mk",
        "w_mv", "g_cross", "w_mq", "w_mo", "g_ffn", "w_router", "b_router", "w_gate_up", "b_gate_up", "w_down", "b_down", "g_final"]
_OUTS = [(1, 256, 1024), (8, 1, 1024), (1, 1, 256, 128), (1, 1, 256, 64), (1, 1, 4, 128, 256), (1, 1, 256, 4, 128), (1, 1, 256, 4, 128),
         (1, 8, 1, 128), (1, 8, 1, 64), (1, 8, 4, 128, 256)]


def kernel(**inputs):
    import concourse.bacc as _bacc
    from concourse.bass_utils import run_bass_kernel_spmd as _run

    nc = _bacc.Bacc("TRN2", target_bir_lowering=False, num_devices=1)
    arrays, ins = {}, []
    for name in _INS:
        a = np.ascontiguousarray(inputs[name])
        arrays[f"in_{name}"] = a
        ins.append(nc.dram_tensor(f"in_{name}", a.shape, mybir.dt.from_np(a.dtype), kind="ExternalInput").ap())
    table = constants()
    arrays["in_constants"] = table
    consts = nc.dram_tensor("in_constants", table.shape, F32, kind="ExternalInput").ap()
    outs = [nc.dram_tensor(f"out_{i}", shape, F32, kind="ExternalOutput").ap() for i, shape in enumerate(_OUTS)]
    build(nc, ins, outs, consts)
    r = _run(nc, [arrays], core_ids=[0])
    return tuple(r.results[0][f"out_{i}"] for i in range(len(_OUTS)))
```

```python
from contextlib import ExitStack

import numpy as np

import concourse.bass as bass
from concourse import mybir

ALU = mybir.AluOpType
ACT = mybir.ActivationFunctionType
F32 = mybir.dt.float32
I32 = mybir.dt.int32
U32 = mybir.dt.uint32
AX = mybir.AxisListType.X

P = 128
D = 1024
KC = D // P
PROMPT, SAMPLE = 256, 8
T = PROMPT + SAMPLE
TILES = [(0, 128), (128, 128), (256, 8)]
H_MLA, NOPE, ROPE, LORA = 8, 128, 64, 128
H_GLA, DK, DV, CH = 4, 128, 256, 64
NCH = PROMPT // CH
H_MEM, NMEM = 4, 256
NE, TOPK, DFF = 32, 4, 1024
CAP = 64
MAX_PASS = -(-T // CAP)
PAST, PAGE, NPAGES = 2048, 128, 16
EPS = 1e-6
ATTN_SCALE = float((NOPE + ROPE) ** -0.5)
MEM_SCALE = float(P ** -0.5)
FAR = 1e4
NEG = -1e30
SLOT = 4096
TRUNK_SLOTS, MOE_SLOTS = 4, 6

C_CQ, C_CKV, C_KR, C_GQ, C_GK, C_GV, C_GG, C_GA, C_ZM, C_ZG = 0, 256, 384, 448, 960, 1472, 2496, 3520, 3536, 4560

GAINS = {"g_attn": 0, "g_mem": 8, "g_cross": 16, "g_ffn": 24, "g_final": 32, "g_q": 40, "g_kv": 42, "g_gla": 43, "b_a": 45}
N_GAINS = 49

CONSTS = {}
for _name, _n in [("ident", 128), ("ones", 128), ("before", 128), ("rot", 64), ("cos", T), ("sin", T),
                  ("carry", PROMPT), ("count", 64), ("causal", 256), ("own", 64), ("upto", 64), ("spread", 128),
                  ("within", 1), ("pick", 8 * 128)]:
    CONSTS[_name] = (sum(n for _, n in CONSTS.values()), _n)
N_CONST = sum(n for _, n in CONSTS.values())


def constants():
    f = np.float32
    c = np.zeros((P, N_CONST), f)

    def put(name, a):
        o, n = CONSTS[name]
        c[:a.shape[0], o:o + n] = a

    i = np.arange(P)
    put("ident", np.eye(P, dtype=f))
    put("ones", np.ones((P, P), f))
    put("before", (i[:, None] < i[None, :]).astype(f))
    r = np.zeros((64, 64), f)
    for a in range(32):
        r[a + 32, a] = -1
        r[a, a + 32] = 1
    put("rot", r)
    inv = (f(10000.0) ** (-np.arange(32, dtype=f) * f(2.0) / f(64))).astype(f)
    pos = np.concatenate([np.arange(PROMPT), np.full(SAMPLE, PAST)]).astype(f)
    ang = (pos[None, :] * inv[:, None]).astype(f)
    put("cos", np.tile(np.cos(ang), (2, 1)))
    put("sin", np.tile(np.sin(ang), (2, 1)))
    put("carry", np.tile((np.arange(PROMPT) % CH != 0).astype(f), (P, 1)))
    put("count", np.tile(np.arange(64, dtype=f), (P, 1)))
    put("causal", np.where(np.arange(256)[None, :] - 128 <= i[:, None], 0, NEG).astype(f))
    own = np.full((8, 8, 8), NEG, f)
    for b in range(8):
        own[b, b] = 0
    put("own", own.reshape(8, 64))
    s = np.arange(CH)
    put("upto", (s[:, None] <= s[None, :]).astype(f))
    put("spread", np.where(i[None, :] // 8 == np.arange(16)[:, None], 8, 0).astype(f))
    put("within", (i % 8).astype(f)[:, None])
    pick = np.zeros((8, 8, 128), f)
    for b in range(8):
        pick[b, b] = 1
    put("pick", pick.reshape(8, 1024))
    return c


EARLY = [f"gv{c}" for c in range(8)] + [f"gq{h}" for h in range(4)] + [f"gk{h}" for h in range(4)]

LIN = (["cq0", "cq1", "ckv", "kr", "rotk"] + [f"mk{h}" for h in range(4)] + ["mv0", "mv1"]
       + [f"qn{h}" for h in range(8)] + [f"qr{h}" for h in range(8)] + [f"rot{h}" for h in range(8)]
       + [f"ql{h}" for h in range(8)] + ["own"] + EARLY[0:2] + ["mmax", EARLY[2], "mbc", EARLY[3], "msum"]
       + [n for b in range(8) for n in EARLY[4 + 2 * b:5 + 2 * b] + [f"att{2 * b}"] + EARLY[5 + 2 * b:6 + 2 * b] + [f"past{b}", f"att{2 * b + 1}"]]
       + [f"uv{h}" for h in range(8)]
       + ["ga"]
       + [f"la{h}" for h in range(4)] + [n for b in range(8) for n in [f"vb{2 * b}", f"vb{2 * b + 1}"] + [f"gg{b}"] * (b < 6)] + [f"A{c}" for c in range(4)]
       + [f"kv{n}" for n in range(8)] + ["gg6", "gg7"]
       + [f"go{n}" for n in range(8)]
       + [f"zm{c}" for c in range(8)] + [f"zg{c}" for c in range(8)]
       + [f"om{c}" for c in range(8)] + [f"og{c}" for c in range(8)] + [f"wo{c}" for c in range(8)]
       + [f"mq{h}" for h in range(4)] + ["xmax", "xbc", "xsum"] + [n for b in range(8) for n in (f"xpast{b}", f"att{16 + b}")]
       + [f"mo{c}" for c in range(8)] + ["lg0", "lg1", "lg2", "rk0", "rk1", "rk2", "cnt"] + [f"bd{c}" for c in range(8)])
LI = {n: i for i, n in enumerate(LIN)}

NORM_CHUNKS = {1: KC, 2: KC, 3: 2, 4: 1, 5: KC, 6: KC, 7: KC, 8: KC}
BY_CHUNK = (1, 2, 6, 7, 8)

TURN = ([f"x{c}" for c in range(8)] + ["gains0", "gains1", "uk0", "uk1"] + [f"m{c}" for c in range(8)]
        + ["mkt0", "mkt1", "ckvt", "krt"]
        + [f"K{b}_{g}" for b in range(8) for g in range(6)] + [f"pt{u}" for u in range(16)]
        + [f"v{n}" for n in range(10)] + [f"ko{c}" for c in range(4)]
        + [f"X{n}" for n in range(16)] + [f"pt{u}" for u in range(16, 24)]
        + [f"hn{n}" for n in range(6)] + ["cwt"] + [f"y{n}" for n in range(6)])
TI = {n: i for i, n in enumerate(TURN)}

RING = [("in_a", "kr"), ("mk", "mk3"), ("mv", "mv1"), ("uq", "qr7"), ("gv0", "gv3"), ("gv1", "gv7"), ("gq", "gq3"), ("gk", "gk3"),
        ("uv", "uv7"), ("gg0", "gg3"), ("gg1", "gg7"), ("zm0", "zm3"), ("zm1", "zm7"), ("zg0", "zg3"), ("zg1", "zg7"),
        ("om0", "om3"), ("om1", "om7"), ("og0", "og3"), ("og1", "og7"), ("wo0", "wo3"), ("wo1", "wo7"), ("mq", "mq3"), ("mo", "mo7")]
RI = {n: i for i, (n, _) in enumerate(RING)}


def build(nc, ins, outs, consts, gains):
    (x_prompt, x_sample, cache_lat, cache_rope, state_gla, mem_k_in, mem_v_in, page_table, mem_prompt, w_in,
     w_uq, w_uk, w_uv, w_a2, w_o_mla, w_o_gla, w_out, w_mk, w_mv, w_mq, w_mo,
     w_router, b_router, w_gate_up, b_gate_up, w_down, b_down) = ins
    (y_prompt, y_sample, o_lat_p, o_rope_p, o_state_p, o_memk_p, o_memv_p, o_lat_s, o_rope_s, o_state_s) = outs

    ctx = ExitStack()
    with ctx:
        sems = {}

        def S(name):
            if name not in sems:
                sems[name] = ctx.enter_context(nc.semaphore("s_" + name))
            return sems[name]

        def sb(name, n, dt=F32, p=P):
            return ctx.enter_context(nc.sbuf_tensor(name, [p, n], dt))

        B = [ctx.enter_context(nc.psum_tensor(f"bank{i}", [P, 512], F32)) for i in range(8)]
        TURN_BANKS, SCORE_BANK = [B[5], B[6]], B[7]
        SCORE_BANKS = [B[7], B[4]]
        C = sb("consts_sb", N_CONST)
        ring = sb("ring", MOE_SLOTS * SLOT)
        resid = sb("resid", KC * T)
        normed = sb("normed", KC * T)
        gT = sb("gains_t", N_GAINS)
        A = sb("arena", 19840)
        whole = sb("npass", 4, I32)

        def con(name, p=P):
            o, n = CONSTS[name]
            return C[0:p, o:o + n]

        ident, ones = con("ident"), con("ones")

        def slot(n):
            return ring[:, n * SLOT:(n + 1) * SLOT]

        def view(o, n, b=None):
            v = A[:, o:o + n]
            return v if b is None else v.rearrange("p (a b) -> p a b", b=b)

        X = ring[:, 4 * SLOT:6 * SLOT]

        def xview(o, n, b=None):
            v = X[:, o:o + n]
            return v if b is None else v.rearrange("p (a b) -> p a b", b=b)

        h_T = resid[:].rearrange("p (c t) -> p c t", t=T)
        n_T = normed[:].rearrange("p (c t) -> p c t", t=T)
        memk = view(0, 1024, NMEM)
        memv = view(1024, 1024, 512)
        squares = view(2048, 2112)
        big2, big3, big4, big5 = (view(4160 + 2112 * i, 2112, T) for i in range(4))
        o = [12608]

        def small(n, b=None):
            v = view(o[0], n, b)
            o[0] += n
            return v

        cq, ckvT, krT, rotk = small(2 * T, T), small(T), small(T), small(T)
        rstd = small(T, T)
        own_s, mxp, mxT, gm, dg, mbc, rinv, psums = (small(n) for n in (64, 64, 136, 1, 64, 64, 64, 64))
        ckv_tok, kr_tok = small(384, 128), small(192, 64)
        assert o[0] <= 15408
        KTl, KTr = [view(15408, 2048), squares[:, 0:2048]], [view(17456, 1024), view(10496, 1024)]
        ukT = KTl[0][:, 0:1024]
        scores = view(18480, 1024)
        pages = view(19504, 24)
        idx = A[:, 19528:19536].bitcast(U32)
        Q2 = view(19536, 128, 64)
        Qs = view(19664, 64)
        exps = view(19728, 4)
        w_r = sb("w_router_sb", 256)
        w_ga = sb("w_ga", 128)
        w_a2_sb = sb("w_a2_sb", 512, p=16)
        ga = A[0:16, 18816:18816 + T]
        b_r = sb("b_router_sb", NE, p=1)

        def lin_bank(name):
            return B[LI[name] % 4]

        def turn_bank(name):
            return TURN_BANKS[TI[name] % 2]

        def turn_sem(name):
            return S("turned_by_dve" if TI[name] % 2 == 0 else "turned_by_act")

        def turned(eng, name):
            eng.wait_ge(turn_sem(name), TI[name] // 2 + 1)

        def lin_done(eng, name):
            eng.wait_ge(S("product_out"), LI[name] + 1)

        def lin_full(eng, name):
            eng.wait_ge(S("product_full"), LI[name] + 1)

        def normed_done(eng, k, c=None):
            eng.wait_ge(S("normed"), sum(NORM_CHUNKS[j] for j in range(1, k)) + (NORM_CHUNKS[k] if c is None else c + 1))

        def squares_before(k):
            return sum(KC if j in BY_CHUNK else 1 for j in range(1, k))

        def w_ready(eng, name):
            n = RI[name]
            eng.wait_ge(S(f"slot{n % TRUNK_SLOTS}_loaded"), 16 * (n // TRUNK_SLOTS + 1))

        x_tok = xview(0, 3072, D)
        m_tok = xview(3072, 2048, D)
        memT = xview(5120, 2048, NMEM)
        gain_rows = view(4160 + 512, 128)
        wuk = view(10496, 1024)
        lat = [xview(2048 * i, 2048, 128) for i in range(2)]
        rop = [xview(4096 + 1024 * i, 1024) for i in range(2)]
        att = [xview(6144 + 256 * i, 256) for i in range(2)]
        attT = [xview(6656 + 256 * i, 256, 128) for i in range(2)]
        nmx = xview(7168, 48)

        UNITS = [(h, qb, (qb + 1) * 128) for h in range(H_MLA) for qb in range(2)] + [(h, qb, 256) for h in range(H_MEM) for qb in range(2)]

        gqT, gkT = view(15408, 1056, T), view(15408 + 1056, 1056, T)
        gla, gb = view(8384, 1056, T), view(8384 + 1056, 1056, T)
        gvT = big5
        ge, gtmp = view(12608, 1056, T), view(12608 + 1056, 1056, T)
        gla_squares = view(15408, 2112)
        states = view(2048, 4096).rearrange("p (h c v) -> p h c v", h=H_GLA, c=NCH)
        vb = view(18816, 1024, 512)
        st_buf = [view(2048 + 1024 * i, 1024, DV) for i in range(4)]
        v_tok = X[0:64, 0:4096].rearrange("p (c v) -> p c v", c=NCH)
        ko_tok = X[0:64, 4096:6144].rearrange("p (c k) -> p c k", c=NCH)
        AT = X[0:64, 6144:7168].rearrange("p (c h t) -> p c h t", c=NCH, h=H_GLA)
        vs_tok = X[0:8, 7168:8192]
        rstd_gla = view(12608, 4 * T, T)
        silu_gg = big5
        gla_out = big4
        mla_out, sig_zm, sig_zg = xview(0, 2112, T), xview(2112, 2112, T), xview(4224, 2112, T)

        qx, xo = view(4160, 1056, T), view(4160 + 1056, 1056, T)
        Kx = view(10496, 8192).rearrange("p (b t n) -> p b t n", b=8, t=2)
        Vx = [xview(1024 * b, 1024, 512) for b in range(8)]
        kxT = [view(8384 + 512 * i, 512) for i in range(2)]
        xs = view(8384 + 1024, 64)
        xmxp, xmxT, xgm, xdg, xmbc, xps, xrinv = (view(8384 + 1100 + 136 * i, 136) for i in range(7))
        xatt = [view(2048 + 256 * i, 256) for i in range(2)]
        xattT = [view(2560 + 256 * i, 256, 128) for i in range(2)]
        xnmx = view(3072, 48)
        rstd2 = view(3200, T, T)

        acc = view(17000, 2112, T)
        hn_tok = view(4160, 3072, D)
        mo_ = [7232]

        def moe_buf(n, b=None):
            v = view(mo_[0], n, b)
            mo_[0] += n
            return v

        xg = moe_buf(1024, P)
        gate, up, sg = moe_buf(512), moe_buf(512), moe_buf(512)
        hT = moe_buf(512, P)
        y_rows = moe_buf(1024)
        sel = moe_buf(3 * 2 * CAP, 2 * CAP)
        wsel = moe_buf(3 * 2 * CAP, 2 * CAP)
        wselT = moe_buf(T)
        pick_b = moe_buf(2 * CAP, CAP)
        b_gu = moe_buf(2 * DFF)
        posm = moe_buf(3 * 36, 36)
        cw = moe_buf(3 * 36, 36)
        take = moe_buf(3 * 32, 32)
        curp, curw, cureye = moe_buf(12, 4), moe_buf(6, 2), moe_buf(4)
        logits = moe_buf(96)
        top8, e4 = moe_buf(24), moe_buf(24)
        top_i = moe_buf(24).bitcast(U32)
        top_f = moe_buf(24)
        cwT = moe_buf(T)
        b_dn = moe_buf(1024)
        cnts = moe_buf(40)
        assert mo_[0] <= 17000
        y_tok = view(4160, 3072, D)

        block = ctx.enter_context(nc.Block())

        w_cols = lambda w, a, n: w[0, :, a:a + n].rearrange("(c p) n -> p c n", p=P)

        @block.sync
        def _(sp):
            def into(n, nk, cols):
                return slot(n)[:, 0:nk * cols].rearrange("p (c n) -> p c n", c=nk)

            trunk = {"in_a": (w_cols(w_in, 0, 448), 8, 448), "mk": (w_cols(w_mk, 0, 512), 8, 512), "mv": (w_cols(w_mv, 0, 512), 8, 512),
                     "uq": (w_cols(w_uq, 0, 1536), 2, 1536),
                     "uv": (w_uv[0].rearrange("r h v -> r (h v)")[:, None, :], 1, 1024),
                     "gq": (w_cols(w_in, C_GQ, 512), 8, 512), "gk": (w_cols(w_in, C_GK, 512), 8, 512),
                     "mq": (w_cols(w_mq, 0, 512), 8, 512), "mo": (w_cols(w_mo, 0, 1024), 4, 1024)}
            for half in range(2):
                for name, w, at in (("gv", w_in, C_GV), ("gg", w_in, C_GG), ("zm", w_in, C_ZM), ("zg", w_in, C_ZG),
                                    ("om", w_o_mla, 0), ("og", w_o_gla, 0), ("wo", w_out, 0)):
                    trunk[f"{name}{half}"] = (w_cols(w, at + 512 * half, 512), 8, 512)
            cut = CONSTS["before"][0]
            sp.dma_start(C[:, 0:cut], consts[:, 0:cut]).then_inc(S("units_loaded"), 16)
            for tt, (t0, n) in enumerate(TILES):
                src = x_prompt[0, t0:t0 + n, :] if tt < 2 else x_sample[:, 0, :]
                sp.dma_start(x_tok[0:n, tt, :], src).then_inc(S("x_loaded"), 16)
            sp.dma_start(gain_rows[0:N_GAINS, :], gains).then_inc(S("gains_loaded"), 16)
            for n, (name, _) in enumerate(RING):
                if n >= TRUNK_SLOTS:
                    lin_full(sp, RING[n - TRUNK_SLOTS][1])
                src, nk, cols = trunk[name]
                sp.dma_start(into(n % TRUNK_SLOTS, nk, cols), src).then_inc(S(f"slot{n % 4}_loaded"), 16)
                if name == "in_a":
                    sp.dma_start(C[:, cut:], consts[:, cut:]).then_inc(S("const_loaded"), 16)
                    sp.dma_start(wuk, w_uk[0].rearrange("r h n -> r (h n)")).then_inc(S("uk_loaded"), 16)
                    sp.dma_start(m_tok, mem_prompt[0].rearrange("(t p) d -> p t d", p=P)).then_inc(S("mem_loaded"), 16)

            def expert_weights(e):
                gu = w_gate_up[0, bass.ds(e, 1)].rearrange("o (c p) n -> p (o c) n", p=P)
                dn = w_down[0, bass.ds(e, 1)].rearrange("o (c p) n -> p (o c) n", p=P)
                return [gu[:, :, 512 * j:512 * j + 512] for j in range(4)] + [dn[:, :, 512 * j:512 * j + 512] for j in range(2)]

            last_reader = {n % TRUNK_SLOTS: reader for n, (_, reader) in enumerate(RING)}
            parts = expert_weights(0)
            for s in (3, 0, 1, 4, 5, 2):
                if s < TRUNK_SLOTS:
                    lin_full(sp, last_reader[s])
                elif s == TRUNK_SLOTS:
                    lin_full(sp, "xpast7")
                sp.dma_start(into(s, 8, 512), parts[s]).then_inc(S(f"expert_slot{s}"), 16)
            with sp.Fori(1, NE) as e:
                for s, src in enumerate(expert_weights(e)):
                    sp.wait_ge(S(f"slot{s}_used"), e)
                    sp.dma_start(into(s, 8, 512), src).then_inc(S(f"expert_slot{s}"), 16)
            sp.wait_ge(S("npass"), 1)
            npass = sp.value_load(whole[0:1, 0:1], min_val=1, max_val=MAX_PASS)
            with sp.If(npass > 1):
                with sp.Fori(1, npass) as p:
                    with sp.Fori(0, NE) as e:
                        for s, src in enumerate(expert_weights(e)):
                            sp.wait_ge(S(f"slot{s}_used"), p * NE + e)
                            sp.dma_start(into(s, 8, 512), src).then_inc(S(f"expert_slot{s}"), 16)
            turned(sp, "y4")
            turned(sp, "y5")
            for tt, (t0, n) in enumerate(TILES):
                dst = y_prompt[0, t0:t0 + n, :] if tt < 2 else y_sample[:, 0, :]
                sp.dma_start(dst, y_tok[0:n, tt, :]).then_inc(S("y_stored"), 16)
            sp.wait_ge(S("y_stored"), 48)

        @block.gpsimd
        def _(pool):
            pool.dma_start(pages[0:16, 0:8].bitcast(I32), page_table.rearrange("b j -> j b"), allow_slow_non_contiguous=True)\
                .then_inc(S("pages_loaded"), 16)
            pool.dma_start(w_ga.rearrange("p (c n) -> p c n", c=KC), w_cols(w_in, C_GA, 16)).then_inc(S("small_loaded"), 16)
            pool.dma_start(w_a2_sb[:], w_a2[0]).then_inc(S("small_loaded"), 16)
            pool.dma_start(w_r[:].rearrange("p (c n) -> p c n", c=KC), w_router[0].rearrange("(c p) n -> p c n", p=P)).then_inc(S("small_loaded"), 16)
            pool.dma_start(b_r[:], b_router).then_inc(S("small_loaded"), 16)

            lat_rows = cache_lat[0].rearrange("n (g t) r -> (n g) (t r)", g=8)
            rope_rows = cache_rope[0].rearrange("n (g t) r -> (n g) (t r)", g=8)
            def store_state(b):
                pool.wait_ge(S("state_new"), b + 1)
                pool.dma_start(o_state_s[0, b].rearrange("h k v -> k h v"), st_buf[b % 4]).then_inc(S(f"state_out{b % 4}"), 16)

            def gather_past(b, with_rope):
                off = bass.IndirectOffsetOnAxis(ap=idx[:, b:b + 1], axis=0)
                pool.indirect_dma_start(lat[b % 2].rearrange("p a b -> p (a b)"), None, lat_rows, off).then_inc(S(f"lat{b % 2}"), 16)
                if with_rope:
                    pool.indirect_dma_start(rop[b % 2], None, rope_rows, off).then_inc(S(f"rope{b % 2}"), 16)

            pool.wait_ge(S("idx"), 1)
            lin_full(pool, "mv1")
            gather_past(0, True)
            gather_past(1, True)
            lin_done(pool, "mv1")
            pool.dma_start(o_memv_p[0, 0].rearrange("(t p) h d -> p t (h d)", p=P), memv).then_inc(S("stored"), 16)
            mk_tok = [squares[:, 512 * i:512 * i + 512] for i in range(2)]
            for tt in range(2):
                turned(pool, f"mkt{tt}")
                pool.dma_start(o_memk_p[0, 0, tt * P:(tt + 1) * P].rearrange("p h d -> p (h d)"), mk_tok[tt]).then_inc(S("mem_k_stored"), 16)
            turned(pool, "ckvt")
            turned(pool, "krt")
            for tt, (t0, n) in enumerate(TILES):
                dl = o_lat_p[0, 0, t0:t0 + n, :] if tt < 2 else o_lat_s[0, :, 0, :]
                dr = o_rope_p[0, 0, t0:t0 + n, :] if tt < 2 else o_rope_s[0, :, 0, :]
                pool.dma_start(dl, ckv_tok[0:n, tt, :]).then_inc(S("stored"), 16)
                pool.dma_start(dr, kr_tok[0:n, tt, :]).then_inc(S("stored"), 16)
            for b in range(2, 8):
                pool.wait_ge(S("turn_full"), TI[f"K{b - 2}_5"] + 1)
                gather_past(b, True)
            for b in range(8):
                if b < 2:
                    pool.wait_ge(S("turn_full"), TI[f"K{b + 6}_5"] + 1)
                else:
                    lin_full(pool, f"past{b - 2}")
                gather_past(b, False)
            pool.wait_ge(S("past_scores"), 8)
            for b in range(8):
                if b == 2:
                    lin_full(pool, "uv7")
                if b >= 4:
                    pool.wait_ge(S(f"state_out{b % 4}"), 16)
                    pool.wait_ge(S("state_read"), b - 3)
                pool.dma_start(st_buf[b % 4], state_gla[0, b].rearrange("h k v -> k h v")).then_inc(S(f"state_in{b % 4}"), 16)
                if b >= 3:
                    store_state(b - 3)
            for b in range(5, 8):
                store_state(b)
            pool.wait_ge(S("states_done"), 1)
            pool.dma_start(o_state_p[0, 0].rearrange("h k v -> k h v"), states[:, :, NCH - 1, :]).then_inc(S("state_p_out"), 16)
            pool.wait_ge(S("state_p_out"), 16)
            lin_full(pool, "og7")
            for b in range(8):
                pool.dma_start(Kx[:, b], mem_k_in[0, b].rearrange("(t p) h d -> p t (h d)", p=P)).then_inc(S(f"xkeys{b}"), 16)
            lin_full(pool, "wo7")
            for b in range(8):
                pool.dma_start(Vx[b], mem_v_in[0, b].rearrange("(t p) h d -> p t (h d)", p=P)).then_inc(S(f"xvalues{b}"), 16)
            lin_full(pool, "xpast7")
            pool.dma_start(b_dn[0:32, :], b_down[0]).then_inc(S("b_down"), 16)
            pool.wait_ge(S("bias_cleared"), 1)
            pool.dma_start(b_gu[0:32, :], b_gate_up[0]).then_inc(S("b_gate_up"), 16)
            pool.wait_ge(S("stored"), 16 * 7)
            for i in range(4):
                pool.wait_ge(S(f"state_out{i}"), 32)

        @block.tensor
        def _(pe):
            order = [0, 0]

            def open_bank(name):
                assert LIN[order[0]] == name, name
                order[0] += 1
                if LI[name] >= 4:
                    pe.wait_ge(S("product_out"), LI[name] - 3)

            def lin(name, parts, width, m=P):
                open_bank(name)
                for j, (l, r) in enumerate(parts):
                    mm = nc.tensor.matmul(lin_bank(name)[0:m, 0:width], l, r, start=(j == 0), stop=(j == len(parts) - 1))
                mm.then_inc(S("product_full"), 1)

            def turn(name, parts):
                assert TURN[order[1]] == name, name
                order[1] += 1
                i = TI[name]
                if i >= 2:
                    pe.wait_ge(turn_sem(name), i // 2)
                for at, src in parts:
                    k, m = src.shape[0], src.shape[-1]
                    r = src.base_partition()
                    mm = nc.tensor.transpose(turn_bank(name)[0:m, at:at + k], src, ident[r:r + k, r:r + k])
                mm.then_inc(S("turn_full"), 1)

            def norm(k, src, nchunk, width, groups=1):
                pe.wait_ge(S("squares"), squares_before(k) + 1)
                for g in range(groups):
                    for c in range(nchunk):
                        mm = nc.tensor.matmul(B[4 + g][:, 0:width], ones, src[:, (g * nchunk + c) * width:(g * nchunk + c + 1) * width],
                                              start=(c == 0), stop=(c == nchunk - 1))
                mm.then_inc(S("square_sums"), 1)

            def norm_chunk(k, c, width=T):
                pe.wait_ge(S("squares"), squares_before(k) + c + 1)
                mm = nc.tensor.matmul(B[4][:, 0:width], ones, squares[:, c * width:(c + 1) * width], start=(c == 0), stop=(c == KC - 1))
                if c == KC - 1:
                    mm.then_inc(S("square_sums"), 1)

            def w(name, nk, cols):
                return slot(RI[name] % TRUNK_SLOTS)[:, 0:nk * cols].rearrange("p (c n) -> p c n", c=nk)

            def project(names, ring_name, nk, cols, rhs, width=T, m=P, first=0, norm_of_rhs=None):
                w_ready(pe, ring_name)
                for j, name in enumerate(names):
                    a = first + m * j
                    open_bank(name)
                    for k in range(nk):
                        if norm_of_rhs is not None and j == 0:
                            normed_done(pe, norm_of_rhs, k)
                        mm = nc.tensor.matmul(lin_bank(name)[0:m, 0:width], w(ring_name, nk, cols)[:, k, a:a + m], rhs[:, k, 0:width],
                                              start=(k == 0), stop=(k == nk - 1))
                    mm.then_inc(S("product_full"), 1)

            pe.wait_ge(S("units_loaded"), 16)
            pe.wait_ge(S("x_loaded"), 48)
            for c in range(KC):
                turn(f"x{c}", [(t0, x_tok[0:n, tt, c * P:(c + 1) * P]) for tt, (t0, n) in enumerate(TILES)])
                if c >= 3:
                    norm_chunk(1, c - 3)
            pe.wait_ge(S("gains_loaded"), 16)
            turn("gains0", [(0, gain_rows[0:32, :])])
            turn("gains1", [(0, gain_rows[32:N_GAINS, :])])
            for c in range(5, KC):
                norm_chunk(1, c)
            pe.wait_ge(S("pages"), 1)
            pe.wait_ge(S("const_loaded"), 16)
            nc.tensor.matmul(SCORE_BANK[:, 0:8], con("spread", 16), pages[0:16, 8:16], start=True, stop=True).then_inc(S("page_rows"), 1)
            pe.wait_ge(S("uk_loaded"), 16)
            for g in range(2):
                turn(f"uk{g}", [(128 * j, wuk[:, (4 * g + j) * 128:(4 * g + j + 1) * 128]) for j in range(4)])
            pe.wait_ge(S("mem_loaded"), 16)
            for c in range(KC):
                turn(f"m{c}", [(128 * t, m_tok[:, t, c * P:(c + 1) * P]) for t in range(2)])
            project(["cq0", "cq1"], "in_a", 8, 448, n_T, norm_of_rhs=1)
            for c in range(KC):
                norm_chunk(2, c, NMEM)
            project(["ckv"], "in_a", 8, 448, n_T, first=256)
            lin("kr", [(w("in_a", 8, 448)[:, k, C_KR:C_KR + ROPE], n_T[:, k, :]) for k in range(KC)], T, ROPE)
            lin_done(pe, "kr")
            lin("rotk", [(con("rot", 64), krT[0:64, :])], T, ROPE)
            project([f"mk{h}" for h in range(4)], "mk", 8, 512, memT, NMEM, norm_of_rhs=2)
            norm(3, squares, 2, T)
            w_ready(pe, "mv")
            for t in range(2):
                lin(f"mv{t}", [(memT[:, k, t * P:(t + 1) * P], w("mv", 8, 512)[:, k, :]) for k in range(KC)], 512)
            norm(4, squares, 1, T)
            normed_done(pe, 3)
            w_ready(pe, "uq")
            for h in range(H_MLA):
                lin(f"qn{h}", [(w("uq", 2, 1536)[:, k, 192 * h:192 * h + 128], cq[:, k, :]) for k in range(2)], T)
            for h in range(H_MLA):
                lin(f"qr{h}", [(w("uq", 2, 1536)[:, k, 192 * h + 128:192 * h + 192], cq[:, k, :]) for k in range(2)], T, ROPE)
            lin_done(pe, "mk3")
            for tt in range(2):
                turn(f"mkt{tt}", [(128 * h, memk[:, h, tt * P:(tt + 1) * P]) for h in range(4)])
            normed_done(pe, 4)
            turn("ckvt", [(128 * tt, ckvT[:, t0:t0 + n]) for tt, (t0, n) in enumerate(TILES)])
            pe.wait_ge(S("k_roped"), 1)
            turn("krt", [(64 * tt, krT[0:64, t0:t0 + n]) for tt, (t0, n) in enumerate(TILES)])
            for h in range(H_MLA):
                lin_done(pe, f"qr{h}")
                lin(f"rot{h}", [(con("rot", 64), big3[0:64, h, :])], T, ROPE)
            turned(pe, "uk0")
            turned(pe, "uk1")
            for h in range(H_MLA):
                lin_done(pe, f"qn{h}")
                lin(f"ql{h}", [(ukT[:, 128 * h:128 * h + 128], big2[:, h, :])], T)
            pe.wait_ge(S("q_sample"), 3)
            lin("own", [(ckvT[:, PROMPT:T], Qs), (krT[0:64, PROMPT:T], Q2[0:64, 0, :])], 64, SAMPLE)
            def turn_keys(b):
                pe.wait_ge(S(f"lat{b % 2}"), 16 * (b // 2 + 1))
                for g in range(4):
                    turn(f"K{b}_{g}", [(128 * j, lat[b % 2][:, 4 * g + j, :]) for j in range(4)])
                pe.wait_ge(S(f"rope{b % 2}"), 16 * (b // 2 + 1))
                for g in range(2):
                    turn(f"K{b}_{4 + g}", [(128 * j, rop[b % 2][:, (4 * g + j) * 128:(4 * g + j + 1) * 128]) for j in range(4)])

            turn_keys(0)
            for b in range(8):
                if b < 7:
                    turn_keys(b + 1)
                if b >= 2:
                    pe.wait_ge(S("past_scores_read"), b - 1)
                turned(pe, f"K{b}_4")
                turned(pe, f"K{b}_5")
                for i in range(8):
                    out = SCORE_BANKS[b % 2][:, 16 * i:16 * i + 16]
                    nc.tensor.matmul(out, KTr[b % 2][:, 128 * i:128 * i + 128], Q2[:, :, 8 * b:8 * b + 8], start=True, stop=False)
                    for j in range(2):
                        mm = nc.tensor.matmul(out[:, 8 * j:8 * j + 8], KTl[b % 2][:, 256 * i + 128 * j:256 * i + 128 * j + 128],
                                              Qs[:, 8 * b:8 * b + 8], start=False, stop=(j == 1))
                mm.then_inc(S("past_scores"), 1)

            def early(*numbers):
                for n in numbers:
                    if n < len(EARLY):
                        group, at = [("gv0", 0), ("gv1", 4), ("gq", 8), ("gk", 12)][n // 4]
                        project([EARLY[n]], group, 8, 512, n_T, first=128 * (n - at))

            def batch_softmax(a, nbh, part, own):
                if a == "m":
                    early(0, 1)
                pe.wait_ge(S(a + "_part_max"), 1)
                open_bank(a + "max")
                mm = nc.tensor.transpose(lin_bank(a + "max")[0:nbh, 0:P], part, ident)
                if own is not None:
                    mm = nc.tensor.transpose(lin_bank(a + "max")[0:nbh, P:P + 8], own, ident[0:8, 0:8])
                mm.then_inc(S("product_full"), 1)
                if a == "m":
                    early(2)
                pe.wait_ge(S(a + "_max_diag"), 1)
                lin(a + "bc", [(ones[0:nbh, :], (dg if a == "m" else xdg)[0:nbh, 0:nbh])], nbh)
                if a == "m":
                    early(3)

            batch_softmax("m", 64, mxp, own_s[0:8, :])
            pe.wait_ge(S("m_part_sum"), 1)
            lin("msum", [(ones, psums), (ones[0:8, :], own_s[0:8, :])], 64)

            def unit_scores(u):
                h, qb, kw = UNITS[u]
                if u % 16 == 0 and u < 16:
                    pe.wait_ge(S("past_scores_read"), 8)
                    pe.wait_ge(S("q_roped"), 1)
                if u >= 2:
                    pe.wait_ge(S("scores_read"), u - 1)
                out = SCORE_BANKS[u % 2][:, 0:kw]
                q0 = qb * P
                if u < 16:
                    nc.tensor.matmul(out, big4[:, h, q0:q0 + P], ckvT[:, 0:kw], start=True, stop=False)
                    mm = nc.tensor.matmul(out, big3[:, h, q0:q0 + P], krT[:, 0:kw], start=False, stop=True)
                else:
                    mm = nc.tensor.matmul(out, qx[:, h, q0:q0 + P], memk[:, h, 0:kw], start=True, stop=True)
                mm.then_inc(S("scores"), 1)

            def unit_values(u):
                h, qb, kw = UNITS[u]
                pe.wait_ge(S("probs"), u + 1)
                buf, bufT = (att, attT) if u < 16 else (xatt, xattT)
                turn(f"pt{u}", [(128 * j, buf[u % 2][:, 128 * j:128 * j + 128]) for j in range(kw // 128)])
                turned(pe, f"pt{u}")
                if u < 16:
                    parts = [(ckv_tok[:, j, :], bufT[u % 2][:, j, :]) for j in range(kw // 128)]
                else:
                    parts = [(memv[:, j, 128 * h:128 * h + 128], bufT[u % 2][:, j, :]) for j in range(kw // 128)]
                lin(f"att{u}", parts, P)

            def past_values(b, first, last):
                out = lin_bank(f"past{b}")[:, 0:8]
                if first == 0:
                    pe.wait_ge(S("product_out"), max(LI[f"past{b}"] - 3, 1))
                    nc.tensor.matmul(out, ckv_tok[0:8, 2, :], own_s[0:8, 8 * b:8 * b + 8], start=True, stop=False)
                    pe.wait_ge(S(f"lat{b % 2}"), 16 * (5 + b // 2))
                else:
                    open_bank(f"past{b}")
                for t in range(first, last):
                    mm = nc.tensor.matmul(out, lat[b % 2][:, t, :], scores[:, 128 * b + 8 * t:128 * b + 8 * t + 8],
                                          start=False, stop=(t == 15))
                if last == 16:
                    mm.then_inc(S("product_full"), 1)

            turned(pe, "ckvt")
            unit_scores(0)
            for u in range(16):
                if u < 15:
                    unit_scores(u + 1)
                early(4 + u)
                past_values(u // 2, 8 * (u % 2), 8 * (u % 2) + 8)
                unit_values(u)
            pe.wait_ge(S("olat_sample"), 1)
            w_ready(pe, "uv")
            lin_done(pe, "att15")
            for h in range(H_MLA):
                lin(f"uv{h}", [(w("uv", 1, 1024)[:, 0, 128 * h:128 * h + 128], big2[:, h, :])], T)

            pe.wait_ge(S("small_loaded"), 64)
            lin("ga", [(w_ga[:, 16 * k:16 * k + 16], n_T[:, k, :]) for k in range(KC)], T, 16)
            lin_done(pe, "ga")
            for h in range(H_GLA):
                lin(f"la{h}", [(w_a2_sb[:, 128 * h:128 * h + 128], ga)], T)
            lin_done(pe, "gv7")
            for c in range(NCH):
                for g in range(2):
                    turn(f"v{2 * c + g}", [(128 * j, gvT[:, 4 * g + j, CH * c:CH * c + CH]) for j in range(4)])
            for g in range(2):
                turn(f"v{8 + g}", [(128 * j, gvT[:, 4 * g + j, PROMPT:T]) for j in range(4)])
            turned(pe, "v8")
            turned(pe, "v9")

            def state_times_q(b):
                pe.wait_ge(S("state_new"), b + 1)
                for hj in range(8):
                    mm = nc.tensor.matmul(SCORE_BANK[:, 8 * hj + b:8 * hj + b + 1],
                                          st_buf[b % 4][:, hj // 2, 128 * (hj % 2):128 * (hj % 2) + 128],
                                          gqT[:, hj // 2, PROMPT + b:PROMPT + b + 1], start=True, stop=True)
                mm.then_inc(S("state_read"), 1)

            for b in range(8):
                for half in range(2):
                    lin(f"vb{2 * b + half}", [(con("pick", 8)[:, 128 * b:128 * b + 128], vs_tok[:, 512 * half:512 * half + 512])], 512)
                if b < 6:
                    project([f"gg{b}"], f"gg{b // 4}", 8, 512, n_T, first=128 * (b % 4))
                if b >= 1:
                    state_times_q(b - 1)
            state_times_q(7)
            pe.wait_ge(S("gla_qk"), 1)
            for c in range(NCH):
                name = f"A{c}"
                open_bank(name)
                for h in range(H_GLA):
                    mm = nc.tensor.matmul(lin_bank(name)[0:CH, CH * h:CH * h + CH], gkT[:, h, CH * c:CH * c + CH],
                                          gqT[:, h, CH * c:CH * c + CH], start=True, stop=True)
                mm.then_inc(S("product_full"), 1)
            pe.wait_ge(S("gla_kout"), 1)
            for c in range(NCH):
                turn(f"ko{c}", [(128 * h, gtmp[:, h, CH * c:CH * c + CH]) for h in range(H_GLA)])
            turned(pe, "v6")
            turned(pe, "v7")
            for h in range(H_GLA):
                for half in range(2):
                    name = f"kv{2 * h + half}"
                    open_bank(name)
                    for c in range(2 * half, 2 * half + 2):
                        turned(pe, f"ko{c}")
                        mm = nc.tensor.matmul(lin_bank(name)[:, DV * (c % 2):DV * (c % 2) + DV], ko_tok[:, c, 128 * h:128 * h + 128],
                                              v_tok[:, c, DV * h:DV * h + DV], start=True, stop=True)
                    mm.then_inc(S("product_full"), 1)
            project(["gg6", "gg7"], "gg1", 8, 512, n_T, first=256)
            pe.wait_ge(S("gla_scores"), 1)
            pe.wait_ge(S("states_done"), 1)
            for h in range(H_GLA):
                for j in range(2):
                    name = f"go{2 * h + j}"
                    open_bank(name)
                    for c in range(NCH):
                        out = lin_bank(name)[:, CH * c:CH * c + CH]
                        a = DV * h + 128 * j
                        mm = nc.tensor.matmul(out, v_tok[:, c, a:a + 128], AT[:, c, h, :], start=True, stop=(c == 0))
                        if c:
                            mm = nc.tensor.matmul(out, states[:, h, c - 1, 128 * j:128 * j + 128], gqT[:, h, CH * c:CH * c + CH],
                                                  start=False, stop=True)
                    mm.then_inc(S("product_full"), 1)
            for name in ("zm", "zg"):
                for half in range(2):
                    project([f"{name}{c}" for c in range(4 * half, 4 * half + 4)], f"{name}{half}", 8, 512, n_T)
                    if (name, half) == ("zm", 0):
                        turned(pe, "ko2")
                        turned(pe, "ko3")
                        norm(5, gla_squares, 2, T, groups=4)
            for half in range(2):
                project([f"om{c}" for c in range(4 * half, 4 * half + 4)], f"om{half}", 8, 512, big3)
            pe.wait_ge(S("gla_gated"), 1)
            for half in range(2):
                project([f"og{c}" for c in range(4 * half, 4 * half + 4)], f"og{half}", 8, 512, gla_out)
            pe.wait_ge(S("merged"), 8)
            for c in range(KC):
                project([f"wo{c}"], f"wo{c // 4}", 8, 512, mla_out, first=128 * (c % 4))
                if c >= 2:
                    norm_chunk(6, c - 2)
            norm_chunk(6, 6)
            norm_chunk(6, 7)
            project([f"mq{h}" for h in range(4)], "mq", 8, 512, n_T, norm_of_rhs=6)
            lin_done(pe, "mq3")
            for n in range(17):
                if n < 16:
                    b, t = n // 2, n % 2
                    pe.wait_ge(S(f"xkeys{b}"), 16)
                    turn(f"X{n}", [(128 * h, Kx[:, b, t, 128 * h:128 * h + 128]) for h in range(4)])
                if n >= 1:
                    m = n - 1
                    turned(pe, f"X{m}")
                    for h in range(4):
                        mm = nc.tensor.matmul(SCORE_BANK[:, 4 * m + h:4 * m + h + 1], kxT[m % 2][:, 128 * h:128 * h + 128],
                                              qx[:, h, PROMPT + m // 2:PROMPT + m // 2 + 1], start=True, stop=True)
                    mm.then_inc(S("x_scores"), 1)
            batch_softmax("x", 32, xmxp[:, 0:32], None)
            pe.wait_ge(S("x_part_sum"), 1)
            lin("xsum", [(ones, xps[:, 0:32])], 32)
            unit_scores(16)
            for b in range(8):
                if b < 7:
                    unit_scores(17 + b)
                open_bank(f"xpast{b}")
                pe.wait_ge(S(f"xvalues{b}"), 16)
                for h in range(4):
                    for t in range(2):
                        mm = nc.tensor.matmul(lin_bank(f"xpast{b}")[:, h:h + 1], Vx[b][:, t, 128 * h:128 * h + 128],
                                              xs[:, 8 * b + 4 * t + h:8 * b + 4 * t + h + 1], start=(t == 0), stop=(t == 1))
                mm.then_inc(S("product_full"), 1)
                unit_values(16 + b)
            pe.wait_ge(S("xo_sample"), 1)
            lin_done(pe, "att23")
            w_ready(pe, "mo")
            for c in range(KC):
                lin(f"mo{c}", [(w("mo", 4, 1024)[:, k, 128 * c:128 * c + 128], xo[:, k, :]) for k in range(4)], T)
                if c >= 2:
                    norm_chunk(7, c - 2)
            norm_chunk(7, 6)
            norm_chunk(7, 7)
            for tt, (t0, n) in enumerate(TILES):
                open_bank(f"lg{tt}")
                logit = lin_bank(f"lg{tt}")[0:n, 0:NE]
                nc.tensor.matmul(logit, ones[0:1, 0:n], b_r[:], start=True, stop=False)
                for k in range(KC):
                    if tt == 0:
                        normed_done(pe, 7, k)
                    mm = nc.tensor.matmul(logit, n_T[:, k, t0:t0 + n], w_r[:, 32 * k:32 * k + 32], start=False, stop=(k == KC - 1))
                mm.then_inc(S("product_full"), 1)
            for i in range(6):
                tt, g = i // 2, i % 2
                t0, n = TILES[tt]
                turn(f"hn{i}", [(128 * j, n_T[:, 4 * g + j, t0:t0 + n]) for j in range(4)])
            pe.wait_ge(S("routed"), 3)
            for tt, (t0, n) in enumerate(TILES):
                lin(f"rk{tt}", [(ones[:, 0:n], take[:, j, :]) for j in range(tt)] + [(con("before")[0:n, 0:n], take[0:n, tt, :])], NE, n)
            lin("cnt", [(ones[0:n, :], take[0:n, tt, :]) for tt, (_, n) in enumerate(TILES)], NE)
            turn("cwt", [(t0, cw[0:n, tt, 0:32]) for tt, (t0, n) in enumerate(TILES)])
            turned(pe, "cwt")
            pe.wait_ge(S("b_down"), 16)
            for c in range(KC):
                lin(f"bd{c}", [(b_dn[0:32, 128 * c:128 * c + 128], cwT[0:32, :])], T)
            lin_done(pe, "bd7")

            def gather():
                for k in range(KC):
                    for tt, (_, n) in enumerate(TILES):
                        mm = nc.tensor.matmul(B[2 + 3 * (k // 4)][:, P * (k % 4):P * (k % 4) + P], hn_tok[0:n, tt, 128 * k:128 * k + 128],
                                              sel[0:n, tt, :], start=(tt == 0), stop=(tt == 2))
                    if k % 4 == 3:
                        mm.then_inc(S("gathered"), 1)

            def slot_w(j):
                return slot(j)[:].rearrange("p (c n) -> p c n", c=KC)

            def both_halves(bank, lhs_of, j, first):
                for k in range(KC):
                    for half in range(2):
                        mm = nc.tensor.matmul(bank[CAP * half:CAP * half + CAP, :], lhs_of(k), slot_w(j + half)[:, k, :],
                                              start=(k == 0 and first), stop=(k == KC - 1))
                        if k == KC - 1:
                            mm.then_inc(S(f"slot{j + half}_used"), 1)

            def scatter(m, first, last):
                pe.wait_ge(S("y_rows"), 4 * m + 4)
                pe.wait_ge(S("weights_copied"), m + 1)
                for c in range(first, last):
                    if c >= 3:
                        pe.wait_ge(S("added"), 8 * m + c - 2)
                    nc.tensor.matmul(B[5 + c % 3][:, 0:T], y_rows[:, 128 * c:128 * c + 128], wselT, start=True, stop=True)\
                        .then_inc(S("scattered"), 1)

            def expert_pair(m, p):
                pe.wait_ge(S("x_pair"), 2 * m + 2 * p + 2)
                pe.wait_ge(S("bias_picked"), m + p + 1)
                for e in range(2):
                    n = 2 * m + e
                    for bank in range(2):
                        if e == 0 and bank == 1:
                            scatter(m, 0, 5)
                        for half in range(2):
                            nc.tensor.matmul(B[bank][CAP * half:CAP * half + CAP, :], pick_b[:, e, :],
                                             b_gu[:, 1024 * bank + 512 * half:1024 * bank + 512 * half + 512], start=True, stop=False)
                        for half in range(2):
                            pe.wait_ge(S(f"expert_slot{2 * bank + half}"), 16 * n + 16)
                        both_halves(B[bank], lambda k: xg[:, k, CAP * e:CAP * e + CAP], 2 * bank, False)
                    if e == 0:
                        scatter(m, 5, KC)
                        pe.wait_ge(S("weighted"), m + 1)
                        for tt, (t0, k) in enumerate(TILES):
                            mm = nc.tensor.transpose(B[2][:, t0:t0 + k], wsel[0:k, tt, :], ident[0:k, 0:k])
                        mm.then_inc(S("weights_turned"), 1)
                    else:
                        pe.wait_ge(S("selected"), m + p + 2)
                        pe.wait_ge(S("weights_copied"), m + 2)
                        pe.wait_ge(S("added"), 8 * m + 8)
                        gather()
                    pe.wait_ge(S("hidden"), n + 1)
                    for j in range(4):
                        mm = nc.tensor.transpose(B[3][:, 128 * j:128 * j + 128], up[:, 128 * j:128 * j + 128], ident)
                    mm.then_inc(S("hidden_turned"), 1)
                    pe.wait_ge(S("hT"), n + 1)
                    pe.wait_ge(S("y_rows"), 2 * n + 4)
                    for half in range(2):
                        pe.wait_ge(S(f"expert_slot{4 + half}"), 16 * n + 16)
                    both_halves(B[4], lambda k: hT[:, k % 4, CAP * (k // 4):CAP * (k // 4) + CAP], 4, True)

            turned(pe, "hn4")
            turned(pe, "hn5")
            pe.wait_ge(S("b_gate_up"), 16)
            pe.wait_ge(S("selected"), 1)
            gather()
            with pe.Fori(0, NE // 2) as q:
                expert_pair(q, 0)
            npass = pe.value_load(whole[0:1, 0:1], min_val=1, max_val=MAX_PASS)
            with pe.If(npass > 1):
                with pe.Fori(1, npass) as p:
                    pe.wait_ge(S("selected"), p * (NE // 2 + 1) + 1)
                    pe.wait_ge(S("x_pair"), 2 * p * (NE // 2 + 1))
                    gather()
                    with pe.Fori(0, NE // 2) as q:
                        expert_pair(p * (NE // 2) + q, p)
            pe.wait_ge(S("added"), npass * (8 * NE // 2))
            scatter(npass * (NE // 2), 0, KC)
            for c in range(KC):
                norm_chunk(8, c)
            normed_done(pe, 8)
            for i in range(6):
                tt, g = i // 2, i % 2
                t0, n = TILES[tt]
                turn(f"y{i}", [(128 * j, n_T[:, 4 * g + j, t0:t0 + n]) for j in range(4)])
            assert order == [len(LIN), len(TURN)]

        @block.scalar
        def _(act):
            order = [0]
            steps = [0]

            def link(ins):
                steps[0] += 1
                ins.then_inc(S("act_step"), 1)
                act.wait_ge(S("act_step"), steps[0])

            def out(name, dst, func=ACT.Copy, m=P, width=T, src=None, **kw):
                assert LIN[order[0]] == name, name
                order[0] += 1
                lin_full(act, name)
                nc.scalar.activation(dst, lin_bank(name)[0:m, 0:width] if src is None else src, func, **kw).then_inc(S("product_out"), 1)

            def turn_out(name, parts):
                assert TI[name] % 2 == 1, name
                act.wait_ge(S("turn_full"), TI[name] + 1)
                for dst, m, (a, b) in parts:
                    ins = nc.scalar.copy(dst, turn_bank(name)[0:m, a:b])
                ins.then_inc(S("turned_by_act"), 1)

            def root(k, dst):
                act.wait_ge(S("inverse"), k)
                nc.scalar.activation(dst, dst, ACT.Sqrt).then_inc(S("rstd"), 1)

            for c in range(1, KC, 2):
                turn_out(f"x{c}", [(h_T[:, c, :], P, (0, T))])
            turn_out("gains1", [(gT[:, 32:N_GAINS], P, (0, N_GAINS - 32))])
            act.wait_ge(S("square_sums"), 1)
            turn_out("uk1", [(ukT[:, 512:1024], P, (0, 512))])
            root(1, rstd)
            for c in range(1, KC, 2):
                turn_out(f"m{c}", [(memT[:, c, :], P, (0, NMEM))])
            for c in range(2):
                out(f"cq{c}", cq[:, c, :])
            out("ckv", ckvT)
            act.wait_ge(S("rope_cleared"), 1)
            out("kr", krT[0:64, :], m=ROPE)
            out("rotk", rotk[0:64, :], m=ROPE)
            root(2, rstd[:, :, 0:NMEM])
            for h in range(4):
                out(f"mk{h}", memk[:, h, :], width=NMEM)
            root(3, rstd)
            for t in range(2):
                out(f"mv{t}", memv[:, t, :], width=512)
            root(4, rstd)
            for h in range(H_MLA):
                out(f"qn{h}", big2[:, h, :])
            for h in range(H_MLA):
                out(f"qr{h}", big3[0:64, h, :], m=ROPE)
            turn_out("mkt1", [(squares[:, 512:1024], P, (0, 512))])
            turn_out("krt", [(kr_tok[:, 0:2, :], P, (0, 128)), (kr_tok[0:8, 2, :], 8, (128, 192))])
            for h in range(H_MLA):
                out(f"rot{h}", big5[0:64, h, :], m=ROPE)
            for h in range(H_MLA):
                out(f"ql{h}", big4[:, h, :])
            out("own", own_s[0:8, :], m=8, width=64, scale=ATTN_SCALE)
            for b in range(8):
                if b >= 2:
                    act.wait_ge(S("past_scores"), b - 1)
                elif b == 1:
                    act.wait_ge(S("mem_k_stored"), 32)
                    act.wait_ge(S("q_roped"), 1)
                else:
                    lin_full(act, "ql7")
                for g in (1, 3, 5):
                    dst = KTl[b % 2][:, 512 * g:512 * g + 512] if g < 4 else KTr[b % 2][:, 512:1024]
                    turn_out(f"K{b}_{g}", [(dst, P, (0, 512))])

            def early(*numbers):
                for n in numbers:
                    if n < 8:
                        out(EARLY[n], gvT[:, n, :])
                    elif n < 12:
                        out(EARLY[n], gqT[:, n - 8, :], scale=float(DK ** -0.5))
                    elif n < 16:
                        out(EARLY[n], gkT[:, n - 12, :])

            def batch(a, nbh, own_n, exps_of):
                if a == "m":
                    early(0, 1)
                out(a + "max", (mxT if a == "m" else xmxT)[0:nbh, 0:P + own_n], m=nbh, width=P + own_n)
                if a == "m":
                    early(2)
                out(a + "bc", (mbc if a == "m" else xmbc)[:, 0:nbh], width=nbh)
                act.wait_ge(S(a + "_shifted"), len(exps_of))
                for e in exps_of:
                    nc.scalar.activation(e, e, ACT.Exp).then_inc(S(a + "_exp"), 1)
                if a == "m":
                    early(3)

            batch("m", 64, 8, [scores, own_s[0:8, :]])
            out("msum", mbc, width=64)

            def unit_exp(u):
                buf, nb = (att, nmx) if u < 16 else (xatt, xnmx)
                kw, v = UNITS[u][2], u % 16
                act.wait_ge(S("shifted"), u + 1)
                nc.scalar.activation(buf[u % 2][:, 0:kw], buf[u % 2][:, 0:kw], ACT.Exp, bias=nb[:, v:v + 1],
                                     accum_out=nb[:, 16 + v:17 + v]).then_inc(S("exped"), 1)

            def unit_out(u):
                h, qb, kw = UNITS[u]
                bufT = attT if u < 16 else xattT
                if TI[f"pt{u}"] % 2:
                    turn_out(f"pt{u}", [(bufT[u % 2].rearrange("p a b -> p (a b)")[:, 0:kw], P, (0, kw))])
                out(f"att{u}", (big2 if u < 16 else xo)[:, h, qb * P:qb * P + P], width=P)

            unit_exp(0)
            for u in range(16):
                if u < 15:
                    unit_exp(u + 1)
                early(4 + u)
                if u % 2:
                    out(f"past{u // 2}", mxp[:, 8 * (u // 2):8 * (u // 2) + 8], width=8)
                unit_out(u)
            for h in range(H_MLA):
                out(f"uv{h}", big3[:, h, :])
            out("ga", ga, m=16)
            for h in range(4):
                out(f"la{h}", gla[:, h, :], ACT.Identity, bias=gT[:, GAINS["b_a"] + h:GAINS["b_a"] + h + 1])
            lin_done(act, "la3")
            link(nc.scalar.activation(gb, gla, ACT.Abs))
            link(nc.scalar.activation(gb, gb, ACT.Exp, scale=-1.0))
            nc.scalar.activation(gb, gb, ACT.Ln, bias=1.0).then_inc(S("softplus"), 1)
            for n in range(10):
                if TI[f"v{n}"] % 2:
                    c, g = n // 2, n % 2
                    dst, m = (v_tok[:, c, 512 * g:512 * g + 512], CH) if n < 8 else (vs_tok[:, 512 * g:512 * g + 512], 8)
                    turn_out(f"v{n}", [(dst, m, (0, 512))])
            act.wait_ge(S("cumulated"), 4)
            nc.scalar.activation(ge[:, :, 0:PROMPT], gb[:, :, 0:PROMPT], ACT.Exp, scale=1.0 / 16)
            nc.scalar.activation(ge[:, :, PROMPT:T], gla[:, :, PROMPT:T], ACT.Exp, scale=1.0 / 16).then_inc(S("decays"), 1)
            act.wait_ge(S("to_chunk_end"), 4)
            nc.scalar.activation(gtmp[:, :, 0:PROMPT], gtmp[:, :, 0:PROMPT], ACT.Exp, scale=1.0 / 16)
            nc.scalar.activation(gb[:, :, 0:PROMPT], gb[:, :, 0:PROMPT], ACT.Exp, scale=-1.0 / 16).then_inc(S("k_factors"), 1)
            for b in range(8):
                if b:
                    act.wait_ge(S("state_new"), b)
                for half in range(2):
                    out(f"vb{2 * b + half}", vb[:, half, :], width=512)
                if b < 6:
                    out(f"gg{b}", silu_gg[:, b, :], ACT.Silu)
            act.wait_ge(S("state_read"), 8)
            act.wait_ge(S("gla_qk"), 1)
            nc.scalar.copy(gla_out[:, :, PROMPT:T], SCORE_BANK[:, 0:64].rearrange("p (c b) -> p c b", b=8)).then_inc(S("gla_sample"), 1)
            for c in range(NCH):
                out(f"A{c}", AT[:, c].rearrange("p h t -> p (h t)"), m=CH, width=256)
            for c in range(NCH):
                if TI[f"ko{c}"] % 2:
                    turn_out(f"ko{c}", [(ko_tok[:, c, :], CH, (0, 512))])
            for i in range(4):
                act.wait_ge(S(f"state_out{i}"), 32)
            for n in range(8):
                h, half = n // 2, n % 2
                out(f"kv{n}", states[:, h, 2 * half:2 * half + 2, :].rearrange("p c v -> p (c v)"), width=512)
            for c in (6, 7):
                out(f"gg{c}", silu_gg[:, c, :], ACT.Silu)
            for n in range(8):
                out(f"go{n}", gla_out[:, n, 0:PROMPT], width=PROMPT)
            for c in range(KC):
                out(f"zm{c}", sig_zm[:, c, :], ACT.Sigmoid)
                if c == 3:
                    root(5, rstd_gla)
            for c in range(KC):
                out(f"zg{c}", sig_zg[:, c, :], ACT.Sigmoid)
            for c in range(KC):
                out(f"om{c}", mla_out[:, c, :])
            act.wait_ge(S("state_p_out"), 16)
            for c in range(KC):
                out(f"og{c}", big2[:, c, :])
            for c in range(KC):
                out(f"wo{c}", big2[:, c, :])
            root(6, rstd2)
            for h in range(4):
                out(f"mq{h}", qx[:, h, :])
            for n in range(16):
                if TI[f"X{n}"] % 2:
                    if n >= 2:
                        act.wait_ge(S("x_scores"), n - 1)
                    turn_out(f"X{n}", [(kxT[n % 2], P, (0, 512))])
            batch("x", 32, 0, [xs])
            out("xsum", xmbc[:, 0:32], width=32)
            unit_exp(16)
            for u in range(16, 24):
                if u < 23:
                    unit_exp(u + 1)
                out(f"xpast{u - 16}", xps[:, 4 * (u - 16):4 * (u - 16) + 4], width=4)
                unit_out(u)
            for c in range(KC):
                out(f"mo{c}", big4[:, c, :])
            root(7, rstd2)
            for tt, (_, n) in enumerate(TILES):
                out(f"lg{tt}", logits[0:n, 32 * tt:32 * tt + 32], m=n, width=NE)
            for i in range(6):
                if TI[f"hn{i}"] % 2:
                    tt, g = i // 2, i % 2
                    n = TILES[tt][1]
                    turn_out(f"hn{i}", [(hn_tok[0:n, tt, 512 * g:512 * g + 512], n, (0, 512))])
            for tt, (_, n) in enumerate(TILES):
                act.wait_ge(S("top_shifted"), tt + 1)
                nc.scalar.activation(e4[0:n, 8 * tt:8 * tt + 4], e4[0:n, 8 * tt:8 * tt + 4], ACT.Exp,
                                     accum_out=e4[0:n, 8 * tt + 4:8 * tt + 5]).then_inc(S("top_exp"), 1)
            for tt, (_, n) in enumerate(TILES):
                out(f"rk{tt}", posm[0:n, tt, 0:NE], m=n, width=NE)
            out("cnt", cnts[:, 0:NE], width=NE)
            if TI["cwt"] % 2:
                turn_out("cwt", [(cwT[0:NE, :], NE, (0, T))])
            for c in range(KC):
                out(f"bd{c}", acc[:, c, :])

            def gathered(g):
                for half in range(2):
                    act.wait_ge(S("gathered"), 2 * g + half + 1)
                    nc.scalar.copy(xg[:, 4 * half:4 * half + 4, :].rearrange("p a b -> p (a b)"), B[2 + 3 * half][:]).then_inc(S("x_pair"), 1)

            def expert_pair(m, p):
                for e in range(2):
                    n = 2 * m + e
                    act.wait_ge(S("gate"), n + 1)
                    nc.scalar.activation(sg, gate, ACT.Sigmoid, scale=1.702).then_inc(S("sigmoid"), 1)
                    if e == 0:
                        act.wait_ge(S("weights_turned"), m + 1)
                        nc.scalar.copy(wselT, B[2][:, 0:T]).then_inc(S("weights_copied"), 1)
                    else:
                        act.wait_ge(S("slot3_used"), n + 1)
                        gathered(m + p + 1)
                    act.wait_ge(S("hidden_turned"), n + 1)
                    nc.scalar.copy(hT.rearrange("p a b -> p (a b)"), B[3][:]).then_inc(S("hT"), 1)
                    act.wait_ge(S("slot5_used"), n + 1)
                    for half in range(2):
                        nc.scalar.copy(y_rows[CAP * e:CAP * e + CAP, 512 * half:512 * half + 512], B[4][CAP * half:CAP * half + CAP, :])\
                            .then_inc(S("y_rows"), 1)

            gathered(0)
            with act.Fori(0, NE // 2) as q:
                expert_pair(q, 0)
            act.wait_ge(S("npass"), 1)
            npass = act.value_load(whole[0:1, 0:1], min_val=1, max_val=MAX_PASS)
            with act.If(npass > 1):
                with act.Fori(1, npass) as p:
                    gathered(p * (NE // 2 + 1))
                    with act.Fori(0, NE // 2) as q:
                        expert_pair(p * (NE // 2) + q, p)
            root(8, rstd2)
            for i in range(6):
                if TI[f"y{i}"] % 2:
                    tt, g = i // 2, i % 2
                    n = TILES[tt][1]
                    turn_out(f"y{i}", [(y_tok[0:n, tt, 512 * g:512 * g + 512], n, (0, 512))])
            assert order[0] == len(LIN)

        @block.vector
        def _(dve):
            V = nc.vector
            steps = [0]

            def link(ins):
                steps[0] += 1
                ins.then_inc(S("dve_step"), 1)
                dve.wait_ge(S("dve_step"), steps[0])

            def turn_out(name, parts):
                assert TI[name] % 2 == 0, name
                dve.wait_ge(S("turn_full"), TI[name] + 1)
                for dst, m, (a, b) in parts:
                    ins = V.tensor_copy(dst, turn_bank(name)[0:m, a:b])
                ins.then_inc(S("turned_by_dve"), 1)

            def square(src, dst):
                V.tensor_tensor(dst, src, src, ALU.mult).then_inc(S("squares"), 1)

            def square_chunk(src, c, width):
                V.tensor_tensor(squares[:, c * width:(c + 1) * width], src, src, ALU.mult).then_inc(S("squares"), 1)

            def scale_by_rms(k, src, dst, gain, nchunk, width, dim, rs, groups=1):
                dve.wait_ge(S("square_sums"), k)
                for g in range(groups):
                    ins = V.tensor_scalar(rs[:, g, 0:width], B[4 + g][:, 0:width], 1.0 / dim, EPS, ALU.mult, ALU.add)
                link(ins)
                V.reciprocal(rs[:, :, 0:width], rs[:, :, 0:width]).then_inc(S("inverse"), 1)
                dve.wait_ge(S("rstd"), k)
                for c in range(nchunk * groups):
                    r = GAINS[gain] + c % nchunk
                    V.scalar_tensor_tensor(out=dst[:, c, :], in0=src[:, c, :], scalar=gT[:, r:r + 1], in1=rs[:, c // nchunk, 0:width],
                                           op0=ALU.mult, op1=ALU.mult).then_inc(S("normed"), 1)

            def flat(v):
                return v.rearrange("p a b -> p (a b)")

            def bc(v, shape):
                return v.to_broadcast(shape)

            V.memset(krT[64:128, :], 0.0)
            V.memset(big3[64:128, :, :], 0.0).then_inc(S("rope_cleared"), 1)
            dve.wait_ge(S("pages_loaded"), 16)
            V.tensor_copy(pages[0:16, 8:16], pages[0:16, 0:8].bitcast(I32)).then_inc(S("pages"), 1)
            for c in range(KC):
                if c % 2 == 0:
                    turn_out(f"x{c}", [(h_T[:, c, :], P, (0, T))])
                turned(dve, f"x{c}")
                square_chunk(h_T[:, c, :], c, T)
            turn_out("gains0", [(gT[:, 0:32], P, (0, 32))])
            dve.wait_ge(S("page_rows"), 1)
            V.tensor_scalar(idx, SCORE_BANK[:, 0:8], con("within"), None, ALU.add).then_inc(S("idx"), 1)
            turn_out("uk0", [(ukT[:, 0:512], P, (0, 512))])
            turned(dve, "gains1")
            scale_by_rms(1, h_T, n_T, "g_attn", KC, T, D, rstd)
            for c in range(KC):
                if c % 2 == 0:
                    turn_out(f"m{c}", [(memT[:, c, :], P, (0, NMEM))])
                turned(dve, f"m{c}")
                square_chunk(memT[:, c, :], c, NMEM)
            scale_by_rms(2, memT, memT, "g_mem", KC, NMEM, D, rstd)
            lin_done(dve, "cq1")
            square(flat(cq), squares[:, 0:2 * T])
            scale_by_rms(3, cq, cq, "g_q", 2, T, 256, rstd)
            lin_done(dve, "rotk")
            V.tensor_tensor(krT[0:64, :], krT[0:64, :], con("cos", 64), ALU.mult)
            link(V.tensor_tensor(rotk[0:64, :], rotk[0:64, :], con("sin", 64), ALU.mult))
            V.tensor_tensor(krT[0:64, :], krT[0:64, :], rotk[0:64, :], ALU.add).then_inc(S("k_roped"), 1)
            square(ckvT, squares[:, 0:T])
            scale_by_rms(4, ckvT[:, None, :], ckvT[:, None, :], "g_kv", 1, T, LORA, rstd)
            turn_out("mkt0", [(squares[:, 0:512], P, (0, 512))])
            turn_out("ckvt", [(flat(ckv_tok)[:, 0:256], P, (0, 256)), (ckv_tok[0:8, 2, :], 8, (256, 384))])
            lin_done(dve, "rot7")
            V.tensor_tensor(big3[0:64], big3[0:64], bc(con("cos", 64)[:, None, :], [64, 8, T]), ALU.mult)
            link(V.tensor_tensor(big5[0:64], big5[0:64], bc(con("sin", 64)[:, None, :], [64, 8, T]), ALU.mult))
            V.tensor_tensor(big3[0:64], big3[0:64], big5[0:64], ALU.add).then_inc(S("q_roped"), 1)
            link(V.memset(Q2, 0.0))
            dve.wait_ge(S("q_roped"), 1)
            for i in range(2):
                V.tensor_copy(Q2[64 * i:64 * i + 64, i, :].rearrange("p (b h) -> p h b", b=8), big3[0:64, :, PROMPT:T]).then_inc(S("q_sample"), 1)
            lin_done(dve, "ql7")
            V.tensor_copy(Qs.rearrange("p (b h) -> p h b", b=8), big4[:, :, PROMPT:T]).then_inc(S("q_sample"), 1)
            def keys_out(b):
                if b >= 2:
                    dve.wait_ge(S("past_scores"), b - 1)
                elif b == 1:
                    dve.wait_ge(S("mem_k_stored"), 32)
                for g in (0, 2, 4):
                    dst = KTl[b % 2][:, 512 * g:512 * g + 512] if g < 4 else KTr[b % 2][:, 0:512]
                    turn_out(f"K{b}_{g}", [(dst, P, (0, 512))])

            keys_out(0)
            for b in range(8):
                if b < 7:
                    keys_out(b + 1)
                dve.wait_ge(S("past_scores"), b + 1)
                V.tensor_scalar(scores[:, 128 * b:128 * b + 128], SCORE_BANKS[b % 2][:, 0:128], ATTN_SCALE, None,
                                ALU.mult).then_inc(S("past_scores_read"), 1)
            lin_done(dve, "own")
            link(V.tensor_tensor(own_s[0:8, :], own_s[0:8, :], con("own", 8), ALU.add))

            def batch(a, nbh, sc, nb, ntile, bufs, own):
                part, mT, g1, diag, mb, ps, inv = bufs
                by_bh = sc.rearrange("p (b i h) -> p b h i", b=nb, i=ntile)
                V.tensor_reduce(part[:, 0:nbh].rearrange("p (b h) -> p b h", b=nb), by_bh, AX, ALU.max).then_inc(S(a + "_part_max"), 1)
                lin_done(dve, a + "max")
                link(V.tensor_reduce(g1[0:nbh, 0:1], mT[0:nbh, 0:P + (8 if own is not None else 0)], AX, ALU.max))
                V.tensor_scalar(diag[0:nbh, 0:nbh], ident[0:nbh, 0:nbh], g1[0:nbh, 0:1], None, ALU.mult).then_inc(S(a + "_max_diag"), 1)
                lin_done(dve, a + "bc")
                V.tensor_tensor(by_bh, by_bh, bc(mb[:, 0:nbh].rearrange("p (b h o) -> p b h o", b=nb, o=1), [P, nb, nbh // nb, ntile]),
                                ALU.subtract).then_inc(S(a + "_shifted"), 1)
                n = 1
                if own is not None:
                    n = 2
                    V.tensor_tensor(own, own, mb[0:8, 0:nbh], ALU.subtract).then_inc(S(a + "_shifted"), 1)
                dve.wait_ge(S(a + "_exp"), n)
                V.tensor_reduce(ps[:, 0:nbh].rearrange("p (b h) -> p b h", b=nb), by_bh, AX, ALU.add).then_inc(S(a + "_part_sum"), 1)
                lin_done(dve, a + "sum")
                link(V.reciprocal(inv[:, 0:nbh], mb[:, 0:nbh]))

            dve.wait_ge(S("past_scores_read"), 8)
            batch("m", 64, scores, 8, 16, (mxp, mxT, gm, dg, mbc, psums, rinv), own_s[0:8, :])

            def unit_scores(u):
                buf, nb = (att, nmx) if u < 16 else (xatt, xnmx)
                h, qb, kw = UNITS[u]
                v = u % 16
                dve.wait_ge(S("scores"), u + 1)
                if u >= 2 and u != 16 and u != 17:
                    dve.wait_ge(S("turn_full"), TI[f"pt{u - 2}"] + 1)
                s, ps = buf[u % 2][:, 0:kw], SCORE_BANKS[u % 2][:, 0:kw]
                if u < 16:
                    V.scalar_tensor_tensor(out=s, in0=ps, scalar=ATTN_SCALE, in1=con("causal")[:, 256 - kw:256], op0=ALU.mult, op1=ALU.add)\
                        .then_inc(S("scores_read"), 1)
                else:
                    V.tensor_scalar(s, ps, MEM_SCALE, None, ALU.mult).then_inc(S("scores_read"), 1)
                dve.wait_ge(S("scores_read"), u + 1)
                V.tensor_reduce(nb[:, v:v + 1], s, AX, ALU.max, negate=True).then_inc(S("shifted"), 1)

            def unit_probs(u):
                buf, nb, bufT = (att, nmx, attT) if u < 16 else (xatt, xnmx, xattT)
                kw, v = UNITS[u][2], u % 16
                dve.wait_ge(S("exped"), u + 1)
                link(V.reciprocal(nb[:, 32 + v:33 + v], nb[:, 16 + v:17 + v]))
                s = buf[u % 2][:, 0:kw]
                V.tensor_scalar(s, s, nb[:, 32 + v:33 + v], None, ALU.mult).then_inc(S("probs"), 1)
                if TI[f"pt{u}"] % 2 == 0:
                    turn_out(f"pt{u}", [(flat(bufT[u % 2])[:, 0:kw], P, (0, kw))])

            unit_scores(0)
            for u in range(16):
                if u < 15:
                    unit_scores(u + 1)
                unit_probs(u)
            lin_done(dve, "past7")
            V.tensor_tensor(big2[:, :, PROMPT:T], mxp.rearrange("p (b h) -> p h b", b=8), rinv.rearrange("p (b h) -> p h b", b=8),
                            ALU.mult).then_inc(S("olat_sample"), 1)
            for n in range(10):
                if TI[f"v{n}"] % 2 == 0:
                    c, g = n // 2, n % 2
                    dst, m = (v_tok[:, c, 512 * g:512 * g + 512], CH) if n < 8 else (vs_tok[:, 512 * g:512 * g + 512], 8)
                    turn_out(f"v{n}", [(dst, m, (0, 512))])
            dve.wait_ge(S("softplus"), 1)
            link(V.scalar_tensor_tensor(out=gla, in0=gla, scalar=0.0, in1=gb, op0=ALU.min, op1=ALU.subtract))
            for h in range(4):
                V.tensor_tensor_scan(gb[:, h, 0:PROMPT], con("carry"), gla[:, h, 0:PROMPT], 0.0, ALU.mult, ALU.add).then_inc(S("cumulated"), 1)
            dve.wait_ge(S("cumulated"), 4)
            for h in range(4):
                bh = gb[:, h, 0:PROMPT].rearrange("p (c t) -> p c t", c=NCH)
                V.tensor_tensor(gtmp[:, h, 0:PROMPT].rearrange("p (c t) -> p c t", c=NCH), bc(bh[:, :, CH - 1:CH], [P, NCH, CH]), bh,
                                ALU.subtract).then_inc(S("to_chunk_end"), 1)
            dve.wait_ge(S("k_factors"), 1)
            pr = slice(0, PROMPT)
            V.tensor_tensor(gtmp[:, :, pr], gtmp[:, :, pr], gkT[:, :, pr], ALU.mult).then_inc(S("gla_kout"), 1)
            V.tensor_tensor(gkT[:, :, pr], gkT[:, :, pr], gb[:, :, pr], ALU.mult)
            V.tensor_tensor(gqT[:, :, pr], gqT[:, :, pr], ge[:, :, pr], ALU.mult).then_inc(S("gla_qk"), 1)
            for b in range(8):
                st = st_buf[b % 4]
                t = PROMPT + b
                dve.wait_ge(S(f"state_in{b % 4}"), 16 * (b // 4 + 1))
                for h in range(4):
                    ins = V.tensor_scalar(st[:, h, :], st[:, h, :], ge[:, h, t:t + 1], None, ALU.mult)
                link(ins)
                lin_done(dve, f"vb{2 * b + 1}")
                for h in range(4):
                    ins = V.scalar_tensor_tensor(out=st[:, h, :], in0=vb[:, h // 2, DV * (h % 2):DV * (h % 2) + DV], scalar=gkT[:, h, t:t + 1],
                                                 in1=st[:, h, :], op0=ALU.mult, op1=ALU.add)
                ins.then_inc(S("state_new"), 1)
            lin_done(dve, "A3")
            AT3 = AT.rearrange("p c h t -> p (c h) t")
            link(V.tensor_scalar(AT3, AT3, 3.0e38, -3.0e38, ALU.min, ALU.max))
            V.tensor_tensor(AT3, AT3, bc(con("upto", CH)[:, None, :], [CH, 16, CH]), ALU.mult).then_inc(S("gla_scores"), 1)
            for c in range(NCH):
                if TI[f"ko{c}"] % 2 == 0:
                    turn_out(f"ko{c}", [(ko_tok[:, c, :], CH, (0, 512))])
            lin_done(dve, "kv7")
            for c in range(1, NCH):
                for h in range(4):
                    ins = V.scalar_tensor_tensor(out=states[:, h, c, :], in0=states[:, h, c - 1, :], scalar=ge[:, h, CH * c + CH - 1:CH * c + CH],
                                                 in1=states[:, h, c, :], op0=ALU.mult, op1=ALU.add)
                if c < NCH - 1:
                    link(ins)
            ins.then_inc(S("states_done"), 1)
            lin_done(dve, "go7")
            dve.wait_ge(S("gla_sample"), 1)
            square(flat(gla_out), gla_squares)
            scale_by_rms(5, gla_out, gla_out, "g_gla", 2, T, DV, rstd_gla, groups=4)
            normed_done(dve, 5)
            lin_done(dve, "gg7")
            V.tensor_tensor(gla_out, gla_out, silu_gg, ALU.mult).then_inc(S("gla_gated"), 1)
            lin_done(dve, "om7")
            link(V.tensor_tensor(mla_out, mla_out, sig_zm, ALU.mult))
            for c in range(KC):
                lin_done(dve, f"og{c}")
                link(V.tensor_tensor(big2[:, c, :], big2[:, c, :], sig_zg[:, c, :], ALU.mult))
                V.tensor_tensor(mla_out[:, c, :], mla_out[:, c, :], big2[:, c, :], ALU.add).then_inc(S("merged"), 1)

            def add_to_residual(parts_of):
                for c in range(KC):
                    link(V.tensor_tensor(h_T[:, c, :], h_T[:, c, :], parts_of(c), ALU.add))
                    square_chunk(h_T[:, c, :], c, T)

            def evacuated(name, src):
                def part(c):
                    lin_done(dve, f"{name}{c}")
                    return src[:, c, :]
                return part

            dve.wait_ge(S("state_p_out"), 16)
            add_to_residual(evacuated("wo", big2))
            scale_by_rms(6, h_T, n_T, "g_cross", KC, T, D, rstd2)
            for n in range(16):
                if TI[f"X{n}"] % 2 == 0:
                    if n >= 2:
                        dve.wait_ge(S("x_scores"), n - 1)
                    turn_out(f"X{n}", [(kxT[n % 2], P, (0, 512))])
            dve.wait_ge(S("x_scores"), 16)
            link(V.tensor_scalar(xs, SCORE_BANK[:, 0:64], MEM_SCALE, None, ALU.mult))
            batch("x", 32, xs, 8, 2, (xmxp, xmxT, xgm, xdg, xmbc, xps, xrinv), None)
            unit_scores(16)
            for u in range(16, 24):
                if u < 23:
                    unit_scores(u + 1)
                unit_probs(u)
            V.memset(posm, FAR)
            V.memset(cw, 0.0)
            V.memset(b_gu, 0.0).then_inc(S("bias_cleared"), 1)
            link(V.memset(take, 0.0))
            lin_done(dve, "xpast7")
            V.tensor_tensor(xo[:, :, PROMPT:T], xps[:, 0:32].rearrange("p (b h) -> p h b", b=8), xrinv[:, 0:32].rearrange("p (b h) -> p h b", b=8),
                            ALU.mult).then_inc(S("xo_sample"), 1)
            add_to_residual(evacuated("mo", big4))
            scale_by_rms(7, h_T, n_T, "g_ffn", KC, T, D, rstd2)
            for tt, (_, n) in enumerate(TILES):
                lin_done(dve, f"lg{tt}")
                lg, t8 = logits[0:n, 32 * tt:32 * tt + 32], top8[0:n, 8 * tt:8 * tt + 8]
                ti, tf = top_i[0:n, 8 * tt:8 * tt + 8], top_f[0:n, 8 * tt:8 * tt + 8]
                link(V.max(t8, lg))
                link(V.max_index(ti, t8, lg))
                V.tensor_copy(tf, ti)
                V.tensor_scalar(e4[0:n, 8 * tt:8 * tt + 4], t8[:, 0:4], t8[:, 0:1], None, ALU.subtract).then_inc(S("top_shifted"), 1)
            for i in range(6):
                if TI[f"hn{i}"] % 2 == 0:
                    tt, g = i // 2, i % 2
                    n = TILES[tt][1]
                    turn_out(f"hn{i}", [(hn_tok[0:n, tt, 512 * g:512 * g + 512], n, (0, 512))])
            def tiles(step):
                for tt, (_, n) in enumerate(TILES):
                    ins = step(logits[0:n, 32 * tt:32 * tt + 32], cw[0:n, tt, 0:NE], top_f[0:n, 8 * tt:8 * tt + 8],
                               e4[0:n, 8 * tt:8 * tt + 8], con("count", n)[:, 0:NE])
                return ins

            dve.wait_ge(S("top_exp"), 3)
            link(tiles(lambda one, w, tf, e, c32: V.reciprocal(e[:, 5:6], e[:, 4:5])))
            link(tiles(lambda one, w, tf, e, c32: V.tensor_scalar(e[:, 0:4], e[:, 0:4], e[:, 5:6], None, ALU.mult)))
            link(tiles(lambda one, w, tf, e, c32: V.tensor_scalar(w, c32, tf[:, 0:1], e[:, 0:1], ALU.is_equal, ALU.mult)))
            for k in range(1, TOPK):
                link(tiles(lambda one, w, tf, e, c32: V.tensor_scalar(one, c32, tf[:, k:k + 1], e[:, k:k + 1], ALU.is_equal, ALU.mult)))
                link(tiles(lambda one, w, tf, e, c32: V.tensor_tensor(w, w, one, ALU.add)))
            for tt, (_, n) in enumerate(TILES):
                V.tensor_scalar(take[0:n, tt, :], cw[0:n, tt, 0:NE], 0.0, None, ALU.is_gt).then_inc(S("routed"), 1)
            if TI["cwt"] % 2 == 0:
                turn_out("cwt", [(cwT[0:NE, :], NE, (0, T))])
            lin_done(dve, "rk2")
            for tt, (_, n) in enumerate(TILES):
                ins = V.tensor_scalar(logits[0:n, 32 * tt:32 * tt + 32], take[0:n, tt, :], -FAR, FAR, ALU.mult, ALU.add)
            link(ins)
            for tt, (_, n) in enumerate(TILES):
                ins = V.tensor_tensor(posm[0:n, tt, 0:NE], posm[0:n, tt, 0:NE], logits[0:n, 32 * tt:32 * tt + 32], ALU.add)
            link(ins)

            def one_hots(dst, ranks, weights, done):
                for e in range(2):
                    for tt, (_, n) in enumerate(TILES):
                        ins = V.tensor_scalar(dst[0:n, tt, CAP * e:CAP * e + CAP], con("count", n), ranks[0:n, tt, e:e + 1],
                                              None if weights is None else weights[0:n, tt, e:e + 1], ALU.is_equal,
                                              ALU.bypass if weights is None else ALU.mult)
                ins.then_inc(S(done), 1)

            def pick_bias(eye):
                V.tensor_copy(pick_b, bc(eye.rearrange("p (e o) -> p e o", o=1), [P, 2, CAP])).then_inc(S("bias_picked"), 1)

            def start_pass():
                one_hots(sel, posm[:, :, 0:2], None, "selected")
                pick_bias(ident[:, 0:2])

            start_pass()
            V.memset(y_rows, 0.0).then_inc(S("y_rows"), 4)
            V.memset(wselT, 0.0).then_inc(S("weights_copied"), 1)
            lin_done(dve, "cnt")
            link(V.tensor_reduce(cnts[0:1, 32:33], cnts[0:1, 0:NE], AX, ALU.max))
            link(V.tensor_scalar(cnts[0:1, 33:34], cnts[0:1, 32:33], float(CAP), 1.0, ALU.is_gt, ALU.add))
            for j in range(2, MAX_PASS):
                link(V.scalar_tensor_tensor(out=cnts[0:1, 32 + j:33 + j], in0=cnts[0:1, 32:33], scalar=float(CAP * j), in1=cnts[0:1, 31 + j:32 + j],
                                            op0=ALU.is_gt, op1=ALU.add))
            V.tensor_copy(whole[0:1, 0:1], cnts[0:1, 31 + MAX_PASS:32 + MAX_PASS]).then_inc(S("npass"), 1)
            lin_done(dve, "bd7")

            def add_scattered(m, first, last):
                for c in range(first, last):
                    dve.wait_ge(S("scattered"), 8 * m + c + 1)
                    V.tensor_tensor(acc[:, c, :], acc[:, c, :], B[5 + c % 3][:, 0:T], ALU.add).then_inc(S("added"), 1)

            def expert_pair(q, m, p):
                dve.wait_ge(S("bias_picked"), m + p + 1)
                V.tensor_copy(curp, posm[:, :, bass.ds(2 * q, 4)])
                V.tensor_copy(curw, cw[:, :, bass.ds(2 * q, 2)])
                V.tensor_copy(cureye, ident[:, bass.ds(2 * q, 4)]).then_inc(S("pair_columns"), 1)
                dve.wait_ge(S("pair_columns"), m + 1)
                one_hots(wsel, curp, curw, "weighted")
                dve.wait_ge(S("gathered"), 2 * m + 2 * p + 2)
                one_hots(sel, curp[:, :, 2:4], None, "selected")
                for e in range(2):
                    n = 2 * m + e
                    dve.wait_ge(S("slot1_used"), n + 1)
                    V.tensor_scalar(gate, B[0][:], 7.0, None, ALU.min).then_inc(S("gate"), 1)
                    if e == 0:
                        add_scattered(m, 0, 5)
                    dve.wait_ge(S("slot3_used"), n + 1)
                    V.tensor_scalar(up, B[1][:], 7.0, -7.0, ALU.min, ALU.max).then_inc(S("up_clipped"), 1)
                    dve.wait_ge(S("up_clipped"), n + 1)
                    V.scalar_tensor_tensor(out=up, in0=up, scalar=1.0, in1=gate, op0=ALU.add, op1=ALU.mult).then_inc(S("gated_up"), 1)
                    dve.wait_ge(S("gated_up"), n + 1)
                    dve.wait_ge(S("sigmoid"), n + 1)
                    V.tensor_tensor(up, up, sg, ALU.mult).then_inc(S("hidden"), 1)
                    if e == 0:
                        add_scattered(m, 5, KC)
                pick_bias(cureye[:, 2:4])

            with dve.Fori(0, NE // 2) as q:
                expert_pair(q, q, 0)
            dve.wait_ge(S("npass"), 1)
            npass = dve.value_load(whole[0:1, 0:1], min_val=1, max_val=MAX_PASS)
            with dve.If(npass > 1):
                with dve.Fori(1, npass) as p:
                    V.tensor_scalar(posm, posm, float(-CAP), None, ALU.add).then_inc(S("next_ranks"), 1)
                    dve.wait_ge(S("next_ranks"), p)
                    dve.wait_ge(S("gathered"), 2 * p * (NE // 2 + 1))
                    start_pass()
                    with dve.Fori(0, NE // 2) as q:
                        expert_pair(q, p * (NE // 2) + q, p)
            add_scattered(npass * (NE // 2), 0, KC)
            dve.wait_ge(S("added"), (npass * (NE // 2) + 1) * 8)
            add_to_residual(lambda c: acc[:, c, :])
            scale_by_rms(8, h_T, n_T, "g_final", KC, T, D, rstd2)
            for i in range(6):
                if TI[f"y{i}"] % 2 == 0:
                    tt, g = i // 2, i % 2
                    n = TILES[tt][1]
                    turn_out(f"y{i}", [(y_tok[0:n, tt, 512 * g:512 * g + 512], n, (0, 512))])


_INS = ["x_prompt", "x_sample", "cache_kv_latent", "cache_k_rope", "state_gla", "cache_mem_k", "cache_mem_v", "page_table", "mem_prompt",
        "g_attn", "w_in", "g_q", "g_kv", "w_uq", "w_uk", "w_uv", "w_a2", "b_a", "g_gla", "w_o_mla", "w_o_gla", "w_out", "g_mem", "w_mk",
        "w_mv", "g_cross", "w_mq", "w_mo", "g_ffn", "w_router", "b_router", "w_gate_up", "b_gate_up", "w_down", "b_down", "g_final"]
_OUTS = [(1, 256, 1024), (8, 1, 1024), (1, 1, 256, 128), (1, 1, 256, 64), (1, 1, 4, 128, 256), (1, 1, 256, 4, 128), (1, 1, 256, 4, 128),
         (1, 8, 1, 128), (1, 8, 1, 64), (1, 8, 4, 128, 256)]


def kernel(**inputs):
    import concourse.bacc as _bacc
    from concourse.bass_utils import run_bass_kernel_spmd as _run

    nc = _bacc.Bacc("TRN2", target_bir_lowering=False, num_devices=1)
    arrays, ins = {}, []
    for name in [n for n in _INS if n not in GAINS]:
        a = np.ascontiguousarray(inputs[name])
        arrays[f"in_{name}"] = a
        ins.append(nc.dram_tensor(f"in_{name}", a.shape, mybir.dt.from_np(a.dtype), kind="ExternalInput").ap())
    rows = np.concatenate([np.ascontiguousarray(inputs[name]).reshape(-1, P) for name in GAINS])
    arrays["in_gains"] = rows
    gains = nc.dram_tensor("in_gains", rows.shape, F32, kind="ExternalInput").ap()
    table = constants()
    arrays["in_constants"] = table
    consts = nc.dram_tensor("in_constants", table.shape, F32, kind="ExternalInput").ap()
    outs = [nc.dram_tensor(f"out_{i}", shape, F32, kind="ExternalOutput").ap() for i, shape in enumerate(_OUTS)]
    build(nc, ins, outs, consts, gains)
    r = _run(nc, [arrays], core_ids=[0])
    return tuple(r.results[0][f"out_{i}"] for i in range(len(_OUTS)))
```
